# Optimizing a Trainium2 kernel written in Bass

```python
import jax, jax.numpy as jnp
from jax import lax
import numpy as np

D_MODEL = 1024
BATCH = 1
SEQ = 512
DEPTH = 2

N_META = 16
EPS = 1e-6
D_FF = 4 * D_MODEL
A_HEADS = 4
A_DQK = D_MODEL // 8
A_DV = D_MODEL // 4
A_CHUNK = 64
B_WIDTH = D_MODEL
B_BLOCKS = 8
B_BLOCK = B_WIDTH // B_BLOCKS
CONV_W = 4
LRU_C = 8.0
C_HEADS = 8
C_Q_LORA = 3 * D_MODEL // 8
C_KV_LORA = D_MODEL // 4
C_NOPE = 64
C_ROPE = 32
C_V = 64
ROPE_THETA = 10000.0
D_HEADS = 8
D_HD = 64
ATT_BLOCK = 128

N_EVEN = (DEPTH + 1) // 2
N_ODD = DEPTH // 2
EVEN_SIZES = (A_HEADS * A_DQK, A_HEADS * A_DQK, A_HEADS * A_DV, A_HEADS * A_DV, A_HEADS, A_HEADS, B_WIDTH, B_WIDTH)
ODD_SIZES = (C_Q_LORA, C_KV_LORA, C_ROPE, D_HEADS * D_HD, D_HEADS * D_HD, D_HEADS * D_HD, D_HEADS)
P_EVEN = sum(EVEN_SIZES)
P_ODD = sum(ODD_SIZES)

kernel_name = "hybrid_mlstm_rglru_mla_fox_trunk"

def rmsnorm(x, g):
    xf = x.astype(jnp.float32)
    y = xf * lax.rsqrt(jnp.mean(xf * xf, axis=-1, keepdims=True) + EPS) * g.astype(jnp.float32)
    return y.astype(x.dtype)

def split_cols(z, sizes):
    out, start = [], 0
    for s in sizes:
        out.append(z[..., start:start + s])
        start += s
    return out

def pad_time(a, n, value=0.0):
    widths = [(0, 0), (0, 0), (n, 0)] + [(0, 0)] * (a.ndim - 3)
    return jnp.pad(a, widths, constant_values=value)

def to_heads(a, n_heads, d):
    b, t, _ = a.shape
    return a.reshape(b, t, n_heads, d).transpose(0, 2, 1, 3)

def from_heads(a):
    b, h, t, d = a.shape
    return a.transpose(0, 2, 1, 3).reshape(b, t, h * d)

def rope(x, pos):
    half = x.shape[-1] // 2
    freqs = ROPE_THETA ** (-jnp.arange(half, dtype=jnp.float32) / half)
    ang = pos[:, None, :, None].astype(jnp.float32) * freqs
    cos, sin = jnp.cos(ang), jnp.sin(ang)
    xf = x.astype(jnp.float32)
    x1, x2 = xf[..., :half], xf[..., half:]
    return jnp.concatenate([x1 * cos - x2 * sin, x1 * sin + x2 * cos], axis=-1).astype(x.dtype)

def mlstm_chunkwise(q, k, v, logi, logf):
    bn, nh, tp, dqk = q.shape
    dv = v.shape[-1]
    nc = tp // A_CHUNK

    def chunks(a):
        a = a.astype(jnp.float32).reshape(bn, nh, nc, A_CHUNK, *a.shape[3:])
        return jnp.moveaxis(a, 2, 0)

    causal = jnp.tril(jnp.ones((A_CHUNK, A_CHUNK), dtype=bool))

    def step(carry, inp):
        c_state, n_state, m_state = carry
        qj, kj, vj, ij, fj = inp
        b = jnp.cumsum(fj, axis=-1)
        dmat = jnp.where(causal, b[..., :, None] - b[..., None, :] + ij[..., None, :], -jnp.inf)
        inter = b + m_state[..., None]
        m_row = jnp.maximum(inter, jnp.max(dmat, axis=-1))
        w_intra = jnp.exp(dmat - m_row[..., None])
        w_inter = jnp.exp(inter - m_row)
        s = jnp.einsum('bhtd,bhsd->bhts', qj, kj) * w_intra
        num = (w_inter[..., None] * jnp.einsum('bhtd,bhde->bhte', qj, c_state)
               + jnp.einsum('bhts,bhse->bhte', s, vj))
        den = w_inter * jnp.einsum('bhtd,bhd->bht', qj, n_state) + jnp.sum(s, axis=-1)
        h = num / jnp.maximum(jnp.abs(den), jnp.exp(-m_row))[..., None]
        g = b[..., -1]
        dk = g[..., None] - b + ij
        m_new = jnp.maximum(g + m_state, jnp.max(dk, axis=-1))
        wk = jnp.exp(dk - m_new[..., None])
        sc = jnp.exp(g + m_state - m_new)
        c_new = sc[..., None, None] * c_state + jnp.einsum('bhs,bhsd,bhse->bhde', wk, kj, vj)
        n_new = sc[..., None] * n_state + jnp.einsum('bhs,bhsd->bhd', wk, kj)
        return (c_new, n_new, m_new), h

    init = (jnp.zeros((bn, nh, dqk, dv), jnp.float32),
            jnp.zeros((bn, nh, dqk), jnp.float32),
            jnp.zeros((bn, nh), jnp.float32))
    _, hs = lax.scan(step, init, (chunks(q), chunks(k), chunks(v), chunks(logi), chunks(logf)))
    return jnp.moveaxis(hs, 0, 2).reshape(bn, nh, tp, dv)

def causal_depthwise_conv(x, w, b):
    k, c = w.shape
    y = lax.conv_general_dilated(x, w[:, None, :], window_strides=(1,), padding=[(k - 1, 0)],
                                 dimension_numbers=('NWC', 'WIO', 'NWC'), feature_group_count=c)
    return y + b

def rglru(x, w_a, b_a, w_x, b_x, lam):
    bn, t, w = x.shape
    xb = x.reshape(bn, t, B_BLOCKS, B_BLOCK)
    r = jax.nn.sigmoid(jnp.einsum('btgi,gij->btgj', xb, w_a).reshape(bn, t, w) + b_a)
    i = jax.nn.sigmoid(jnp.einsum('btgi,gij->btgj', xb, w_x).reshape(bn, t, w) + b_x)
    log_a = -LRU_C * r.astype(jnp.float32) * jax.nn.softplus(-lam.astype(jnp.float32))
    a = jnp.exp(log_a)
    u = jnp.sqrt(-jnp.expm1(2.0 * log_a)) * (i * x).astype(jnp.float32)

    def combine(left, right):
        a1, u1 = left
        a2, u2 = right
        return a1 * a2, a2 * u1 + u2

    _, h = lax.associative_scan(combine, (a, u), axis=1)
    return h.astype(x.dtype)

def blocked_causal_attention(q, k, v, scale, n_pad, fcum=None):
    bn, nh, tp, _ = q.shape
    nb = tp // ATT_BLOCK
    kpos = jnp.arange(tp)
    kvalid = kpos >= n_pad

    def one_block(i):
        start = i * ATT_BLOCK
        qb = lax.dynamic_slice_in_dim(q, start, ATT_BLOCK, axis=2)
        qpos = start + jnp.arange(ATT_BLOCK)
        logits = jnp.einsum('bhqd,bhkd->bhqk', qb, k, preferred_element_type=jnp.float32) * scale
        if fcum is not None:
            fq = lax.dynamic_slice_in_dim(fcum, start, ATT_BLOCK, axis=2)
            logits = logits + (fq[..., :, None] - fcum[..., None, :])
        mask = (kpos[None, :] <= qpos[:, None]) & (kvalid[None, :] | (kpos[None, :] == qpos[:, None]))
        p = jax.nn.softmax(jnp.where(mask, logits, -jnp.inf), axis=-1)
        return jnp.einsum('bhqk,bhkd->bhqd', p.astype(v.dtype), v)

    out = lax.map(one_block, jnp.arange(nb))
    return jnp.moveaxis(out, 0, 2).reshape(bn, nh, tp, v.shape[-1])

def even_mixer(h, ln, w_in, b_if, a_norm_g, conv_w, conv_b, w_ra, b_ra, w_rx, b_rx, lam, w_out):
    bn, t, _ = h.shape
    z = rmsnorm(h, ln) @ w_in
    q, k, v, o, ig, fg, xb, gb = split_cols(z, EVEN_SIZES)
    q = to_heads(q, A_HEADS, A_DQK)
    k = to_heads(k, A_HEADS, A_DQK) * (A_DQK ** -0.5)
    v = to_heads(v, A_HEADS, A_DV)
    gates = (jnp.concatenate([ig, fg], axis=-1) + b_if).astype(jnp.float32)
    logi = gates[..., :A_HEADS].transpose(0, 2, 1)
    logf = jax.nn.log_sigmoid(gates[..., A_HEADS:]).transpose(0, 2, 1)
    pad = A_CHUNK - N_META
    ha = mlstm_chunkwise(pad_time(q, pad), pad_time(k, pad), pad_time(v, pad),
                         pad_time(logi, pad, -jnp.inf), pad_time(logf, pad))[:, :, pad:]
    ha = rmsnorm(ha.astype(h.dtype), a_norm_g) * jax.nn.sigmoid(to_heads(o, A_HEADS, A_DV))
    xc = causal_depthwise_conv(xb, conv_w, conv_b)
    hb = rglru(xc, w_ra, b_ra, w_rx, b_rx, lam) * jax.nn.gelu(gb)
    return jnp.concatenate([from_heads(ha), hb], axis=-1) @ w_out

def odd_mixer(h, pos_full, ln, w_in, b_f, g_qa, g_kva, w_uq, w_ukv, g_qn, g_qr, g_kn, g_kr,
              g_fq, g_fk, w_out):
    bn, t, _ = h.shape
    z = rmsnorm(h, ln) @ w_in
    cq, ckv, kr, fq, fk, fv, ff = split_cols(z, ODD_SIZES)
    pad = ATT_BLOCK - N_META
    q = to_heads(rmsnorm(cq, g_qa) @ w_uq, C_HEADS, C_NOPE + C_ROPE)
    kv = to_heads(rmsnorm(ckv, g_kva) @ w_ukv, C_HEADS, C_NOPE + C_V)
    q_nope = rmsnorm(q[..., :C_NOPE], g_qn)
    q_rope = rope(rmsnorm(q[..., C_NOPE:], g_qr), pos_full)
    k_nope = rmsnorm(kv[..., :C_NOPE], g_kn)
    k_rope = rope(rmsnorm(kr, g_kr)[:, None], pos_full)
    q_mla = jnp.concatenate([q_nope, q_rope], axis=-1)
    k_mla = jnp.concatenate([k_nope, jnp.broadcast_to(k_rope, (bn, C_HEADS, t, C_ROPE))], axis=-1)
    v_mla = kv[..., C_NOPE:]
    hc = blocked_causal_attention(pad_time(q_mla, pad), pad_time(k_mla, pad), pad_time(v_mla, pad),
                                  (C_NOPE + C_ROPE) ** -0.5, pad)[:, :, pad:]
    qf = rmsnorm(to_heads(fq, D_HEADS, D_HD), g_fq)
    kf = rmsnorm(to_heads(fk, D_HEADS, D_HD), g_fk)
    vf = to_heads(fv, D_HEADS, D_HD)
    logf = jax.nn.log_sigmoid((ff + b_f).astype(jnp.float32)).transpose(0, 2, 1)
    fcum = jnp.cumsum(pad_time(logf, pad), axis=-1)
    hd = blocked_causal_attention(pad_time(qf, pad), pad_time(kf, pad), pad_time(vf, pad),
                                  D_HD ** -0.5, pad, fcum)[:, :, pad:]
    return jnp.concatenate([from_heads(hc), from_heads(hd)], axis=-1) @ w_out

def sqrelu_mlp(h, ln, w1, w2):
    return jnp.square(jax.nn.relu(rmsnorm(h, ln) @ w1)) @ w2

def setup_inputs(seed: int = 0) -> dict:
    key = jax.random.key(seed)
    ks = iter(jax.random.split(key, 48))
    nrm = lambda shape, s: jax.random.normal(next(ks), shape, jnp.float32) * s
    gain = lambda shape: 1.0 + nrm(shape, 0.02)
    ne, no = N_EVEN, N_ODD
    x = jax.random.normal(next(ks), (BATCH, SEQ, D_MODEL), jnp.float32)
    positions = (jnp.arange(SEQ, dtype=jnp.int32)[None, :]
                 + jax.random.randint(next(ks), (BATCH, 1), 0, 1024, dtype=jnp.int32))
    meta = nrm((N_META, D_MODEL), 1.0)
    ev_ln = gain((ne, D_MODEL))
    ev_w_in = nrm((ne, D_MODEL, P_EVEN), D_MODEL ** -0.5)
    ev_b_if = jnp.concatenate([nrm((ne, A_HEADS), 0.1),
                               3.0 + 3.0 * jax.random.uniform(next(ks), (ne, A_HEADS))], axis=-1)
    ev_a_norm = gain((ne, A_DV))
    ev_conv_w = nrm((ne, CONV_W, B_WIDTH), CONV_W ** -0.5)
    ev_conv_b = nrm((ne, B_WIDTH), 0.01)
    ev_w_ra = nrm((ne, B_BLOCKS, B_BLOCK, B_BLOCK), B_BLOCK ** -0.5)
    ev_b_ra = nrm((ne, B_WIDTH), 0.01)
    ev_w_rx = nrm((ne, B_BLOCKS, B_BLOCK, B_BLOCK), B_BLOCK ** -0.5)
    ev_b_rx = nrm((ne, B_WIDTH), 0.01)
    a0 = jax.random.uniform(next(ks), (ne, B_WIDTH), jnp.float32, 0.9, 0.999)
    s0 = a0 ** (1.0 / LRU_C)
    ev_lam = jnp.log(s0) - jnp.log1p(-s0)
    ev_w_out = nrm((ne, A_HEADS * A_DV + B_WIDTH, D_MODEL), (A_HEADS * A_DV + B_WIDTH) ** -0.5)
    od_ln = gain((no, D_MODEL))
    od_w_in = nrm((no, D_MODEL, P_ODD), D_MODEL ** -0.5)
    od_b_f = 2.0 + nrm((no, D_HEADS), 0.5)
    od_g_qa = gain((no, C_Q_LORA))
    od_g_kva = gain((no, C_KV_LORA))
    od_w_uq = nrm((no, C_Q_LORA, C_HEADS * (C_NOPE + C_ROPE)), C_Q_LORA ** -0.5)
    od_w_ukv = nrm((no, C_KV_LORA, C_HEADS * (C_NOPE + C_V)), C_KV_LORA ** -0.5)
    od_g_qn = gain((no, C_NOPE))
    od_g_qr = gain((no, C_ROPE))
    od_g_kn = gain((no, C_NOPE))
    od_g_kr = gain((no, C_ROPE))
    od_g_fq = gain((no, D_HD))
    od_g_fk = gain((no, D_HD))
    od_w_out = nrm((no, C_HEADS * C_V + D_HEADS * D_HD, D_MODEL), (C_HEADS * C_V + D_HEADS * D_HD) ** -0.5)
    mlp_ln = gain((DEPTH, D_MODEL))
    w_ff1 = nrm((DEPTH, D_MODEL, D_FF), D_MODEL ** -0.5)
    w_ff2 = nrm((DEPTH, D_FF, D_MODEL), D_FF ** -0.5)
    return {"x": x, "positions": positions, "meta": meta,
            "ev_ln": ev_ln, "ev_w_in": ev_w_in, "ev_b_if": ev_b_if, "ev_a_norm": ev_a_norm,
            "ev_conv_w": ev_conv_w, "ev_conv_b": ev_conv_b, "ev_w_ra": ev_w_ra, "ev_b_ra": ev_b_ra,
            "ev_w_rx": ev_w_rx, "ev_b_rx": ev_b_rx, "ev_lam": ev_lam, "ev_w_out": ev_w_out,
            "od_ln": od_ln, "od_w_in": od_w_in, "od_b_f": od_b_f, "od_g_qa": od_g_qa,
            "od_g_kva": od_g_kva, "od_w_uq": od_w_uq, "od_w_ukv": od_w_ukv, "od_g_qn": od_g_qn,
            "od_g_qr": od_g_qr, "od_g_kn": od_g_kn, "od_g_kr": od_g_kr, "od_g_fq": od_g_fq,
            "od_g_fk": od_g_fk, "od_w_out": od_w_out,
            "mlp_ln": mlp_ln, "w_ff1": w_ff1, "w_ff2": w_ff2}

def reference(x, positions, meta,
              ev_ln, ev_w_in, ev_b_if, ev_a_norm, ev_conv_w, ev_conv_b, ev_w_ra, ev_b_ra,
              ev_w_rx, ev_b_rx, ev_lam, ev_w_out,
              od_ln, od_w_in, od_b_f, od_g_qa, od_g_kva, od_w_uq, od_w_ukv, od_g_qn, od_g_qr,
              od_g_kn, od_g_kr, od_g_fq, od_g_fk, od_w_out,
              mlp_ln, w_ff1, w_ff2):
    bn = x.shape[0]
    h = jnp.concatenate([jnp.broadcast_to(meta.astype(x.dtype), (bn, N_META, D_MODEL)), x], axis=1)
    meta_pos = jnp.broadcast_to(jnp.arange(N_META, dtype=jnp.int32)[None, :], (bn, N_META))
    pos_full = jnp.concatenate([meta_pos, positions + N_META], axis=1)
    for layer in range(DEPTH):
        if layer % 2 == 0:
            e = layer // 2
            h = h + even_mixer(h, ev_ln[e], ev_w_in[e], ev_b_if[e], ev_a_norm[e], ev_conv_w[e],
                               ev_conv_b[e], ev_w_ra[e], ev_b_ra[e], ev_w_rx[e], ev_b_rx[e],
                               ev_lam[e], ev_w_out[e])
        else:
            o = layer // 2
            h = h + odd_mixer(h, pos_full, od_ln[o], od_w_in[o], od_b_f[o], od_g_qa[o], od_g_kva[o],
                              od_w_uq[o], od_w_ukv[o], od_g_qn[o], od_g_qr[o], od_g_kn[o],
                              od_g_kr[o], od_g_fq[o], od_g_fk[o], od_w_out[o])
        h = h + sqrelu_mlp(h, mlp_ln[layer], w_ff1[layer], w_ff2[layer])
    return h[:, N_META:]


_drawn_inputs = setup_inputs


def setup_inputs(seed=0):
    import zlib

    import numpy as np

    out = dict(_drawn_inputs(seed))
    spreads = {}
    factors = {'ev_ln': 3.26,
     'ev_a_norm': 6.977,
     'ev_b_ra': 8.0,
     'ev_b_rx': 8.0,
     'od_ln': 8.0,
     'od_g_qa': 8.0,
     'od_g_kva': 8.0,
     'od_g_qn': 8.0,
     'od_g_qr': 8.0,
     'od_g_kn': 8.0,
     'od_g_kr': 8.0,
     'od_g_fq': 8.0,
     'od_g_fk': 8.0}
    for name, (base, spread) in spreads.items():
        noise = np.random.default_rng([zlib.crc32(name.encode()), seed]).standard_normal(out[name].shape)
        drawn = base * np.exp(spread * noise) if base else spread * noise
        out[name] = __import__('jax').numpy.asarray(drawn.astype(out[name].dtype))
    for name, factor in factors.items():
        out[name] = (out[name] * factor).astype(out[name].dtype)
    return out
```

```python
import numpy as np

import concourse.bass as bass
from concourse import mybir
from contextlib import ExitStack


P = 128
D_MODEL, SEQ, N_META = 1024, 512, 16
T = N_META + SEQ
HALF = T // 2
KT = D_MODEL // P
D_FF = 4 * D_MODEL
QUARTERS = D_FF // D_MODEL
A_HEADS, A_DQK, A_DV = 4, 128, 256
HEADS, C_NOPE, C_ROPE, HD = 8, 64, 32, 64
Q_LORA, KV_LORA = 384, 256
EPS = 1e-6
BLOCKS = [(0, N_META)] + [(N_META + P * i, P) for i in range(SEQ // P)]
NB = len(BLOCKS)
MASKED = -1e30

TILE = 8 * P
S_RG = 0
S_GATES = S_RG + 2 * KT
S_QK = S_GATES + 1
S_V = S_QK + 8
S_O = S_V + 8
S_OUT0 = S_O + 8
S_MLP0 = S_OUT0 + 16
S_LORA = S_MLP0 + 64
S_KRFF = S_LORA + 5
S_FQK = S_KRFF + 1
S_FV = S_FQK + 8
S_UQ = S_FV + 4
S_UK = S_UQ + 3
S_UV = S_UK + 1
S_OUT1 = S_UV + 1
S_MLP1 = S_OUT1 + 8
S_END = S_MLP1 + 64

Y_RG = 0
Y_GATES = Y_RG + 16
Y_QK = Y_GATES + 1
Y_V = Y_QK + 8
Y_O = Y_V + 8
Y_OUT0 = Y_O + 8
Y_MLP0 = Y_OUT0 + 8
Y_LORA = Y_MLP0 + 64
Y_KRFF = Y_LORA + 5
Y_FQK = Y_KRFF + 1
Y_FV = Y_FQK + 8
Y_UQ = Y_FV + 4
Y_UK = Y_UQ + 6
Y_UV = Y_UK + 4
Y_OUT1 = Y_UV + 4
Y_MLP1 = Y_OUT1 + 8

R_X0 = 0
R_HB = R_X0 + KT
R_HA = R_HB + KT
R_X1 = R_HA + KT
R_MLP0 = R_X1 + KT
R_X2 = R_MLP0 + KT * QUARTERS
R_LORA = R_X2 + KT
R_ATT_D = R_LORA + 5
R_ATT_C = R_ATT_D + 4
R_X3 = R_ATT_C + 4
R_MLP1 = R_X3 + KT

COLS = {}


def _col(name, n):
    COLS[name] = sum(w for _, w in COLS.values()), n


for _name, _n in (("ev_ln", 8), ("od_ln", 8), ("mlp_ln0", 8), ("mlp_ln1", 8), ("conv_w", 32), ("conv_b", 8),
                  ("b_ra", 8), ("b_rx", 8), ("lam", 8), ("a_norm", 2), ("g_qa", 3), ("g_kva", 2), ("g_qn", 1),
                  ("g_qr", 1), ("g_kn", 1), ("g_kr", 1), ("g_fq", 1), ("g_fk", 1), ("b_i", 1), ("b_f", 1),
                  ("od_b_f", 1), ("freq", 1)):
    _col(_name, _n)
N_COLS = sum(w for _, w in COLS.values())
C_IDENT, C_ONES, C_BLK64, C_BLK32, C_ROT, C_MASK_ST, C_MASK_TS, C_SEL = range(8)
N_CONST = C_SEL + A_HEADS


def trunk(nc, h_in, positions, stream, gate_w, cols_in, const_in, out):
    F32, F32R, BF16, I32 = mybir.dt.float32, mybir.dt.float32r, mybir.dt.bfloat16, mybir.dt.int32
    ALU, ACT, AX = mybir.AluOpType, mybir.ActivationFunctionType, mybir.AxisListType
    ctx = ExitStack()
    with ctx:
        def sb(name, shape, dt=F32, scope=ctx):
            return scope.enter_context(nc.sbuf_tensor(name, shape, dt))

        def sem(name):
            return ctx.enter_context(nc.semaphore(name))

        h = sb("h", [P, KT, T])
        a_hi, a_lo = sb("a_hi", [P, KT, T], F32R), sb("a_lo", [P, KT, T], F32R)
        b_hi, b_lo = sb("b_hi", [P, KT, T], F32R), sb("b_lo", [P, KT, T], F32R)
        raw = sb("raw", [P, 4, TILE])
        w_hi, w_lo = sb("w_hi", [P, 2, TILE], F32R), sb("w_lo", [P, 2, TILE], F32R)
        cols = sb("cols", [P, N_COLS])
        const = sb("const", [P, N_CONST * P])
        ident_bf, mask_st_bf, mask_ts_bf = (sb(n, [P, P], BF16) for n in ("ident_bf", "mask_st_bf", "mask_ts_bf"))
        inv_ms = sb("inv_ms", [P, T])
        rstd = inv_ms
        sq = sb("sq", [P, 2, T])
        sq_sum = sb("sq_sum", [P, T])
        tmp = sb("tmp", [P, 2, T])

        even = ExitStack()
        c_hi, c_lo = sb("c_hi", [P, KT, T], F32R, even), sb("c_lo", [P, KT, T], F32R, even)
        qk = sb("qk", [P, 2 * A_HEADS, T], F32, even)
        v = sb("v", [P, NB, A_HEADS * A_DV], F32, even)
        even.close()
        rg = ExitStack()
        xb = sb("xb", [P, T + 3], F32, rg)
        xc, gate_r, gate_i, den_t, sqrt_t, decay, gb, gel, hs = (
            sb(n, [P, T], F32, rg) for n in ("xc", "gate_r", "gate_i", "den_t", "sqrt_t", "decay", "gb", "gel", "hs"))
        wr = sb("wr", [P, 2 * KT * P], F32, rg)
        sp4 = sb("sp4", [P, KT], F32, rg)
        spt = sb("spt", [P, 5, KT], F32, rg)
        rg.close()
        ml = ExitStack()
        N_ST = 2 * T - N_META + sum(T - t0 for t0, _ in BLOCKS[2:])
        expw = sb("expw", [P, N_ST], F32, ml)
        st = sb("st", [P, N_ST], F32, ml)
        abc, em, rs_a = (sb(n, [P, T], F32, ml) for n in ("abc", "em", "rs_a"))
        ccol = sb("ccol", [P, NB * A_HEADS], F32, ml)
        ml.close()

        odd = ExitStack()
        q_aug = sb("q_aug", [P, HEADS, T], F32, odd)
        k_aug = sb("k_aug", [P, HEADS, T], F32, odd)
        vp = sb("vp", [P, NB, 4, 192], F32, odd)
        N_PT = 2 * SEQ + sum(T - t0 for t0, _ in BLOCKS[2:])
        pt = sb("pt", [P, 2, N_PT], F32, odd)
        kr = sb("kr", [C_ROPE, T], F32, odd)
        stg = sb("stg", [P, 2, T], F32, odd)
        maxes = sb("maxes", [P, 4, HEADS], F32, odd)
        odd.close()
        od2 = ExitStack()
        sb("pad_aug", [P, 2 * HEADS * T], F32, od2)
        lora_sq = sb("lora_sq", [P, 5, T], F32, od2)
        sb("pad_vp", [P, NB * 4 * 192 - 5 * T], F32, od2)
        lora = sb("lora", [P, 5, T], F32, od2)
        od2.close()
        g_f, g_l, g_i, g_F, g_m = tmp[0:HEADS, 0], tmp[0:HEADS, 1], sq[0:HEADS, 0], sq[0:HEADS, 1], sq_sum[0:HEADS]
        g_pos = sq_sum[:].bitcast(I32)

        prod = ctx.enter_context(nc.psum_tensor("prod", [P, 2, 1024], F32))
        aux = ctx.enter_context(nc.psum_tensor("aux", [P, 2048], F32))

        names = ["h_loaded", "cols_loaded", "const_loaded", "wr_loaded", "raw_full0", "raw_full1", "raw_full2",
                 "raw_full3", "w_hi_ready", "w_lo_ready", "w_used", "part_ready", "psum_free", "operand_ready",
                 "a_hi_ready", "sq_ready", "sq_summed", "stat_ready", "ms_ready", "rstd_ready", "h_ready",
                 "dve_chain", "act_chain", "pool_chain", "bf_ready", "sp4_ready", "lam_e_ready",
                 "conv0_ready", "xc_ready", "gates_ready", "sig_ready", "tanh_ready", "sqrt_ready", "den_ready",
                 "ix_ready", "sd_ready", "decay_ready", "u_ready", "hs_ready", "hb_ready", "gsq_ready",
                 "gz_ready", "gsig_ready", "gelu_ready", "split_hi", "zero_ready",
                 "gf_ready", "gl_ready", "rows_ready", "ccol_psum", "ccol_ready", "bc_ready", "abc_ready",
                 "em_ready", "diag_ready", "expw_ready", "s_ready", "st_ready", "acc_ready", "absden_ready",
                 "hn_ready", "hnsq_ready", "hstat_ready", "hms_ready", "hrs_ready", "head_done",
                 "osig_ready", "osig_raw", "ha_ready", "vt_ready", "v_copied", "relu_ready", "hid_ready",
                 "trig_pos", "trig_ready", "trig_arg", "lsq_ready", "lstat_ready", "lms_ready", "lrs_ready",
                 "ln_ready", "fF_ready", "fgf_ready", "fgl_ready", "augF", "aug_one",
                 "item_sq", "item_stat", "item_ms", "item_rs", "item_done", "item_rot", "item_dma0", "item_dma1",
                 "logit_ready", "max_ready", "mxrow_ready", "mxneg_ready", "mx_dma", "l_ready", "p_ready",
                 "o_ready", "ot_ready", "ot_free", "stored", "pos_loaded"]
        S = {n: sem(n) for n in names}
        raw_full = [S[f"raw_full{i}"] for i in range(4)]
        item_dma = [S["item_dma0"], S["item_dma1"]]

        def cm(i, rows_=P, width=P):
            return const[0:rows_, i * P:i * P + width]

        def col(name, j=0, rows_=P, p0=0):
            c = COLS[name][0] + j
            return cols[p0:p0 + rows_, c:c + 1]

        def two(ap):
            return ap.rearrange("p (b n) -> p b n", b=2)

        def slot(y, rows_=P, p0=0):
            return prod[p0:p0 + rows_, y % 2].rearrange("p (b n) -> p b n", b=2)[:, :, 0:HALF]

        def slot_real(y):
            return prod[:, y % 2, 0:SEQ]

        def aux_two(b, rows_=P):
            return aux[0:rows_, b * 512:(b + 2) * 512].rearrange("p (b n) -> p b n", b=2)[:, :, 0:HALF]

        def units(with_meta_queries):
            found, off = [], 0
            if with_meta_queries:
                found.append((0, 0, N_META, 0, N_META))
                off = N_META
            for j, (t0, _) in enumerate(BLOCKS):
                first = max(t0, N_META)
                found.append((j, first, T - first, off, P if j else 0))
                off += T - first
            return found

        N_EXP = sum((n > diag) + (diag > 0) for _, _, n, _, diag in units(True))

        block = ctx.enter_context(nc.Block())

        @block.sync
        def _(sp):
            sp.dma_start(cols[:], cols_in).then_inc(S["cols_loaded"], 16)
            sp.dma_start(h[:], h_in.rearrange("(m p) t -> p m t", p=P)).then_inc(S["h_loaded"], 16)
            for n in range(4):
                sp.dma_start(raw[:, n], stream[n]).then_inc(raw_full[n], 16)
            sp.dma_start(const[:], const_in).then_inc(S["const_loaded"], 16)
            sp.dma_start(wr[:].rearrange("p (g n) -> p g n", n=P), gate_w.rearrange("g p n -> p g n")).then_inc(
                S["wr_loaded"], 16)

            def load(first, iterations):
                with sp.Fori(0, iterations) as i:
                    row = sp.snap(i * 4 + first)
                    for j in range(4):
                        sp.wait_ge(S["w_lo_ready"], i * 4 + (first + j - 3))
                        sp.dma_start(raw[:, j], stream[bass.ds(row + j, 1)].rearrange("a p n -> p (a n)")).then_inc(
                            raw_full[j], 16)

            load(4, (S_END - 4) // 4)

        @block.gpsimd
        def _(pool):
            chain = [0]

            def link(ins):
                chain[0] += 1
                ins.then_inc(S["pool_chain"], 1)
                pool.wait_ge(S["pool_chain"], chain[0])

            def sum_squares(base, t0):
                for m in range(KT):
                    pool.wait_ge(S["sq_ready"], base + m + 1)
                    if m == 0:
                        nc.gpsimd.tensor_copy(sq_sum[:, t0:], sq[:, 0, t0:]).then_inc(S["sq_summed"], 1)
                    else:
                        pool.wait_ge(S["sq_summed"], base + m)
                        nc.gpsimd.tensor_tensor(sq_sum[:, t0:], sq_sum[:, t0:], sq[:, m % 2, t0:], ALU.add).then_inc(
                            S["sq_summed"], 1)

            nc.gpsimd.memset(xb[:, 0:3], 0.0).then_inc(S["zero_ready"], 1)
            sum_squares(0, 0)
            for g in range(KT):
                pool.wait_ge(S["gsq_ready"], g + 1)
                link(nc.gpsimd.tensor_scalar(gel[:], gel[:], 0.044715, 1.0, ALU.mult, ALU.add))
                nc.gpsimd.tensor_tensor(gel[:], gel[:], gb[:], ALU.mult).then_inc(S["gz_ready"], 1)
                pool.wait_ge(S["sig_ready"], g + 1)
                nc.gpsimd.tensor_tensor(gate_i[:], gate_i[:], xc[:], ALU.mult).then_inc(S["ix_ready"], 1)
                pool.wait_ge(S["gsig_ready"], g + 1)
                nc.gpsimd.tensor_tensor(gel[:], gel[:], gb[:], ALU.mult).then_inc(S["gelu_ready"], 1)
                pool.wait_ge(S["sqrt_ready"], g + 1)
                pool.wait_ge(S["den_ready"], g + 1)
                nc.gpsimd.tensor_tensor(sqrt_t[:], sqrt_t[:], den_t[:], ALU.mult).then_inc(S["sd_ready"], 1)
                if g:
                    pool.wait_ge(S["hs_ready"], g)
                nc.gpsimd.tensor_scalar(decay[:], den_t[:], 2.0, -1.0, ALU.mult, ALU.add).then_inc(
                    S["decay_ready"], 1)
            sum_squares(KT, 0)

            def mlp(y0, r0, t0, q, sq_base):
                for j in range(8):
                    pool.wait_ge(S["psum_free"], y0 + j + 1 + q * 16)
                    nc.gpsimd.tensor_tensor(tmp[:, j % 2, t0:], tmp[:, j % 2, t0:], tmp[:, j % 2, t0:],
                                            ALU.mult).then_inc(S["hid_ready"], 1)

            with pool.Fori(0, QUARTERS - 1) as q:
                mlp(Y_MLP0, 0, 0, q, None)
            mlp(Y_MLP0, 0, 0, QUARTERS - 1, None)
            sum_squares(2 * KT, 0)
            pool.wait_ge(S["mx_dma"], 16 * HEADS)
            nc.gpsimd.iota(g_pos[:, 0:N_META], pattern=[[1, N_META]], base=0, channel_multiplier=0).then_inc(
                S["trig_pos"], 1)
            sum_squares(3 * KT, N_META)
            with pool.Fori(0, QUARTERS - 1) as q:
                mlp(Y_MLP1, 0, N_META, q, None)
            mlp(Y_MLP1, 0, N_META, QUARTERS - 1, None)

        @block.scalar
        def _(act):
            chain = [0]

            def link(ins):
                chain[0] += 1
                ins.then_inc(S["act_chain"], 1)
                act.wait_ge(S["act_chain"], chain[0])

            def split_weights(nb, i4=0):
                act.wait_ge(raw_full[nb % 4], 16 * (nb // 4 + 1) + i4 * 16)
                if nb >= 2:
                    act.wait_ge(S["w_used"], nb - 1 + i4 * 4)
                nc.scalar.activation(w_hi[:, nb % 2], raw[:, nb % 4], ACT.Copy).then_inc(S["w_hi_ready"], 1)

            def next_operand(m, base, gain, hi, t0):
                if base == 2 * KT:
                    act.wait_ge(S["h_ready"], m + 1)
                elif base:
                    act.wait_ge(S["psum_free"], {KT: Y_OUT0, 3 * KT: Y_OUT1}[base] + m + 1)
                nc.scalar.activation(hi[:, m, t0:], h[:, m, t0:], ACT.Copy, scale=col(gain, m)).then_inc(
                    S["a_hi_ready"], 1)
                if m >= 2:
                    act.wait_ge(S["sq_summed"], base + m - 1)
                nc.scalar.activation(sq[:, m % 2, t0:], h[:, m, t0:], ACT.Square).then_inc(S["sq_ready"], 1)

            def token_factor(k, t0=0):
                act.wait_ge(S["ms_ready"], k + 1)
                nc.scalar.activation(rstd[:, t0:], inv_ms[:, t0:], ACT.Sqrt).then_inc(S["rstd_ready"], 1)

            act.wait_ge(S["cols_loaded"], 16)
            lam = cols[:, COLS["lam"][0]:COLS["lam"][0] + KT]
            link(nc.scalar.activation(spt[:, 0], lam, ACT.Abs))
            nc.scalar.activation(spt[:, 0], spt[:, 0], ACT.Exp, scale=-1.0).then_inc(S["lam_e_ready"], 1)
            act.wait_ge(S["h_loaded"], 16)
            for m in range(KT):
                next_operand(m, 0, "ev_ln", a_hi, 0)
                if m < 2:
                    split_weights(m)
            act.wait_ge(S["const_loaded"], 16)
            nc.scalar.activation(ident_bf[:], cm(C_IDENT), ACT.Copy).then_inc(S["bf_ready"], 1)
            nc.scalar.activation(mask_st_bf[:], cm(C_MASK_ST), ACT.Copy).then_inc(S["bf_ready"], 1)
            nc.scalar.activation(mask_ts_bf[:], cm(C_MASK_TS), ACT.Copy).then_inc(S["bf_ready"], 1)
            token_factor(0)

            for g in range(KT):
                split_weights(2 * g + 2)
                act.wait_ge(S["psum_free"], 2 * g + 1)
                if g == 0:
                    act.wait_ge(S["zero_ready"], 1)
                else:
                    act.wait_ge(S["ix_ready"], g)
                nc.scalar.activation(xc[:], xb[:, 0:T], ACT.Identity, bias=col("conv_b", g),
                                     scale=col("conv_w", g)).then_inc(S["conv0_ready"], 1)
                split_weights(2 * g + 3)
                act.wait_ge(S["psum_free"], 2 * g + 2)
                nc.scalar.activation(gel[:], gb[:], ACT.Square).then_inc(S["gsq_ready"], 1)
                if g:
                    act.wait_ge(S["hb_ready"], g)
                    nc.scalar.activation(b_hi[:, g - 1], hs[:], ACT.Copy).then_inc(S["split_hi"], 1)
                act.wait_ge(S["gates_ready"], g + 1)
                if g:
                    act.wait_ge(S["u_ready"], g)
                if g == 0:
                    act.wait_ge(S["sp4_ready"], 1)
                nc.scalar.activation(two(gate_r[:]), aux_two(0), ACT.Sigmoid, bias=col("b_ra", g)).then_inc(
                    S["act_chain"], 1)
                chain[0] += 1
                nc.scalar.activation(two(gate_i[:]), aux_two(2), ACT.Sigmoid, bias=col("b_rx", g)).then_inc(
                    S["sig_ready"], 1)
                act.wait_ge(S["act_chain"], chain[0])
                nc.scalar.activation(gate_r[:], gate_r[:], ACT.Tanh, scale=sp4[:, g:g + 1]).then_inc(
                    S["tanh_ready"], 1)
                act.wait_ge(S["gz_ready"], g + 1)
                nc.scalar.activation(gel[:], gel[:], ACT.Sigmoid, scale=float(2.0 * np.sqrt(2.0 / np.pi))).then_inc(
                    S["gsig_ready"], 1)
                act.wait_ge(S["tanh_ready"], g + 1)
                nc.scalar.activation(sqrt_t[:], gate_r[:], ACT.Sqrt, scale=4.0).then_inc(S["sqrt_ready"], 1)
            act.wait_ge(S["hb_ready"], KT)
            nc.scalar.activation(b_hi[:, KT - 1], hs[:], ACT.Copy).then_inc(S["split_hi"], 1)

            split_weights(S_GATES + 2)
            act.wait_ge(S["gf_ready"], 1)
            link(nc.scalar.activation(g_l[0:A_HEADS], g_f[0:A_HEADS], ACT.Abs, bias=col("b_f", 0, A_HEADS)))
            link(nc.scalar.activation(g_l[0:A_HEADS], g_l[0:A_HEADS], ACT.Exp, scale=-1.0))
            nc.scalar.activation(g_l[0:A_HEADS], g_l[0:A_HEADS], ACT.Ln, bias=1.0).then_inc(S["gl_ready"], 1)
            for j in range(8):
                split_weights(S_QK + 2 + j)

            def copy_v(j, dst_meta, dst_real, base, pairs=False):
                act.wait_ge(S["vt_ready"], base + j + 1)
                a = (j % 2) * 1024
                nc.scalar.activation(dst_meta, aux[0:N_META, a:a + P] if not pairs else
                                     aux[0:N_META, a:a + P].rearrange("p (c n) -> p c n", c=2), ACT.Copy)
                src = aux[:, a + 512:a + 1024].rearrange("p (b n) -> p b n", b=4)
                if pairs:
                    for b in range(4):
                        last = nc.scalar.activation(dst_real[:, b], src[:, b].rearrange("p (c n) -> p c n", c=2),
                                                    ACT.Copy)
                else:
                    last = nc.scalar.activation(dst_real, src, ACT.Copy)
                last.then_inc(S["v_copied"], 1)

            for j in range(8):
                split_weights(S_V + 2 + j)
                if j:
                    copy_v(j - 1, v[0:N_META, 0, (j - 1) * P:j * P], v[:, 1:NB, (j - 1) * P:j * P], 0)
            copy_v(7, v[0:N_META, 0, 7 * P:8 * P], v[:, 1:NB, 7 * P:8 * P], 0)

            act.wait_ge(S["ccol_psum"], 1)
            nc.scalar.activation(ccol[:], aux[:, 0:NB * A_HEADS], ACT.Copy).then_inc(S["ccol_ready"], 1)
            mu = units(True)
            for hd in range(A_HEADS):
                act.wait_ge(S["bc_ready"], 2 * hd + 1)
                if hd:
                    act.wait_ge(S["head_done"], hd)
                nc.scalar.activation(two(abc[:]), aux_two(2), ACT.Copy).then_inc(S["abc_ready"], 1)
                act.wait_ge(S["bc_ready"], 2 * hd + 2)
                nc.scalar.activation(two(em[:]), aux_two(2), ACT.Exp).then_inc(S["em_ready"], 1)
                act.wait_ge(S["abc_ready"], hd + 1)
                act.wait_ge(S["ccol_ready"], 1)
                for u, (j, t0, n, off, diag) in enumerate(mu):
                    rows_ = BLOCKS[j][1]
                    if n > diag:
                        nc.scalar.activation(expw[0:rows_, off + diag:off + n], abc[0:rows_, t0 + diag:t0 + n],
                                             ACT.Exp, bias=ccol[0:rows_, j * A_HEADS + hd:j * A_HEADS + hd + 1]
                                             ).then_inc(S["expw_ready"], 1)
                    if diag:
                        act.wait_ge(S["diag_ready"], (hd + 1) * NB)
                        nc.scalar.activation(expw[0:rows_, off:off + diag], expw[0:rows_, off:off + diag],
                                             ACT.Exp).then_inc(S["expw_ready"], 1)
                act.wait_ge(S["acc_ready"], hd + 1)
                nc.scalar.activation(abc[:], aux[:, 496:1024], ACT.Abs).then_inc(S["absden_ready"], 1)
                for e in range(2):
                    act.wait_ge(S["hn_ready"], 2 * hd + e + 1)
                    nc.scalar.activation(expw[:, e * T:(e + 1) * T], qk[:, hd + e * A_HEADS], ACT.Square).then_inc(
                        S["hnsq_ready"], 1)
                act.wait_ge(S["hms_ready"], hd + 1)
                nc.scalar.activation(rs_a[:], rs_a[:], ACT.Sqrt).then_inc(S["hrs_ready"], 1)

            for j in range(8):
                split_weights(S_O + 2 + j)
                act.wait_ge(S["psum_free"], Y_O + j + 1)
                nc.scalar.activation(tmp[:, j % 2], tmp[:, j % 2], ACT.Sigmoid).then_inc(S["osig_ready"], 1)
                act.wait_ge(S["ha_ready"], j + 1)
                nc.scalar.activation(c_hi[:, j], tmp[:, j % 2], ACT.Copy).then_inc(S["split_hi"], 1)
            for m in range(KT):
                split_weights(S_OUT0 + 2 + 2 * m)
                split_weights(S_OUT0 + 3 + 2 * m)
                next_operand(m, KT, "mlp_ln0", a_hi, 0)

            def mlp(s0, y0, hid, t0, q, last_quarter=None):
                for j in range(8):
                    if s0 + j + 2 < S_END:
                        split_weights(s0 + 2 + j, q * 4)
                    act.wait_ge(S["hid_ready"], hid + j + 1 + q * 8)
                    nc.scalar.activation((b_hi if y0 == Y_MLP0 else a_hi)[:, j, t0:], tmp[:, j % 2, t0:],
                                         ACT.Copy).then_inc(S["split_hi"], 1)
                for j in range(8):
                    if not (last_quarter == 1 and s0 + 8 + j + 2 + 16 * q >= S_END):
                        split_weights(s0 + 10 + j, q * 4)
                    if last_quarter == 0:
                        next_operand(j, 2 * KT, "od_ln", a_hi, 0)

            with act.Fori(0, QUARTERS - 1) as q:
                mlp(S_MLP0, Y_MLP0, 0, 0, q)
            mlp(S_MLP0, Y_MLP0, 0, 0, QUARTERS - 1, 0)
            token_factor(2)

            for j in range(5):
                split_weights(S_LORA + 2 + j)
                act.wait_ge(S["psum_free"], Y_LORA + j + 1)
                nc.scalar.activation(lora_sq[:, j], lora[:, j], ACT.Square).then_inc(S["lsq_ready"], 1)
            split_weights(S_KRFF + 2)
            act.wait_ge(S["fgf_ready"], 1)
            link(nc.scalar.activation(g_l, g_f, ACT.Abs, bias=col("od_b_f", 0, HEADS)))
            link(nc.scalar.activation(g_l, g_l, ACT.Exp, scale=-1.0))
            nc.scalar.activation(g_l, g_l, ACT.Ln, bias=1.0).then_inc(S["fgl_ready"], 1)
            act.wait_ge(S["fF_ready"], 1)
            for hd in range(HEADS):
                act.dma_start(k_aug[HD:HD + 1, hd], g_F[hd:hd + 1]).then_inc(S["augF"], 16)
            for k in range(2):
                act.wait_ge(S["lms_ready"], k + 1)
                nc.scalar.activation(tmp[:, k], tmp[:, k], ACT.Sqrt).then_inc(S["lrs_ready"], 1)
            for j in range(5):
                act.wait_ge(S["ln_ready"], j + 1)
                nc.scalar.activation(b_hi[:, j], lora[:, j], ACT.Copy).then_inc(S["split_hi"], 1)

            def item(k, y, where, rows_=P, staged=None):
                src = stg[0:rows_, k % 2] if staged is None else staged
                act.wait_ge(S["psum_free"], y + 1)
                nc.scalar.activation(tmp[0:rows_, 0], src, ACT.Square).then_inc(S["item_sq"], 1)
                act.wait_ge(S["item_ms"], k + 1)
                nc.scalar.activation(tmp[0:rows_, 1], tmp[0:rows_, 1], ACT.Sqrt).then_inc(S["item_rs"], 1)

            for k in range(8):
                split_weights(S_FQK + 2 + k)
                item(k, Y_FQK + k, None)
                act.wait_ge(S["item_done"], k + 1)
                dst = q_aug if k < 4 else k_aug
                for e in range(2):
                    act.dma_start(dst[0:HD, 2 * (k % 4) + e], stg[e * HD:(e + 1) * HD, k % 2]).then_inc(
                        item_dma[k % 2], 16)
            for j in range(4):
                split_weights(S_FV + 2 + j)
                if j:
                    copy_v(j - 1, vp[0:N_META, 0, j - 1].rearrange("p (c n) -> p c n", c=3)[:, 0:3:2],
                           vp[:, 1:NB, j - 1].rearrange("p b (c n) -> p b c n", c=3)[:, :, 0:3:2], 8, True)
            copy_v(3, vp[0:N_META, 0, 3].rearrange("p (c n) -> p c n", c=3)[:, 0:3:2],
                   vp[:, 1:NB, 3].rearrange("p b (c n) -> p b c n", c=3)[:, :, 0:3:2], 8, True)

            au = units(False)

            def attend(group, row, tile0):
                act.wait_ge(S["mxrow_ready"], group + 1)
                nc.scalar.activation(g_m[:, 0:SEQ], aux[0:HEADS, 0:SEQ], ACT.Copy, scale=-1.0).then_inc(
                    S["mxneg_ready"], 1)
                act.wait_ge(S["mxneg_ready"], group + 1)
                for hd in range(HEADS):
                    act.dma_start(q_aug[row:row + 1, hd, N_META:], g_m[hd:hd + 1, 0:SEQ]).then_inc(S["mx_dma"], 16)
                for hd in range(HEADS):
                    gh = group * HEADS + hd
                    if hd >= 2:
                        act.wait_ge(S["o_ready"], gh - 1)
                    for u, (j, t0, n, off, _) in enumerate(au):
                        act.wait_ge(S["l_ready"], gh * NB + u + 1)
                        bank = (gh * NB + u) % 4
                        nc.scalar.activation(pt[0:BLOCKS[j][1], hd % 2, off:off + n],
                                             aux[0:BLOCKS[j][1], bank * 512:bank * 512 + n], ACT.Exp).then_inc(
                            S["p_ready"], 1)
                    if hd % 2 == 1 and hd > 1:
                        pair_hi(group, hd // 2 - 1, tile0)
                pair_hi(group, 3, tile0)

            def pair_hi(group, pair, tile0):
                k = group * 4 + pair
                act.wait_ge(S["ot_ready"], 2 * k + 2)
                nc.scalar.activation(a_hi[:, tile0 + pair, N_META:], tmp[:, pair % 2, 0:SEQ], ACT.Copy).then_inc(
                    S["split_hi"], 1)

            attend(0, HD + 1, 4)

            act.wait_ge(S["mx_dma"], 16 * HEADS)
            act.dma_start(g_pos[:, N_META:], positions.to_broadcast([P, SEQ])).then_inc(S["pos_loaded"], 16)
            act.wait_ge(S["trig_arg"], 1)
            nc.scalar.activation(sq[:, 0], sq[:, 0], ACT.Sin).then_inc(S["trig_ready"], 1)
            act.wait_ge(S["trig_arg"], 2)
            nc.scalar.activation(sq[:, 1], sq[:, 1], ACT.Sin).then_inc(S["trig_ready"], 1)
            for k in range(8, 19):
                c = k - 8
                if c < 6 and c % 2 == 1:
                    split_weights(S_UQ + 2 + c // 2)
                if c == 9:
                    split_weights(S_UK + 2)
                if c < 10:
                    item(k, Y_UQ + c, None)
                else:
                    item(k, Y_UQ + 9, None, C_ROPE, kr[:])
                act.wait_ge(S["item_done"], k + 1)
                if c < 4 or 6 <= c < 10:
                    dst = q_aug if c < 4 else k_aug
                    pair = c if c < 4 else c - 6
                    for e in range(2):
                        act.dma_start(dst[0:C_NOPE, 2 * pair + e], stg[e * HD:(e + 1) * HD, k % 2]).then_inc(
                            item_dma[k % 2], 16)
                elif c < 6:
                    for e in range(4):
                        act.dma_start(q_aug[C_NOPE:C_NOPE + C_ROPE, 4 * (c - 4) + e],
                                      stg[e * C_ROPE:(e + 1) * C_ROPE, k % 2]).then_inc(item_dma[k % 2], 16)
                else:
                    for e in range(HEADS):
                        act.dma_start(k_aug[C_NOPE:C_NOPE + C_ROPE, e], kr[:]).then_inc(
                            item_dma[k % 2], 16)
            split_weights(S_UV + 2)
            for j in range(4):
                copy_v(j, vp[0:N_META, 0, j].rearrange("p (c n) -> p c n", c=3)[:, 0:3:2],
                       vp[:, 1:NB, j].rearrange("p b (c n) -> p b c n", c=3)[:, :, 0:3:2], 12, True)
            attend(1, C_NOPE + C_ROPE, 0)

            for m in range(KT):
                split_weights(S_OUT1 + 2 + m)
                next_operand(m, 3 * KT, "mlp_ln1", b_hi, N_META)
            with act.Fori(0, QUARTERS - 1) as q:
                mlp(S_MLP1, Y_MLP1, 32, N_META, q)
            mlp(S_MLP1, Y_MLP1, 32, N_META, QUARTERS - 1, 1)
            out_v = out.rearrange("(m p) t -> p m t", p=P)
            for m in range(KT):
                act.wait_ge(S["h_ready"], KT + m + 1)
                act.dma_start(out_v[:, m], h[:, m, N_META:]).then_inc(S["stored"], 16)
            act.wait_ge(S["stored"], 16 * KT)

        @block.vector
        def _(dve):
            chain = [0]

            def link(ins):
                chain[0] += 1
                ins.then_inc(S["dve_chain"], 1)
                dve.wait_ge(S["dve_chain"], chain[0])

            def split_weights(nb, i4=0):
                dve.wait_ge(S["w_hi_ready"], nb + 1 + i4 * 4)
                nc.vector.tensor_tensor(w_lo[:, nb % 2], raw[:, nb % 4], w_hi[:, nb % 2].bitcast(F32),
                                        ALU.subtract).then_inc(S["w_lo_ready"], 1)

            def next_operand(m, base, gain, hi, lo, t0):
                dve.wait_ge(S["a_hi_ready"], base + m + 1)
                nc.vector.scalar_tensor_tensor(out=lo[:, m, t0:], in0=h[:, m, t0:], scalar=col(gain, m),
                                               in1=hi[:, m, t0:].bitcast(F32), op0=ALU.mult,
                                               op1=ALU.subtract).then_inc(S["operand_ready"], 1)

            def split_low(lo, hi, full, hi_count):
                dve.wait_ge(S["split_hi"], hi_count)
                nc.vector.tensor_tensor(lo, full, hi.bitcast(F32), ALU.subtract).then_inc(S["operand_ready"], 1)

            def mean_square(k, bank, t0):
                dve.wait_ge(S["stat_ready"], k + 1)
                if t0:
                    o, i = inv_ms[:, t0:], aux[:, bank * 512:bank * 512 + SEQ]
                else:
                    o, i = two(inv_ms[:]), aux_two(bank)
                link(nc.vector.tensor_scalar(o, i, 1.0 / D_MODEL, EPS, ALU.mult, ALU.add))
                nc.vector.reciprocal(inv_ms[:, t0:], inv_ms[:, t0:]).then_inc(S["ms_ready"], 1)

            dve.wait_ge(S["lam_e_ready"], 1)
            lam = cols[:, COLS["lam"][0]:COLS["lam"][0] + KT]
            link(nc.vector.tensor_scalar(spt[:, 1], spt[:, 0], 2.0, None, ALU.add))
            link(nc.vector.reciprocal(spt[:, 1], spt[:, 1]))
            link(nc.vector.tensor_tensor(spt[:, 1], spt[:, 0], spt[:, 1], ALU.mult))
            link(nc.vector.tensor_tensor(spt[:, 2], spt[:, 1], spt[:, 1], ALU.mult))
            link(nc.vector.tensor_scalar(spt[:, 3], spt[:, 2], 1.0 / 15, None, ALU.mult))
            for k in (13, 11, 9, 7, 5, 3):
                link(nc.vector.scalar_tensor_tensor(out=spt[:, 3], in0=spt[:, 3], scalar=1.0 / k, in1=spt[:, 2],
                                                    op0=ALU.add, op1=ALU.mult))
            link(nc.vector.scalar_tensor_tensor(out=spt[:, 3], in0=spt[:, 3], scalar=1.0, in1=spt[:, 1],
                                                op0=ALU.add, op1=ALU.mult))
            link(nc.vector.tensor_scalar(spt[:, 4], lam, -1.0, 0.0, ALU.mult, ALU.max))
            link(nc.vector.scalar_tensor_tensor(out=spt[:, 3], in0=spt[:, 3], scalar=2.0, in1=spt[:, 4],
                                                op0=ALU.mult, op1=ALU.add))
            nc.vector.tensor_scalar(sp4[:], spt[:, 3], 4.0, None, ALU.mult).then_inc(S["sp4_ready"], 1)

            for m in range(KT):
                next_operand(m, 0, "ev_ln", a_hi, a_lo, 0)
                if m < 2:
                    split_weights(m)
            mean_square(0, 0, 0)
            dve.wait_ge(S["rstd_ready"], 1)

            def recurrence(g):
                dve.wait_ge(S["tanh_ready"], g + 1)
                if g:
                    dve.wait_ge(S["decay_ready"], g)
                link(nc.vector.tensor_scalar(den_t[:], gate_r[:], 1.0, None, ALU.add))
                nc.vector.reciprocal(den_t[:], den_t[:]).then_inc(S["den_ready"], 1)
                dve.wait_ge(S["sd_ready"], g + 1)
                dve.wait_ge(S["ix_ready"], g + 1)
                nc.vector.tensor_tensor(gate_i[:], gate_i[:], sqrt_t[:], ALU.mult).then_inc(S["u_ready"], 1)
                dve.wait_ge(S["decay_ready"], g + 1)
                dve.wait_ge(S["u_ready"], g + 1)
                nc.vector.tensor_tensor_scan(hs[:], decay[:], gate_i[:], 0.0, ALU.mult, ALU.add).then_inc(
                    S["hs_ready"], 1)
                dve.wait_ge(S["gelu_ready"], g + 1)
                dve.wait_ge(S["hs_ready"], g + 1)
                nc.vector.tensor_tensor(hs[:], hs[:], gel[:], ALU.mult).then_inc(S["hb_ready"], 1)

            for g in range(KT):
                dve.wait_ge(S["w_used"], 2 * g + 1)
                nc.vector.tensor_tensor(two(xb[:, 3:T + 3]), slot(2 * g), two(rstd[:]), ALU.mult).then_inc(
                    S["psum_free"], 1)
                split_weights(2 * g + 2)
                dve.wait_ge(S["conv0_ready"], g + 1)
                for j in (1, 2):
                    link(nc.vector.scalar_tensor_tensor(out=xc[:], in0=xb[:, j:j + T], scalar=col("conv_w", j * KT + g),
                                                        in1=xc[:], op0=ALU.mult, op1=ALU.add))
                nc.vector.scalar_tensor_tensor(out=xc[:], in0=xb[:, 3:3 + T], scalar=col("conv_w", 3 * KT + g),
                                               in1=xc[:], op0=ALU.mult, op1=ALU.add).then_inc(S["xc_ready"], 1)
                if g:
                    recurrence(g - 1)
                dve.wait_ge(S["w_used"], 2 * g + 2)
                nc.vector.tensor_tensor(two(gb[:]), slot(2 * g + 1), two(rstd[:]), ALU.mult).then_inc(
                    S["psum_free"], 1)
                split_weights(2 * g + 3)
                if g:
                    split_low(b_lo[:, g - 1], b_hi[:, g - 1], hs[:], g)
            recurrence(KT - 1)
            split_low(b_lo[:, KT - 1], b_hi[:, KT - 1], hs[:], KT)

            dve.wait_ge(S["w_used"], S_GATES + 1)
            link(nc.vector.tensor_tensor(two(g_i[0:A_HEADS]), slot(Y_GATES, A_HEADS), two(rstd[0:A_HEADS]), ALU.mult))
            nc.vector.tensor_tensor(two(g_f[0:A_HEADS]), slot(Y_GATES, A_HEADS, 32), two(rstd[32:32 + A_HEADS]),
                                    ALU.mult).then_inc(S["psum_free"], 1)
            dve.wait_ge(S["psum_free"], Y_GATES + 1)
            nc.vector.memset(g_m[0:A_HEADS], 0.0).then_inc(S["gf_ready"], 1)
            split_weights(S_GATES + 2)
            link(nc.vector.tensor_scalar(g_i[0:A_HEADS], g_i[0:A_HEADS], col("b_i", 0, A_HEADS), None, ALU.add))
            dve.wait_ge(S["gl_ready"], 1)
            link(nc.vector.tensor_scalar(g_f[0:A_HEADS], g_f[0:A_HEADS], col("b_f", 0, A_HEADS), 0.0, ALU.add, ALU.min))
            link(nc.vector.tensor_tensor(g_l[0:A_HEADS], g_f[0:A_HEADS], g_l[0:A_HEADS], ALU.subtract))
            link(nc.vector.tensor_tensor_scan(g_F[0:A_HEADS], g_l[0:A_HEADS], g_m[0:A_HEADS], 0.0, ALU.add, ALU.add))
            link(nc.vector.tensor_tensor_scan(g_m[0:A_HEADS], g_l[0:A_HEADS], g_i[0:A_HEADS], 0.0, ALU.add, ALU.max))
            link(nc.vector.tensor_tensor(g_i[0:A_HEADS], g_i[0:A_HEADS], g_F[0:A_HEADS], ALU.subtract))
            link(nc.vector.tensor_tensor(g_F[0:A_HEADS], g_F[0:A_HEADS], g_m[0:A_HEADS], ALU.subtract))
            nc.vector.tensor_scalar(g_m[0:A_HEADS], g_m[0:A_HEADS], -1.0, None, ALU.mult).then_inc(S["rows_ready"], 1)
            for j in range(8):
                dve.wait_ge(S["w_used"], S_QK + j + 1)
                nc.vector.tensor_tensor(two(qk[:, j]), slot(Y_QK + j), two(rstd[:]), ALU.mult).then_inc(
                    S["psum_free"], 1)
                split_weights(S_QK + 2 + j)
            for j in range(8):
                dve.wait_ge(S["w_used"], S_V + j + 1)
                if j >= 2:
                    dve.wait_ge(S["vt_ready"], j - 1)
                nc.vector.tensor_tensor(two(tmp[:, j % 2]), slot(Y_V + j), two(rstd[:]), ALU.mult).then_inc(
                    S["psum_free"], 1)
                split_weights(S_V + 2 + j)

            mu = units(True)
            for hd in range(A_HEADS):
                dve.wait_ge(S["abc_ready"], hd + 1)
                if hd == 0:
                    dve.wait_ge(S["ccol_ready"], 1)
                    dve.wait_ge(S["const_loaded"], 16)
                for j, t0, n, off, diag in mu:
                    if diag:
                        rows_ = BLOCKS[j][1]
                        nc.vector.scalar_tensor_tensor(
                            out=expw[0:rows_, off:off + diag], in0=abc[0:rows_, t0:t0 + diag],
                            scalar=ccol[0:rows_, j * A_HEADS + hd:j * A_HEADS + hd + 1],
                            in1=cm(C_MASK_ST, rows_, diag), op0=ALU.add, op1=ALU.add).then_inc(S["diag_ready"], 1)
                done = 0
                for u, (j, t0, n, off, diag) in enumerate(mu):
                    rows_ = BLOCKS[j][1]
                    done += (n > diag) + (diag > 0)
                    dve.wait_ge(S["expw_ready"], hd * N_EXP + done)
                    dve.wait_ge(S["s_ready"], hd * len(mu) + u + 1)
                    bank = 2 + u % 2
                    nc.vector.scalar_tensor_tensor(
                        out=st[0:rows_, off:off + n], in0=aux[0:rows_, bank * 512:bank * 512 + n],
                        scalar=float(A_DQK) ** -0.5, in1=expw[0:rows_, off:off + n], op0=ALU.mult,
                        op1=ALU.mult).then_inc(S["st_ready"], 1)
                dve.wait_ge(S["absden_ready"], hd + 1)
                dve.wait_ge(S["em_ready"], hd + 1)
                link(nc.vector.tensor_tensor(abc[:], abc[:], em[:], ALU.max))
                link(nc.vector.reciprocal(abc[:], abc[:]))
                for e in range(2):
                    nc.vector.tensor_tensor(qk[:, hd + e * A_HEADS], prod[:, e, 496:1024], abc[:], ALU.mult).then_inc(
                        S["hn_ready"], 1)
                dve.wait_ge(S["hstat_ready"], hd + 1)
                link(nc.vector.tensor_scalar(two(rs_a[:]), aux_two(2), 1.0 / A_DV, EPS, ALU.mult, ALU.add))
                nc.vector.reciprocal(rs_a[:], rs_a[:]).then_inc(S["hms_ready"], 1)
                dve.wait_ge(S["hrs_ready"], hd + 1)
                for e in range(2):
                    last = nc.vector.scalar_tensor_tensor(out=qk[:, hd + e * A_HEADS], in0=qk[:, hd + e * A_HEADS],
                                                          scalar=col("a_norm", e), in1=rs_a[:], op0=ALU.mult,
                                                          op1=ALU.mult)
                last.then_inc(S["head_done"], 1)

            dve.wait_ge(S["head_done"], A_HEADS)
            for j in range(8):
                dve.wait_ge(S["w_used"], S_O + j + 1)
                if j >= 2:
                    dve.wait_ge(S["split_hi"], KT + j - 1)
                nc.vector.tensor_tensor(two(tmp[:, j % 2]), slot(Y_O + j), two(rstd[:]), ALU.mult).then_inc(
                    S["psum_free"], 1)
                split_weights(S_O + 2 + j)
                dve.wait_ge(S["osig_ready"], j + 1)
                nc.vector.tensor_tensor(tmp[:, j % 2], tmp[:, j % 2], qk[:, j // 2 + (j % 2) * A_HEADS],
                                        ALU.mult).then_inc(S["ha_ready"], 1)
                split_low(c_lo[:, j], c_hi[:, j], tmp[:, j % 2], KT + j + 1)

            for m in range(KT):
                dve.wait_ge(S["w_used"], S_OUT0 + 2 * m + 1)
                split_weights(S_OUT0 + 2 + 2 * m)
                dve.wait_ge(S["w_used"], S_OUT0 + 2 * m + 2)
                nc.vector.tensor_tensor(two(h[:, m]), slot(Y_OUT0 + m), two(h[:, m]), ALU.add).then_inc(
                    S["psum_free"], 1)
                split_weights(S_OUT0 + 3 + 2 * m)
                next_operand(m, KT, "mlp_ln0", a_hi, a_lo, 0)
            mean_square(1, 0, 0)

            def mlp(s0, y0, hi0, t0, q, layer, last=False):
                real = t0 > 0
                x_hi, x_lo = (b_hi, b_lo) if layer == 0 else (a_hi, a_lo)
                for j in range(8):
                    y = y0 + j
                    dve.wait_ge(S["w_used"], s0 + j + 1 + q * 16)
                    if real:
                        o, i = tmp[:, j % 2, t0:], slot_real(y)
                    else:
                        o, i = two(tmp[:, j % 2]), slot(y)
                    nc.vector.tensor_scalar(o, i, 0.0, None, ALU.max).then_inc(S["psum_free"], 1)
                    split_weights(s0 + 2 + j, q * 4)
                    dve.wait_ge(S["split_hi"], hi0 + j + 1 + q * 8)
                    nc.vector.tensor_tensor(x_lo[:, j, t0:], tmp[:, j % 2, t0:], x_hi[:, j, t0:].bitcast(F32),
                                            ALU.subtract).then_inc(S["operand_ready"], 1)
                for j in range(8):
                    y = y0 + 8 + j
                    dve.wait_ge(S["w_used"], s0 + 8 + j + 1 + q * 16)
                    if real:
                        o, i, f = tmp[:, j % 2, t0:], slot_real(y), inv_ms[:, t0:]
                    else:
                        o, i, f = two(tmp[:, j % 2]), slot(y), two(inv_ms[:])
                    nc.vector.tensor_tensor(o, i, f, ALU.mult).then_inc(S["psum_free"], 1)
                    if not (last and layer == 1 and j >= 6):
                        split_weights(s0 + 10 + j, q * 4)
                    dve.wait_ge(S["psum_free"], y + 1 + q * 16)
                    add = nc.vector.tensor_tensor(h[:, j, t0:], h[:, j, t0:], tmp[:, j % 2, t0:], ALU.add)
                    if last:
                        add.then_inc(S["h_ready"], 1)
                        if layer == 0:
                            next_operand(j, 2 * KT, "od_ln", a_hi, a_lo, 0)

            with dve.Fori(0, QUARTERS - 1) as q:
                mlp(S_MLP0, Y_MLP0, 2 * KT, 0, q, 0)
            mlp(S_MLP0, Y_MLP0, 2 * KT, 0, QUARTERS - 1, 0, True)
            HI = 2 * KT + KT * QUARTERS
            mean_square(2, 0, 0)

            dve.wait_ge(S["rstd_ready"], 2)
            for j in range(5):
                dve.wait_ge(S["w_used"], S_LORA + j + 1)
                nc.vector.tensor_tensor(two(lora[:, j]), slot(Y_LORA + j), two(rstd[:]), ALU.mult).then_inc(
                    S["psum_free"], 1)
                split_weights(S_LORA + 2 + j)
            dve.wait_ge(S["w_used"], S_KRFF + 1)
            link(nc.vector.tensor_tensor(two(kr[:]), slot(Y_KRFF, C_ROPE), two(rstd[0:C_ROPE]), ALU.mult))
            nc.vector.tensor_tensor(two(g_f), slot(Y_KRFF, HEADS, 32), two(rstd[32:32 + HEADS]),
                                    ALU.mult).then_inc(S["psum_free"], 1)
            dve.wait_ge(S["psum_free"], Y_KRFF + 1)
            nc.vector.memset(g_m, 0.0).then_inc(S["fgf_ready"], 1)
            split_weights(S_KRFF + 2)
            link(nc.vector.memset(q_aug[HD:HD + 2], 1.0))
            nc.vector.memset(k_aug[HD:HD + 2], 1.0).then_inc(S["aug_one"], 1)
            dve.wait_ge(S["aug_one"], 1)
            dve.wait_ge(S["fgl_ready"], 1)
            link(nc.vector.tensor_scalar(g_f, g_f, col("od_b_f", 0, HEADS), 0.0, ALU.add, ALU.min))
            link(nc.vector.tensor_tensor(g_l, g_l, g_f, ALU.subtract))
            nc.vector.tensor_tensor_scan(g_F, g_l, g_m, 0.0, ALU.add, ALU.add).then_inc(S["fF_ready"], 1)
            for k, (n, width) in enumerate(((3, Q_LORA), (2, KV_LORA))):
                dve.wait_ge(S["lstat_ready"], k + 1)
                link(nc.vector.tensor_scalar(two(tmp[:, k]), aux_two(2 * k), 1.0 / width, EPS, ALU.mult, ALU.add))
                nc.vector.reciprocal(tmp[:, k], tmp[:, k]).then_inc(S["lms_ready"], 1)
            for j in range(5):
                dve.wait_ge(S["lrs_ready"], 1 if j < 3 else 2)
                nc.vector.scalar_tensor_tensor(out=lora[:, j], in0=lora[:, j],
                                               scalar=col("g_qa", j) if j < 3 else col("g_kva", j - 3),
                                               in1=tmp[:, 0 if j < 3 else 1], op0=ALU.mult, op1=ALU.mult).then_inc(
                    S["ln_ready"], 1)
            for j in range(5):
                split_low(b_lo[:, j], b_hi[:, j], lora[:, j], HI + j + 1)

            link(nc.vector.memset(vp[:, :, :, HD:2 * HD], 1.0))

            def item_evac(k, y, ready, dma_counts):
                dve.wait_ge(ready[0], ready[1])
                if dma_counts[k % 2]:
                    dve.wait_ge(item_dma[k % 2], dma_counts[k % 2])
                factor = two(rstd[:])
                if y >= Y_UQ:
                    nc.vector.tensor_copy(two(stg[:, k % 2]), slot(y)).then_inc(S["psum_free"], 1)
                else:
                    nc.vector.tensor_tensor(two(stg[:, k % 2]), slot(y), factor, ALU.mult).then_inc(
                        S["psum_free"], 1)

            def item_finish(k, gain, scale, rows_=P, rope=False, staged=None):
                x = stg[0:rows_, k % 2] if staged is None else staged
                t = tmp[0:rows_, 1]
                dve.wait_ge(S["item_stat"], k + 1)
                link(nc.vector.tensor_scalar(two(t), aux_two(0, rows_), 1.0 / scale ** 2, EPS / scale ** 2, ALU.mult,
                                             ALU.add))
                nc.vector.reciprocal(t, t).then_inc(S["item_ms"], 1)
                dve.wait_ge(S["item_rs"], k + 1)
                ins = nc.vector.scalar_tensor_tensor(out=x, in0=x, scalar=col(gain, 0, rows_), in1=t, op0=ALU.mult,
                                                     op1=ALU.mult)
                if rope:
                    ins.then_inc(S["ln_ready"], 1)
                    rope_count[0] += 1
                    dve.wait_ge(S["item_rot"], rope_count[0])
                    dve.wait_ge(S["trig_ready"], 2)
                    link(nc.vector.tensor_tensor(two(t), aux_two(2, rows_), two(sq[0:rows_, 0]), ALU.mult))
                    link(nc.vector.tensor_tensor(x, x, sq[0:rows_, 1], ALU.mult))
                    ins = nc.vector.tensor_tensor(x, x, t, ALU.add)
                ins.then_inc(S["item_done"], 1)

            rope_count = [0]
            sent = [0, 0]
            scale_d, scale_c = float(HD) ** -0.5, float(C_NOPE + C_ROPE) ** -0.5
            for k in range(8):
                item_evac(k, Y_FQK + k, (S["w_used"], S_FQK + k + 1), sent)
                split_weights(S_FQK + 2 + k)
                item_finish(k, "g_fq" if k < 4 else "g_fk", scale_d if k < 4 else 1.0)
                sent[k % 2] += 32
            for j in range(4):
                dve.wait_ge(S["w_used"], S_FV + j + 1)
                if j >= 2:
                    dve.wait_ge(S["vt_ready"], 8 + j - 1)
                nc.vector.tensor_tensor(two(tmp[:, j % 2]), slot(Y_FV + j), two(rstd[:]), ALU.mult).then_inc(
                    S["psum_free"], 1)
                split_weights(S_FV + 2 + j)

            au = units(False)

            def attend(group, tile0):
                for hd in range(HEADS):
                    for i in range(4):
                        k = (group * HEADS + hd) * 4 + i
                        dve.wait_ge(S["logit_ready"], k + 1)
                        src = prod[:, k % 4, 496:512 + P * (i + 1)] if k % 4 < 2 else \
                            aux[:, (k % 4 - 2) * 1024 + 496:(k % 4 - 2) * 1024 + 512 + P * (i + 1)]
                        nc.vector.reduce_max(maxes[:, i, hd:hd + 1], src, AX.X).then_inc(S["max_ready"], 1)
                for hd in range(HEADS):
                    gh = group * HEADS + hd
                    pair = hd // 2
                    lo_, hi_ = (0, HD) if hd % 2 == 0 else (HD, 0)
                    dve.wait_ge(S["o_ready"], gh + 1)
                    if hd % 2 == 0 and pair >= 2:
                        dve.wait_ge(S["split_hi"], HI + 5 + group * 4 + pair - 1)
                    o = prod[:, gh % 2, 0:SEQ]
                    link(nc.vector.reciprocal(stg[lo_:lo_ + HD, 0, 0:SEQ], o[hi_:hi_ + HD]))
                    nc.vector.tensor_tensor(tmp[lo_:lo_ + HD, pair % 2, 0:SEQ], o[lo_:lo_ + HD],
                                            stg[lo_:lo_ + HD, 0, 0:SEQ], ALU.mult).then_inc(S["ot_ready"], 1)
                    if hd % 2 == 1:
                        split_low(a_lo[:, tile0 + pair, N_META:], a_hi[:, tile0 + pair, N_META:],
                                  tmp[:, pair % 2, 0:SEQ], HI + 5 + group * 4 + pair + 1)

            attend(0, 4)

            dve.wait_ge(S["pos_loaded"], 16)
            dve.wait_ge(S["trig_pos"], 1)
            two_pi = 2.0 * np.pi
            c1 = 6.28125
            c2 = float(np.float32(0.0019350051879882812))
            c3 = float(two_pi - c1 - c2)
            magic = 12582912.0
            link(nc.vector.tensor_copy(stg[:, 0], g_pos))
            link(nc.vector.tensor_scalar(stg[:, 0, N_META:], stg[:, 0, N_META:], float(N_META), None, ALU.add))
            link(nc.vector.tensor_scalar(stg[:, 0], stg[:, 0], col("freq"), None, ALU.mult))
            for k, shift in ((0, 0.0), (1, 0.25)):
                t, r = stg[:, 1], sq[:, k]
                link(nc.vector.tensor_scalar(t, stg[:, 0], 1.0 / two_pi, shift, ALU.mult, ALU.add))
                link(nc.vector.tensor_scalar(t, t, magic, None, ALU.add))
                link(nc.vector.tensor_scalar(t, t, magic, None, ALU.subtract))
                link(nc.vector.scalar_tensor_tensor(out=r, in0=t, scalar=-c1, in1=stg[:, 0], op0=ALU.mult,
                                                    op1=ALU.add))
                link(nc.vector.scalar_tensor_tensor(out=r, in0=t, scalar=-c2, in1=r, op0=ALU.mult, op1=ALU.add))
                link(nc.vector.scalar_tensor_tensor(out=r, in0=t, scalar=-c3, in1=r, op0=ALU.mult, op1=ALU.add))
                if k:
                    link(nc.vector.tensor_scalar(r, r, float(np.pi / 2), None, ALU.add))
                nc.vector.tensor_scalar(r, r, 3.1415925, -3.1415925, ALU.min, ALU.max).then_inc(S["trig_arg"], 1)
            dve.wait_ge(S["trig_arg"], 2)

            for k in range(8, 19):
                c = k - 8
                if c < 10:
                    if c < 6:
                        ready = (S["part_ready"], c // 2 + 1) if c % 2 == 0 else (S["w_used"], S_UQ + c // 2 + 1)
                    else:
                        ready = (S["part_ready"], 3 + c - 5) if c < 9 else (S["w_used"], S_UK + 1)
                    item_evac(k, Y_UQ + c, ready, sent)
                if c < 6 and c % 2 == 1:
                    split_weights(S_UQ + 2 + c // 2)
                if c == 9:
                    split_weights(S_UK + 2)
                if c < 4:
                    item_finish(k, "g_qn", scale_c)
                    sent[k % 2] += 32
                elif c < 6:
                    item_finish(k, "g_qr", scale_c, P, True)
                    sent[k % 2] += 64
                elif c < 10:
                    item_finish(k, "g_kn", 1.0)
                    sent[k % 2] += 32
                else:
                    item_finish(k, "g_kr", 1.0, C_ROPE, True, kr[:])
                    nc.vector.memset(k_aug[96:97], 1.0).then_inc(S["aug_one"], 1)
            for j in range(4):
                if j < 3:
                    dve.wait_ge(S["part_ready"], 6 + j + 1)
                else:
                    dve.wait_ge(S["w_used"], S_UV + 1)
                if j >= 2:
                    dve.wait_ge(S["vt_ready"], 12 + j - 1)
                nc.vector.tensor_copy(two(tmp[:, j % 2]), slot(Y_UV + j)).then_inc(S["psum_free"], 1)
            split_weights(S_UV + 2)
            attend(1, 0)

            for m in range(KT):
                dve.wait_ge(S["w_used"], S_OUT1 + m + 1)
                nc.vector.tensor_tensor(h[:, m, N_META:], slot_real(Y_OUT1 + m), h[:, m, N_META:], ALU.add).then_inc(
                    S["psum_free"], 1)
                split_weights(S_OUT1 + 2 + m)
                next_operand(m, 3 * KT, "mlp_ln1", b_hi, b_lo, N_META)
            mean_square(3, 0, N_META)
            HI1 = HI + 5 + 8
            with dve.Fori(0, QUARTERS - 1) as q:
                mlp(S_MLP1, Y_MLP1, HI1, N_META, q, 1)
            mlp(S_MLP1, Y_MLP1, HI1, N_META, QUARTERS - 1, 1, True)

        @block.tensor
        def _(pe):
            FULL = ((0, 0, HALF), (512, HALF, HALF))
            REAL = ((0, N_META, SEQ),)

            def product(nb, y, x, spans, q16=0, k0=0, nk=8, kb=0, start=True, stop=True, waits=None):
                hi, lo = x
                if start and y >= 2:
                    pe.wait_ge(S["psum_free"], y - 1 + q16)
                pe.wait_ge(S["w_lo_ready"], nb + 1 + q16)
                for k in range(nk):
                    if waits is not None:
                        pe.wait_ge(S["operand_ready"], waits + k + 1)
                    blk = slice((k0 + k) * P, (k0 + k + 1) * P)
                    for i, (w, xx) in enumerate(((w_hi, hi), (w_hi, lo), (w_lo, hi))):
                        for c, t0, n in spans:
                            last = nc.tensor.matmul(prod[:, y % 2, c:c + n], w[:, nb % 2, blk],
                                                    xx[:, kb + k, t0:t0 + n], start=start and k == 0 and i == 0,
                                                    stop=stop and k == nk - 1 and i == 2)
                return last

            A, B, C = (a_hi, a_lo), (b_hi, b_lo), (c_hi, c_lo)

            def stats(k, t0=0):
                pe.wait_ge(S["sq_summed"], (k + 1) * KT)
                if t0:
                    nc.tensor.matmul(aux[:, 0:SEQ], cm(C_ONES), sq_sum[:, t0:], start=True, stop=True).then_inc(
                        S["stat_ready"], 1)
                else:
                    for c, f, n in FULL:
                        last = nc.tensor.matmul(aux[:, c:c + n], cm(C_ONES), sq_sum[:, f:f + n], start=True, stop=True)
                    last.then_inc(S["stat_ready"], 1)

            for g in range(KT):
                product(2 * g, 2 * g, A, FULL, waits=R_X0 if g == 0 else None).then_inc(S["w_used"], 1)
                if g == 0:
                    pe.wait_ge(S["const_loaded"], 16)
                    stats(0)
                    pe.wait_ge(S["wr_loaded"], 16)
                    pe.wait_ge(S["ms_ready"], 1)
                product(2 * g + 1, 2 * g + 1, A, FULL).then_inc(S["w_used"], 1)
                pe.wait_ge(S["xc_ready"], g + 1)
                if g:
                    pe.wait_ge(S["sig_ready"], g)
                for which in range(2):
                    for c, f, n in FULL:
                        last = nc.tensor.matmul(aux[:, which * 1024 + c:which * 1024 + c + n],
                                                wr[:, (which * KT + g) * P:(which * KT + g + 1) * P], xc[:, f:f + n],
                                                start=True, stop=True)
                last.then_inc(S["gates_ready"], 1)
            product(S_GATES, Y_GATES, A, FULL).then_inc(S["w_used"], 1)
            for j in range(8):
                product(S_QK + j, Y_QK + j, A, FULL).then_inc(S["w_used"], 1)

            def transpose_v(j, y, base):
                pe.wait_ge(S["psum_free"], y + 1)
                if base + j >= 2:
                    pe.wait_ge(S["v_copied"], base + j - 1)
                a = (j % 2) * 1024
                for b, (t0, n) in enumerate(BLOCKS):
                    c = a if b == 0 else a + 512 + (b - 1) * P
                    last = nc.tensor.transpose(aux[0:n, c:c + P], tmp[:, j % 2, t0:t0 + n], cm(C_IDENT))
                last.then_inc(S["vt_ready"], 1)

            pe.wait_ge(S["sig_ready"], KT)
            for j in range(8):
                product(S_V + j, Y_V + j, A, FULL).then_inc(S["w_used"], 1)
                if j:
                    transpose_v(j - 1, Y_V + j - 1, 0)
            transpose_v(7, Y_V + 7, 0)

            pe.wait_ge(S["rows_ready"], 1)
            pe.wait_ge(S["v_copied"], 8)
            for j, (t0, n) in enumerate(BLOCKS):
                last = nc.tensor.matmul(aux[0:n, j * A_HEADS:(j + 1) * A_HEADS], g_i[0:A_HEADS, t0:t0 + n],
                                        cm(C_IDENT, A_HEADS, A_HEADS), start=True, stop=True)
            last.then_inc(S["ccol_psum"], 1)
            pe.wait_ge(S["ccol_ready"], 1)
            pe.wait_ge(S["psum_free"], Y_V + 8)
            mu = units(True)
            for hd in range(A_HEADS):
                if hd:
                    pe.wait_ge(S["hms_ready"], hd)
                for k, row in enumerate((g_F, g_m)):
                    if k:
                        pe.wait_ge(S["abc_ready"], hd + 1)
                    for c, f, n in FULL:
                        last = nc.tensor.matmul(aux[:, 1024 + c:1024 + c + n], cm(C_SEL + hd, A_HEADS),
                                                row[0:A_HEADS, f:f + n], start=True, stop=True)
                    last.then_inc(S["bc_ready"], 1)
                pe.wait_ge(S["em_ready"], hd + 1)

                def scores(u):
                    j, t0, n, off, _ = mu[u]
                    if u >= 2:
                        pe.wait_ge(S["st_ready"], hd * len(mu) + u - 1)
                    b = (2 + u % 2) * 512
                    nc.tensor.matmul(aux[0:BLOCKS[j][1], b:b + n],
                                     qk[:, A_HEADS + hd, BLOCKS[j][0]:BLOCKS[j][0] + BLOCKS[j][1]],
                                     qk[:, hd, t0:t0 + n], start=True, stop=True).then_inc(S["s_ready"], 1)

                scores(0)
                for u, (j, t0, n, off, _) in enumerate(mu):
                    if u + 1 < len(mu):
                        scores(u + 1)
                    rows_ = BLOCKS[j][1]
                    pe.wait_ge(S["st_ready"], hd * len(mu) + u + 1)
                    for e in range(3):
                        acc = prod[:, e, 496 + t0:496 + t0 + n] if e < 2 else aux[:, 496 + t0:496 + t0 + n]
                        w = v[0:rows_, j, hd * A_DV + e * P:hd * A_DV + (e + 1) * P] if e < 2 else cm(C_ONES, rows_)
                        last = nc.tensor.matmul(acc, w, st[0:rows_, off:off + n], start=u <= 1,
                                                stop=u in (0, len(mu) - 1))
                last.then_inc(S["acc_ready"], 1)
                pe.wait_ge(S["hnsq_ready"], 2 * hd + 2)
                for e in range(2):
                    for c, f, n in FULL:
                        last = nc.tensor.matmul(aux[:, 1024 + c:1024 + c + n], cm(C_ONES),
                                                expw[:, e * T + f:e * T + f + n], start=e == 0, stop=e == 1)
                last.then_inc(S["hstat_ready"], 1)

            for j in range(8):
                product(S_O + j, Y_O + j, A, FULL).then_inc(S["w_used"], 1)
            for m in range(KT):
                first = m == 0
                product(S_OUT0 + 2 * m, Y_OUT0 + m, B, FULL, stop=False).then_inc(S["w_used"], 1)
                product(S_OUT0 + 2 * m + 1, Y_OUT0 + m, C, FULL, start=False,
                        waits=R_HA if first else None).then_inc(S["w_used"], 1)
            stats(1)

            def mlp(s0, y0, r_hid, x, hid, spans, q, first_wait, q8):
                for j in range(8):
                    product(s0 + j, y0 + j, x, spans, q * 16, waits=first_wait if j == 0 else None).then_inc(
                        S["w_used"], 1)
                for j in range(8):
                    product(s0 + 8 + j, y0 + 8 + j, hid, spans, q * 16,
                            waits=(r_hid + q * 8) if j == 0 else None).then_inc(S["w_used"], 1)

            pe.wait_ge(S["operand_ready"], R_X1 + KT)
            with pe.Fori(0, QUARTERS - 1) as q:
                mlp(S_MLP0, Y_MLP0, R_MLP0, A, B, FULL, q, None, None)
            mlp(S_MLP0, Y_MLP0, R_MLP0, A, B, FULL, QUARTERS - 1, None, None)

            product(S_LORA, Y_LORA, A, FULL, waits=R_X2).then_inc(S["w_used"], 1)
            stats(2)
            for j in range(1, 5):
                product(S_LORA + j, Y_LORA + j, A, FULL).then_inc(S["w_used"], 1)
            product(S_KRFF, Y_KRFF, A, FULL).then_inc(S["w_used"], 1)
            pe.wait_ge(S["ms_ready"], 3)
            for k, (j0, n_) in enumerate(((0, 3), (3, 2))):
                pe.wait_ge(S["lsq_ready"], j0 + n_)
                for j in range(n_):
                    for c, f, n in FULL:
                        last = nc.tensor.matmul(aux[:, k * 1024 + c:k * 1024 + c + n], cm(C_ONES),
                                                lora_sq[:, j0 + j, f:f + n], start=j == 0, stop=j == n_ - 1)
                last.then_inc(S["lstat_ready"], 1)

            def item_stat(k, mat, rows_=P):
                pe.wait_ge(S["item_sq"], k + 1)
                if k == 0:
                    pe.wait_ge(S["lms_ready"], 2)
                else:
                    pe.wait_ge(S["item_ms"], k)
                for c, f, n in FULL:
                    last = nc.tensor.matmul(aux[0:rows_, c:c + n], cm(mat, rows_, rows_), tmp[0:rows_, 0, f:f + n],
                                            start=True, stop=True)
                last.then_inc(S["item_stat"], 1)

            def rotate(k, count, rows_, x):
                pe.wait_ge(S["ln_ready"], 5 + count)
                for c, f, n in FULL:
                    last = nc.tensor.matmul(aux[0:rows_, 1024 + c:1024 + c + n], cm(C_ROT, rows_, rows_),
                                            x[:, f:f + n], start=True, stop=True)
                last.then_inc(S["item_rot"], 1)

            for k in range(8):
                product(S_FQK + k, Y_FQK + k, A, FULL).then_inc(S["w_used"], 1)
                item_stat(k, C_BLK64)
            for j in range(4):
                product(S_FV + j, Y_FV + j, A, FULL).then_inc(S["w_used"], 1)
                if j == 1:
                    pe.wait_ge(S["item_ms"], 8)
                if j:
                    transpose_v(j - 1, Y_FV + j - 1, 8)
            transpose_v(3, Y_FV + 3, 8)

            au = units(False)

            def attend(group, k_rows, row_count, dma_wait):
                for s, val in dma_wait:
                    pe.wait_ge(s, val)
                pe.wait_ge(S["bf_ready"], 3)
                for hd in range(HEADS):
                    for i in range(4):
                        k = (group * HEADS + hd) * 4 + i
                        if k >= 4 and (hd > 0 or i > 3):
                            pe.wait_ge(S["max_ready"], k - 3)
                        o = prod[:, k % 4] if k % 4 < 2 else aux[:, (k % 4 - 2) * 1024:(k % 4 - 1) * 1024]
                        qs = q_aug[0:k_rows, hd, BLOCKS[i + 1][0]:BLOCKS[i + 1][0] + P]
                        n = P * (i + 1)
                        nc.tensor.matmul(o[:, 496:512], qs, k_aug[0:k_rows, hd, 0:N_META], start=True, stop=True)
                        nc.tensor.matmul(o[:, 512:512 + n], qs, k_aug[0:k_rows, hd, N_META:N_META + n], start=True,
                                         stop=False)
                        nc.tensor.matmul(o[:, 512 + n - P:512 + n], ident_bf[:], mask_ts_bf[:], start=False,
                                         stop=True).then_inc(S["logit_ready"], 1)
                pe.wait_ge(S["max_ready"], (group + 1) * HEADS * 4)
                for i in range(4):
                    last = nc.tensor.matmul(aux[0:HEADS, i * P:(i + 1) * P], maxes[:, i, :], cm(C_IDENT), start=True,
                                            stop=True)
                last.then_inc(S["mxrow_ready"], 1)
                pe.wait_ge(S["mxneg_ready"], group + 1)
                pe.wait_ge(S["mx_dma"], 16 * HEADS * (group + 1))

                def logits(hd, u):
                    j, t0, n, off, diag = au[u]
                    k = (group * HEADS + hd) * NB + u
                    if hd > 0 or u >= 4:
                        pe.wait_ge(S["p_ready"], k - 3)
                    o = aux[0:BLOCKS[j][1], (k % 4) * 512:(k % 4) * 512 + n]
                    last = nc.tensor.matmul(o, k_aug[0:row_count, hd, BLOCKS[j][0]:BLOCKS[j][0] + BLOCKS[j][1]],
                                            q_aug[0:row_count, hd, t0:t0 + n], start=True, stop=not diag)
                    if diag:
                        last = nc.tensor.matmul(o[:, 0:P], ident_bf[:], mask_st_bf[:], start=False, stop=True)
                    last.then_inc(S["l_ready"], 1)

                def weigh(hd, u):
                    j, t0, n, off, diag = au[u]
                    gh = group * HEADS + hd
                    if u == 0 and hd >= 2:
                        pe.wait_ge(S["ot_ready"], gh - 1)
                    pe.wait_ge(S["p_ready"], gh * NB + u + 1)
                    rows_ = BLOCKS[j][1]
                    last = nc.tensor.matmul(prod[:, gh % 2, t0 - N_META:t0 - N_META + n],
                                            vp[0:rows_, j, hd // 2, (hd % 2) * HD:(hd % 2) * HD + P],
                                            pt[0:rows_, hd % 2, off:off + n], start=u == 0, stop=u == NB - 1)
                    if u == NB - 1:
                        last.then_inc(S["o_ready"], 1)

                for hd in range(HEADS):
                    for u in range(NB):
                        logits(hd, u)
                        if hd:
                            weigh(hd - 1, u)
                for u in range(NB):
                    weigh(HEADS - 1, u)
                pe.wait_ge(S["ot_ready"], (group + 1) * HEADS)

            attend(0, HD + 1, HD + 2, ((S["augF"], 16 * HEADS), (item_dma[0], 128), (item_dma[1], 128), (S["v_copied"], 12),
                                       (S["psum_free"], Y_FV + 4)))
            for c in range(6):
                t = S_UQ + c // 2
                last = product(t, Y_UQ + c, B, FULL, k0=3 * (c % 2), nk=3, waits=R_LORA if c == 0 else None)
                last.then_inc(S["w_used"] if c % 2 else S["part_ready"], 1)
                item_stat(8 + c, C_BLK64 if c < 4 else C_BLK32)
                if c >= 4:
                    rotate(8 + c, c - 3, P, stg[:, c % 2])
            for c in range(4):
                last = product(S_UK, Y_UK + c, B, FULL, k0=2 * c, nk=2, kb=3)
                last.then_inc(S["part_ready"] if c < 3 else S["w_used"], 1)
                item_stat(14 + c, C_BLK64)
            item_stat(18, C_BLK32, C_ROPE)
            rotate(18, 3, C_ROPE, kr[:])
            pe.wait_ge(S["item_done"], 19)
            for c in range(4):
                last = product(S_UV, Y_UV + c, B, FULL, k0=2 * c, nk=2, kb=3)
                last.then_inc(S["part_ready"] if c < 3 else S["w_used"], 1)
                if c:
                    transpose_v(c - 1, Y_UV + c - 1, 12)
            transpose_v(3, Y_UV + 3, 12)
            attend(1, C_NOPE + C_ROPE, C_NOPE + C_ROPE + 1,
                   ((S["aug_one"], 2), (item_dma[0], DMA_TOTAL[0]), (item_dma[1], DMA_TOTAL[1]), (S["v_copied"], 16),
                    (S["psum_free"], Y_UV + 4)))

            pe.wait_ge(S["operand_ready"], R_ATT_C + 4)
            for m in range(KT):
                product(S_OUT1 + m, Y_OUT1 + m, A, REAL).then_inc(S["w_used"], 1)
            stats(3, N_META)
            pe.wait_ge(S["operand_ready"], R_X3 + KT)
            with pe.Fori(0, QUARTERS - 1) as q:
                mlp(S_MLP1, Y_MLP1, R_MLP1, B, A, REAL, q, None, None)
            mlp(S_MLP1, Y_MLP1, R_MLP1, B, A, REAL, QUARTERS - 1, None, None)


def _dma_totals():
    total = [128, 128]
    for k in range(8, 19):
        c = k - 8
        total[k % 2] += 32 if c < 4 or 6 <= c < 10 else 64 if c < 6 else 16 * HEADS
    return total


DMA_TOTAL = _dma_totals()


def _blocks(w, columns):
    return w[:, columns].reshape(-1, P, len(columns)).transpose(1, 0, 2)


def _stream(ev_w_in, ev_w_out, od_w_in, od_w_uq, od_w_ukv, od_w_out, w_ff1, w_ff2):
    s = np.zeros((S_END, P, 8, P), np.float32)
    q0, k0, v0, o0, i0, f0, x0, b0 = np.cumsum([0, 512, 512, 1024, 1024, A_HEADS, A_HEADS, D_MODEL])
    for g in range(KT):
        s[S_RG + 2 * g] = _blocks(ev_w_in, range(x0 + g * P, x0 + (g + 1) * P))
        s[S_RG + 2 * g + 1] = _blocks(ev_w_in, range(b0 + g * P, b0 + (g + 1) * P))
    s[S_GATES][:, :, 0:A_HEADS] = _blocks(ev_w_in, range(i0, i0 + A_HEADS))
    s[S_GATES][:, :, 32:32 + A_HEADS] = _blocks(ev_w_in, range(f0, f0 + A_HEADS))
    for first, at, n in ((S_QK, q0, 8), (S_V, v0, 8), (S_O, o0, 8)):
        for j in range(n):
            s[first + j] = _blocks(ev_w_in, range(at + j * P, at + (j + 1) * P))
    for m in range(KT):
        c = range(m * P, (m + 1) * P)
        s[S_OUT0 + 2 * m] = _blocks(ev_w_out[D_MODEL:], c)
        s[S_OUT0 + 2 * m + 1] = _blocks(ev_w_out[:D_MODEL], c)
        s[S_OUT1 + m] = _blocks(od_w_out, c)
    for first, layer in ((S_MLP0, 0), (S_MLP1, 1)):
        for q in range(QUARTERS):
            for j in range(8):
                c = q * D_MODEL + j * P
                s[first + 16 * q + j] = _blocks(w_ff1[layer], range(c, c + P))
                s[first + 16 * q + 8 + j] = _blocks(w_ff2[layer][q * D_MODEL:(q + 1) * D_MODEL],
                                                    range(j * P, (j + 1) * P))
    kr0 = Q_LORA + KV_LORA
    fq0 = kr0 + C_ROPE
    for j in range(5):
        s[S_LORA + j] = _blocks(od_w_in, range(j * P, (j + 1) * P))
    s[S_KRFF][:, :, 0:C_ROPE] = _blocks(od_w_in, range(kr0, kr0 + C_ROPE))
    s[S_KRFF][:, :, 32:32 + HEADS] = _blocks(od_w_in, range(fq0 + 3 * 512, fq0 + 3 * 512 + HEADS))
    for j in range(12):
        s[(S_FQK if j < 8 else S_FV - 8) + j] = _blocks(od_w_in, range(fq0 + j * P, fq0 + (j + 1) * P))
    for m in range(6):
        if m < 4:
            c = [hd * 96 + f for hd in (2 * m, 2 * m + 1) for f in range(C_NOPE)]
        else:
            c = [hd * 96 + C_NOPE + f for hd in range(4 * (m - 4), 4 * (m - 4) + 4) for f in range(C_ROPE)]
        s[S_UQ + m // 2][:, 3 * (m % 2):3 * (m % 2) + 3] = _blocks(od_w_uq, c)
    for m in range(4):
        for first, off in ((S_UK, 0), (S_UV, C_NOPE)):
            c = [hd * 128 + off + f for hd in (2 * m, 2 * m + 1) for f in range(64)]
            s[first][:, 2 * m:2 * m + 2] = _blocks(od_w_ukv, c)
    return s.reshape(S_END, P, TILE)


def _columns(x):
    c = np.zeros((P, N_COLS), np.float32)

    def put(name, values):
        at = COLS[name][0]
        values = np.asarray(values, np.float32).reshape(-1, P).T
        c[:, at:at + values.shape[1]] = values

    put("ev_ln", x["ev_ln"]), put("od_ln", x["od_ln"])
    put("mlp_ln0", x["mlp_ln"][0]), put("mlp_ln1", x["mlp_ln"][1])
    for ours, theirs in (("conv_w", "ev_conv_w"), ("conv_b", "ev_conv_b"), ("b_ra", "ev_b_ra"), ("b_rx", "ev_b_rx"),
                         ("lam", "ev_lam"), ("a_norm", "ev_a_norm"), ("g_qa", "od_g_qa"), ("g_kva", "od_g_kva")):
        put(ours, x[theirs])
    for name in ("g_qn", "g_qr", "g_kn", "g_kr", "g_fq", "g_fk"):
        g = x["od_" + name].reshape(-1)
        put(name, np.tile(g, P // g.size))
    c[0:A_HEADS, COLS["b_i"][0]] = x["ev_b_if"][0, :A_HEADS]
    c[0:A_HEADS, COLS["b_f"][0]] = x["ev_b_if"][0, A_HEADS:]
    c[0:HEADS, COLS["od_b_f"][0]] = x["od_b_f"][0]
    half = C_ROPE // 2
    freqs = np.float32(10000.0) ** (-np.arange(half, dtype=np.float32) / np.float32(half))
    c[:, COLS["freq"][0]] = np.tile(freqs.astype(np.float32), P // half)
    return c


def _constants():
    c = np.zeros((N_CONST, P, P), np.float32)
    i = np.arange(P)
    c[C_IDENT] = np.eye(P)
    c[C_ONES] = 1.0
    c[C_BLK64] = (i[:, None] // 64 == i[None, :] // 64) / 64.0
    c[C_BLK32] = (i[:, None] // 32 == i[None, :] // 32) / 32.0
    for m in range(P):
        c[C_ROT, m + 16 if m % 32 < 16 else m - 16, m] = -1.0 if m % 32 < 16 else 1.0
    c[C_MASK_ST] = np.where(i[:, None] > i[None, :], MASKED, 0.0)
    c[C_MASK_TS] = c[C_MASK_ST].T
    for hd in range(A_HEADS):
        c[C_SEL + hd, hd] = 1.0
    return c.transpose(1, 0, 2).reshape(P, N_CONST * P)


def kernel(**inputs):
    import concourse.bacc as bacc
    from concourse.bass_utils import run_bass_kernel_spmd

    x = {k: np.asarray(a) for k, a in inputs.items()}
    arrays = {
        "in_h": np.ascontiguousarray(np.concatenate([x["meta"], x["x"][0]], axis=0).T),
        "in_positions": np.ascontiguousarray(x["positions"]),
        "in_stream": _stream(x["ev_w_in"][0], x["ev_w_out"][0], x["od_w_in"][0], x["od_w_uq"][0], x["od_w_ukv"][0],
                             x["od_w_out"][0], x["w_ff1"], x["w_ff2"]),
        "in_gate_w": np.ascontiguousarray(np.concatenate([x["ev_w_ra"][0], x["ev_w_rx"][0]], axis=0)),
        "in_cols": _columns(x),
        "in_const": _constants(),
    }
    nc = bacc.Bacc("TRN2", target_bir_lowering=False, num_devices=1)
    args = [nc.dram_tensor(n, a.shape, mybir.dt.from_np(a.dtype), kind="ExternalInput").ap()
            for n, a in arrays.items()]
    args.append(nc.dram_tensor("out_t", (D_MODEL, SEQ), mybir.dt.float32, kind="ExternalOutput").ap())
    trunk(nc, *args)
    r = run_bass_kernel_spmd(nc, [arrays], core_ids=[0])
    got = np.asarray(r.results[0]["out_t"])
    return np.ascontiguousarray(got.T).reshape(1, SEQ, D_MODEL)
```

```python
import numpy as np

import concourse.bass as bass
from concourse import mybir
from contextlib import ExitStack


P = 128
D_MODEL, SEQ, N_META = 1024, 512, 16
T = N_META + SEQ
HALF = T // 2
KT = D_MODEL // P
D_FF = 4 * D_MODEL
QUARTERS = D_FF // D_MODEL
A_HEADS, A_DQK, A_DV = 4, 128, 256
HEADS, C_NOPE, C_ROPE, HD = 8, 64, 32, 64
Q_LORA, KV_LORA = 384, 256
EPS = 1e-6
BLOCKS = [(0, N_META)] + [(N_META + P * i, P) for i in range(SEQ // P)]
NB = len(BLOCKS)
MASKED = -1e30

TILE = 8 * P
S_RG = 0
S_GATES = S_RG + 2 * KT
S_QK = S_GATES + 1
S_V = S_QK + 8
S_O = S_V + 8
S_OUT0 = S_O + 8
S_MLP0 = S_OUT0 + 16
S_LORA = S_MLP0 + 64
S_KRFF = S_LORA + 5
S_FQK = S_KRFF + 1
S_FV = S_FQK + 8
S_UQ = S_FV + 4
S_UK = S_UQ + 3
S_UV = S_UK + 1
S_OUT1 = S_UV + 1
S_MLP1 = S_OUT1 + 8
S_END = S_MLP1 + 64

Y_RG = 0
Y_GATES = Y_RG + 16
Y_QK = Y_GATES + 1
Y_V = Y_QK + 8
Y_O = Y_V + 8
Y_OUT0 = Y_O + 8
Y_MLP0 = Y_OUT0 + 8
Y_LORA = Y_MLP0 + 64
Y_KRFF = Y_LORA + 5
Y_FQK = Y_KRFF + 1
Y_FV = Y_FQK + 8
Y_UQ = Y_FV + 4
Y_UK = Y_UQ + 6
Y_UV = Y_UK + 4
Y_OUT1 = Y_UV + 4
Y_MLP1 = Y_OUT1 + 8

R_X0 = 0
R_HB = R_X0 + KT
R_HA = R_HB + KT
R_X1 = R_HA + KT
R_MLP0 = R_X1 + KT
R_X2 = R_MLP0 + KT * QUARTERS
R_LORA = R_X2 + KT
R_ATT_D = R_LORA + 5
R_ATT_C = R_ATT_D + 4
R_X3 = R_ATT_C + 4
R_MLP1 = R_X3 + KT

COLS = {}


def _col(name, n):
    COLS[name] = sum(w for _, w in COLS.values()), n


for _name, _n in (("ev_ln", 8), ("od_ln", 8), ("mlp_ln0", 8), ("mlp_ln1", 8), ("conv_w", 32), ("conv_b", 8),
                  ("b_ra", 8), ("b_rx", 8), ("lam", 8), ("a_norm", 2), ("g_qa", 3), ("g_kva", 2), ("g_qn", 1),
                  ("g_qr", 1), ("g_kn", 1), ("g_kr", 1), ("g_fq", 1), ("g_fk", 1), ("b_i", 1), ("b_f", 1),
                  ("od_b_f", 1), ("freq", 1), ("eps", 3)):
    _col(_name, _n)
N_COLS = sum(w for _, w in COLS.values())
C_IDENT, C_ONES, C_BLK64, C_BLK32, C_ROT, C_MASK_ST, C_MASK_TS, C_SEL = range(8)
STEPS = [("norm", Y_FQK + k, P, C_BLK64, "g_fq" if k < 4 else "g_fk", HD if k < 4 else 1) for k in range(8)]
STEPS += [("value", Y_FV + j, P, None, None, None) for j in range(4)]
STEPS += [("rope", Y_UQ + c, P, C_BLK32, "g_qr", C_NOPE + C_ROPE) for c in range(2)]
STEPS += [("rope", None, C_ROPE, C_BLK32, "g_kr", 1)]
STEPS += [("norm", Y_UQ + 2 + c, P, C_BLK64, "g_qn", C_NOPE + C_ROPE) for c in range(4)]
STEPS += [("norm", Y_UK + c, P, C_BLK64, "g_kn", 1) for c in range(4)]
N_STEPS = len(STEPS)
D_STEPS, KR_STEP = 12, 14


def item_of(s):
    return sum(kind != "value" for kind, *_ in STEPS[:s])


def rope_of(s):
    return sum(kind == "rope" for kind, *_ in STEPS[:s])


def item_moves(s):
    kind, y, rows, _, gain, _ = STEPS[s]
    if s == KR_STEP:
        return "k", [(hd, C_NOPE, 0, C_ROPE) for hd in range(HEADS)]
    if kind == "rope":
        return "q", [(4 * (y - Y_UQ) + e, C_NOPE, e * C_ROPE, C_ROPE) for e in range(4)]
    first = s % 4 if s < D_STEPS else y - (Y_UQ + 2 if gain == "g_qn" else Y_UK)
    return ("q" if gain in ("g_fq", "g_qn") else "k"), [(2 * first + e, 0, e * HD, HD) for e in range(2)]


def slot_moves(s, slot):
    return sum(16 * len(item_moves(i)[1]) for i in range(s) if i % 4 == slot and STEPS[i][0] != "value")


def product_end(y):
    c = y - Y_UQ
    if c < 6:
        return ("part_ready", c // 2 + 1) if c % 2 == 0 else ("w_used", S_UQ + c // 2 + 1)
    tile, i = divmod(c - 6, 4)
    return ("part_ready", 3 + 3 * tile + i + 1) if i < 3 else ("w_used", S_UK + tile + 1)


def out_tile(group, pair):
    return 1 + pair if group else (5, 6, 7, 0)[pair]

N_CONST = C_SEL + A_HEADS


def trunk(nc, h_in, positions, stream, gate_w, cols_in, const_in, out):
    F32, F32R, BF16, I32 = mybir.dt.float32, mybir.dt.float32r, mybir.dt.bfloat16, mybir.dt.int32
    ALU, ACT, AX = mybir.AluOpType, mybir.ActivationFunctionType, mybir.AxisListType
    ctx = ExitStack()
    with ctx:
        def sb(name, shape, dt=F32, scope=ctx):
            return scope.enter_context(nc.sbuf_tensor(name, shape, dt))

        def sem(name):
            return ctx.enter_context(nc.semaphore(name))

        h = sb("h", [P, KT, T])
        a_hi, a_lo = sb("a_hi", [P, KT, T], F32R), sb("a_lo", [P, KT, T], F32R)
        b_hi, b_lo = sb("b_hi", [P, KT, T], F32R), sb("b_lo", [P, KT, T], F32R)
        raw = sb("raw", [P, 4, TILE])
        w_hi, w_lo = sb("w_hi", [P, 2, TILE], F32R), sb("w_lo", [P, 2, TILE], F32R)
        cols = sb("cols", [P, N_COLS])
        const = sb("const", [P, N_CONST * P])
        ident_bf, mask_st_bf, mask_ts_bf = (sb(n, [P, P], BF16) for n in ("ident_bf", "mask_st_bf", "mask_ts_bf"))
        inv_ms = sb("inv_ms", [P, T])
        rstd = inv_ms
        sq = sb("sq", [P, 2, T])
        sq_sum = sb("sq_sum", [P, T])
        tmp = sb("tmp", [P, 2, T])

        even = ExitStack()
        c_hi, c_lo = sb("c_hi", [P, KT, T], F32R, even), sb("c_lo", [P, KT, T], F32R, even)
        qk = sb("qk", [P, 2 * A_HEADS, T], F32, even)
        v = sb("v", [P, NB, A_HEADS * A_DV], F32, even)
        even.close()
        rg = ExitStack()
        xb = sb("xb", [P, T + 3], F32, rg)
        xc, gate_r, gate_i, den_t, sqrt_t, decay, gb, gel, hs = (
            sb(n, [P, T], F32, rg) for n in ("xc", "gate_r", "gate_i", "den_t", "sqrt_t", "decay", "gb", "gel", "hs"))
        wr = sb("wr", [P, 2 * KT * P], F32, rg)
        sp4 = sb("sp4", [P, KT], F32, rg)
        spt = sb("spt", [P, 5, KT], F32, rg)
        rg.close()
        ml = ExitStack()
        N_ST = 2 * T - N_META + sum(T - t0 for t0, _ in BLOCKS[2:])
        expw = sb("expw", [P, N_ST], F32, ml)
        st = sb("st", [P, N_ST], F32, ml)
        abc, em, rs_a = (sb(n, [P, T], F32, ml) for n in ("abc", "em", "rs_a"))
        ccol = sb("ccol", [P, NB * A_HEADS], F32, ml)
        ml.close()

        odd = ExitStack()
        q_aug = sb("q_aug", [P, HEADS, T], F32R, odd)
        k_aug = sb("k_aug", [P, HEADS, T], F32R, odd)
        vp = sb("vp", [P, NB, 4, 192], F32, odd)
        N_PT = 2 * SEQ + sum(T - t0 for t0, _ in BLOCKS[2:])
        pt = sb("pt", [P, 2, N_PT], F32, odd)
        kr = sb("kr", [C_ROPE, T], F32, odd)
        stg = sb("stg", [P, 4, T], F32, odd)
        maxes = sb("maxes", [P, 2, 4, HEADS], F32, odd)
        odd.close()
        od2 = ExitStack()
        sb("pad_aug", [P, 2 * HEADS * T], F32, od2)
        lora_sq = sb("lora_sq", [P, 5, T], F32, od2)
        sb("pad_vp", [P, NB * 4 * 192 - 5 * T], F32, od2)
        lora = sb("lora", [P, 5, T], F32, od2)
        od2.close()
        g_f, g_l, g_i, g_F, g_m = tmp[0:HEADS, 0], tmp[0:HEADS, 1], sq[0:HEADS, 0], sq[0:HEADS, 1], sq_sum[0:HEADS]
        g_zero = stg[0:HEADS, 3]
        g_Fhi = tmp[0:HEADS, 0].bitcast(F32R)
        g_pos = sq_sum[:].bitcast(I32)
        rope_t = sq_sum
        angle, turns = lora[:, 0], lora[:, 1]
        q_of, k_of = (q_aug, a_hi), (k_aug, a_lo)
        neg_max = (sq_sum[0:HEADS, 0:SEQ], stg[0:HEADS, 1, 0:SEQ])

        prod = ctx.enter_context(nc.psum_tensor("prod", [P, 2, 1024], F32))
        aux = ctx.enter_context(nc.psum_tensor("aux", [P, 2048], F32))

        names = ["h_loaded", "cols_loaded", "const_loaded", "wr_loaded", "raw_full0", "raw_full1", "raw_full2",
                 "raw_full3", "w_hi_ready", "w_lo_ready", "w_used", "part_ready", "psum_free", "operand_ready",
                 "a_hi_ready", "sq_ready", "sq_summed", "stat_ready", "ms_ready", "rstd_ready", "h_ready",
                 "dve_chain", "act_chain", "pool_chain", "bf_ready", "sp4_ready", "lam_e_ready",
                 "conv0_ready", "xc_ready", "gates_ready", "sig_ready", "tanh_ready", "sqrt_ready", "den_ready",
                 "ix_ready", "sd_ready", "decay_ready", "u_ready", "hs_ready", "hb_ready", "gsq_ready",
                 "gz_ready", "gsig_ready", "gelu_ready", "split_hi", "zero_ready",
                 "gf_ready", "gl_ready", "rows_ready", "ccol_psum", "ccol_ready", "bc_ready", "abc_ready",
                 "em_ready", "diag_ready", "expw_ready", "s_ready", "st_ready", "acc_ready", "absden_ready",
                 "hn_ready", "hnsq_ready", "hstat_ready", "hms_ready", "hrs_ready", "head_done",
                 "osig_ready", "osig_raw", "ha_ready", "vt_ready", "v_copied", "relu_ready", "hid_ready",
                 "trig_pos", "trig_ready", "trig_arg", "lsq_ready", "lstat_ready", "lms_ready", "lrs_ready",
                 "ln_ready", "fF_ready", "fgf_ready", "fgl_ready", "augF", "aug_one",
                 "item_sq", "item_stat", "item_ms", "item_rs", "item_done", "item_rot", "item_dma0", "item_dma1",
                 "item_dma2", "item_dma3", "rope_ready", "fhi_ready", "flo_ready",
                 "logit_ready", "max_ready", "mxrow_ready", "mxneg_ready", "mx_dma0", "mx_dma1", "l_ready", "p_ready",
                 "o_ready", "ot_ready", "ot_free", "stored", "pos_loaded"]
        S = {n: sem(n) for n in names}
        raw_full = [S[f"raw_full{i}"] for i in range(4)]
        mx_dma = [S["mx_dma0"], S["mx_dma1"]]
        item_dma = [S[f"item_dma{i}"] for i in range(4)]

        def cm(i, rows_=P, width=P):
            return const[0:rows_, i * P:i * P + width]

        def col(name, j=0, rows_=P, p0=0):
            c = COLS[name][0] + j
            return cols[p0:p0 + rows_, c:c + 1]

        def two(ap):
            return ap.rearrange("p (b n) -> p b n", b=2)

        def slot(y, rows_=P, p0=0):
            return prod[p0:p0 + rows_, y % 2].rearrange("p (b n) -> p b n", b=2)[:, :, 0:HALF]

        def slot_real(y):
            return prod[:, y % 2, 0:SEQ]

        def aux_two(b, rows_=P):
            return aux[0:rows_, b * 512:(b + 2) * 512].rearrange("p (b n) -> p b n", b=2)[:, :, 0:HALF]

        def v_bank(j, base):
            return 1024 if base == 8 else (j % 2) * 1024

        def pair_of_banks(k):
            return prod[:, k % 4] if k % 4 < 2 else aux[:, (k % 4 - 2) * 1024:(k % 4 - 1) * 1024]

        def units(with_meta_queries):
            found, off = [], 0
            if with_meta_queries:
                found.append((0, 0, N_META, 0, N_META))
                off = N_META
            for j, (t0, _) in enumerate(BLOCKS):
                first = max(t0, N_META)
                found.append((j, first, T - first, off, P if j else 0))
                off += T - first
            return found

        N_EXP = sum((n > diag) + (diag > 0) for _, _, n, _, diag in units(True))

        block = ctx.enter_context(nc.Block())

        @block.sync
        def _(sp):
            sp.dma_start(cols[:], cols_in).then_inc(S["cols_loaded"], 16)
            sp.dma_start(h[:], h_in.rearrange("(m p) t -> p m t", p=P)).then_inc(S["h_loaded"], 16)
            for n in range(4):
                sp.dma_start(raw[:, n], stream[n]).then_inc(raw_full[n], 16)
            sp.dma_start(const[:], const_in).then_inc(S["const_loaded"], 16)
            sp.dma_start(wr[:].rearrange("p (g n) -> p g n", n=P), gate_w.rearrange("g p n -> p g n")).then_inc(
                S["wr_loaded"], 16)

            def load(first, iterations):
                with sp.Fori(0, iterations) as i:
                    row = sp.snap(i * 4 + first)
                    for j in range(4):
                        sp.wait_ge(S["w_lo_ready"], i * 4 + (first + j - 3))
                        sp.dma_start(raw[:, j], stream[bass.ds(row + j, 1)].rearrange("a p n -> p (a n)")).then_inc(
                            raw_full[j], 16)

            load(4, (S_END - 4) // 4)

        @block.gpsimd
        def _(pool):
            chain = [0]

            def link(ins):
                chain[0] += 1
                ins.then_inc(S["pool_chain"], 1)
                pool.wait_ge(S["pool_chain"], chain[0])

            def sum_squares(base, t0):
                for m in range(KT):
                    pool.wait_ge(S["sq_ready"], base + m + 1)
                    if m == 0:
                        nc.gpsimd.tensor_copy(sq_sum[:, t0:], sq[:, 0, t0:]).then_inc(S["sq_summed"], 1)
                    else:
                        pool.wait_ge(S["sq_summed"], base + m)
                        nc.gpsimd.tensor_tensor(sq_sum[:, t0:], sq_sum[:, t0:], sq[:, m % 2, t0:], ALU.add).then_inc(
                            S["sq_summed"], 1)

            nc.gpsimd.memset(xb[:, 0:3], 0.0).then_inc(S["zero_ready"], 1)
            sum_squares(0, 0)
            for g in range(KT):
                pool.wait_ge(S["gsq_ready"], g + 1)
                link(nc.gpsimd.tensor_scalar(gel[:], gel[:], 0.044715, 1.0, ALU.mult, ALU.add))
                nc.gpsimd.tensor_tensor(gel[:], gel[:], gb[:], ALU.mult).then_inc(S["gz_ready"], 1)
                pool.wait_ge(S["sig_ready"], g + 1)
                nc.gpsimd.tensor_tensor(gate_i[:], gate_i[:], xc[:], ALU.mult).then_inc(S["ix_ready"], 1)
                pool.wait_ge(S["gsig_ready"], g + 1)
                nc.gpsimd.tensor_tensor(gel[:], gel[:], gb[:], ALU.mult).then_inc(S["gelu_ready"], 1)
                pool.wait_ge(S["sqrt_ready"], g + 1)
                pool.wait_ge(S["den_ready"], g + 1)
                nc.gpsimd.tensor_tensor(sqrt_t[:], sqrt_t[:], den_t[:], ALU.mult).then_inc(S["sd_ready"], 1)
                if g:
                    pool.wait_ge(S["hs_ready"], g)
                nc.gpsimd.tensor_scalar(decay[:], den_t[:], 2.0, -1.0, ALU.mult, ALU.add).then_inc(
                    S["decay_ready"], 1)
            sum_squares(KT, 0)

            def mlp(y0, r0, t0, q, sq_base):
                for j in range(8):
                    pool.wait_ge(S["psum_free"], y0 + j + 1 + q * 16)
                    nc.gpsimd.tensor_tensor(tmp[:, j % 2, t0:], tmp[:, j % 2, t0:], tmp[:, j % 2, t0:],
                                            ALU.mult).then_inc(S["hid_ready"], 1)

            with pool.Fori(0, QUARTERS - 1) as q:
                mlp(Y_MLP0, 0, 0, q, None)
            mlp(Y_MLP0, 0, 0, QUARTERS - 1, None)
            sum_squares(2 * KT, 0)
            pool.wait_ge(S["stat_ready"], 3)
            nc.gpsimd.iota(g_pos[:, 0:N_META], pattern=[[1, N_META]], base=0, channel_multiplier=0).then_inc(
                S["trig_pos"], 1)
            for s in range(N_STEPS):
                if STEPS[s][0] == "value":
                    continue
                if s == D_STEPS:
                    pool.wait_ge(S["w_used"], S_FV + 4)
                group = 0 if s < D_STEPS else 1
                pool.wait_ge(S["item_done"], item_of(s) + 1)
                src = kr if s == KR_STEP else stg[:, s % 4]
                which, moves = item_moves(s)
                for hd, row, at, n in moves:
                    pool.dma_start((q_of if which == "q" else k_of)[group][row:row + n, hd].bitcast(F32), src[at:at + n]).then_inc(
                        item_dma[s % 4], 16)
            sum_squares(3 * KT, N_META)
            with pool.Fori(0, QUARTERS - 1) as q:
                mlp(Y_MLP1, 0, N_META, q, None)
            mlp(Y_MLP1, 0, N_META, QUARTERS - 1, None)

        @block.scalar
        def _(act):
            chain = [0]

            def link(ins):
                chain[0] += 1
                ins.then_inc(S["act_chain"], 1)
                act.wait_ge(S["act_chain"], chain[0])

            def split_weights(nb, i4=0):
                act.wait_ge(raw_full[nb % 4], 16 * (nb // 4 + 1) + i4 * 16)
                if nb >= 2:
                    act.wait_ge(S["w_used"], nb - 1 + i4 * 4)
                nc.scalar.activation(w_hi[:, nb % 2], raw[:, nb % 4], ACT.Copy).then_inc(S["w_hi_ready"], 1)

            def next_operand(m, base, gain, hi, t0):
                if base == 2 * KT:
                    act.wait_ge(S["h_ready"], m + 1)
                elif base:
                    act.wait_ge(S["psum_free"], {KT: Y_OUT0, 3 * KT: Y_OUT1}[base] + m + 1)
                nc.scalar.activation(hi[:, m, t0:], h[:, m, t0:], ACT.Copy, scale=col(gain, m)).then_inc(
                    S["a_hi_ready"], 1)
                if m >= 2:
                    act.wait_ge(S["sq_summed"], base + m - 1)
                nc.scalar.activation(sq[:, m % 2, t0:], h[:, m, t0:], ACT.Square).then_inc(S["sq_ready"], 1)

            def mean_square(k, power, t0=0):
                act.wait_ge(S["stat_ready"], k + 1)
                if t0:
                    o, i = inv_ms[:, t0:], aux[:, 0:SEQ]
                else:
                    o, i = two(inv_ms[:]), aux_two(0)
                link(nc.scalar.activation(o, i, ACT.Ln, bias=col("eps"), scale=1.0 / D_MODEL))
                nc.scalar.activation(inv_ms[:, t0:], inv_ms[:, t0:], ACT.Exp, scale=power).then_inc(S["ms_ready"], 1)

            act.wait_ge(S["cols_loaded"], 16)
            lam = cols[:, COLS["lam"][0]:COLS["lam"][0] + KT]
            link(nc.scalar.activation(spt[:, 0], lam, ACT.Abs))
            nc.scalar.activation(spt[:, 0], spt[:, 0], ACT.Exp, scale=-1.0).then_inc(S["lam_e_ready"], 1)
            act.wait_ge(S["h_loaded"], 16)
            for m in range(KT):
                next_operand(m, 0, "ev_ln", a_hi, 0)
                if m < 2:
                    split_weights(m)
            act.wait_ge(S["const_loaded"], 16)
            nc.scalar.activation(ident_bf[:], cm(C_IDENT), ACT.Copy).then_inc(S["bf_ready"], 1)
            nc.scalar.activation(mask_st_bf[:], cm(C_MASK_ST), ACT.Copy).then_inc(S["bf_ready"], 1)
            nc.scalar.activation(mask_ts_bf[:], cm(C_MASK_TS), ACT.Copy).then_inc(S["bf_ready"], 1)
            mean_square(0, -0.5)

            for g in range(KT):
                split_weights(2 * g + 2)
                act.wait_ge(S["psum_free"], 2 * g + 1)
                if g == 0:
                    act.wait_ge(S["zero_ready"], 1)
                else:
                    act.wait_ge(S["ix_ready"], g)
                nc.scalar.activation(xc[:], xb[:, 0:T], ACT.Identity, bias=col("conv_b", g),
                                     scale=col("conv_w", g)).then_inc(S["conv0_ready"], 1)
                split_weights(2 * g + 3)
                act.wait_ge(S["psum_free"], 2 * g + 2)
                nc.scalar.activation(gel[:], gb[:], ACT.Square).then_inc(S["gsq_ready"], 1)
                if g:
                    act.wait_ge(S["hb_ready"], g)
                    nc.scalar.activation(b_hi[:, g - 1], hs[:], ACT.Copy).then_inc(S["split_hi"], 1)
                act.wait_ge(S["gates_ready"], g + 1)
                if g:
                    act.wait_ge(S["u_ready"], g)
                if g == 0:
                    act.wait_ge(S["sp4_ready"], 1)
                nc.scalar.activation(two(gate_r[:]), aux_two(0), ACT.Sigmoid, bias=col("b_ra", g)).then_inc(
                    S["act_chain"], 1)
                chain[0] += 1
                nc.scalar.activation(two(gate_i[:]), aux_two(2), ACT.Sigmoid, bias=col("b_rx", g)).then_inc(
                    S["sig_ready"], 1)
                act.wait_ge(S["act_chain"], chain[0])
                nc.scalar.activation(gate_r[:], gate_r[:], ACT.Tanh, scale=sp4[:, g:g + 1]).then_inc(
                    S["tanh_ready"], 1)
                act.wait_ge(S["gz_ready"], g + 1)
                nc.scalar.activation(gel[:], gel[:], ACT.Sigmoid, scale=float(2.0 * np.sqrt(2.0 / np.pi))).then_inc(
                    S["gsig_ready"], 1)
                act.wait_ge(S["tanh_ready"], g + 1)
                nc.scalar.activation(sqrt_t[:], gate_r[:], ACT.Sqrt, scale=4.0).then_inc(S["sqrt_ready"], 1)
            act.wait_ge(S["hb_ready"], KT)
            nc.scalar.activation(b_hi[:, KT - 1], hs[:], ACT.Copy).then_inc(S["split_hi"], 1)

            split_weights(S_GATES + 2)
            act.wait_ge(S["gf_ready"], 1)
            link(nc.scalar.activation(g_l[0:A_HEADS], g_f[0:A_HEADS], ACT.Abs, bias=col("b_f", 0, A_HEADS)))
            link(nc.scalar.activation(g_l[0:A_HEADS], g_l[0:A_HEADS], ACT.Exp, scale=-1.0))
            nc.scalar.activation(g_l[0:A_HEADS], g_l[0:A_HEADS], ACT.Ln, bias=1.0).then_inc(S["gl_ready"], 1)
            for j in range(8):
                split_weights(S_QK + 2 + j)

            def copy_v(j, dst_meta, dst_real, base, pairs=False):
                act.wait_ge(S["vt_ready"], base + j + 1)
                a = v_bank(j, base)
                nc.scalar.activation(dst_meta, aux[0:N_META, a:a + P] if not pairs else
                                     aux[0:N_META, a:a + P].rearrange("p (c n) -> p c n", c=2), ACT.Copy)
                src = aux[:, a + 512:a + 1024].rearrange("p (b n) -> p b n", b=4)
                if pairs:
                    for b in range(4):
                        last = nc.scalar.activation(dst_real[:, b], src[:, b].rearrange("p (c n) -> p c n", c=2),
                                                    ACT.Copy)
                else:
                    last = nc.scalar.activation(dst_real, src, ACT.Copy)
                last.then_inc(S["v_copied"], 1)

            for j in range(8):
                split_weights(S_V + 2 + j)
                if j:
                    copy_v(j - 1, v[0:N_META, 0, (j - 1) * P:j * P], v[:, 1:NB, (j - 1) * P:j * P], 0)
            copy_v(7, v[0:N_META, 0, 7 * P:8 * P], v[:, 1:NB, 7 * P:8 * P], 0)

            act.wait_ge(S["ccol_psum"], 1)
            nc.scalar.activation(ccol[:], aux[:, 0:NB * A_HEADS], ACT.Copy).then_inc(S["ccol_ready"], 1)
            mu = units(True)
            for hd in range(A_HEADS):
                act.wait_ge(S["bc_ready"], 2 * hd + 1)
                if hd:
                    act.wait_ge(S["head_done"], hd)
                nc.scalar.activation(two(abc[:]), aux_two(2), ACT.Copy).then_inc(S["abc_ready"], 1)
                act.wait_ge(S["bc_ready"], 2 * hd + 2)
                nc.scalar.activation(two(em[:]), aux_two(2), ACT.Exp).then_inc(S["em_ready"], 1)
                act.wait_ge(S["abc_ready"], hd + 1)
                act.wait_ge(S["ccol_ready"], 1)
                for u, (j, t0, n, off, diag) in enumerate(mu):
                    rows_ = BLOCKS[j][1]
                    if n > diag:
                        nc.scalar.activation(expw[0:rows_, off + diag:off + n], abc[0:rows_, t0 + diag:t0 + n],
                                             ACT.Exp, bias=ccol[0:rows_, j * A_HEADS + hd:j * A_HEADS + hd + 1]
                                             ).then_inc(S["expw_ready"], 1)
                    if diag:
                        act.wait_ge(S["diag_ready"], (hd + 1) * NB)
                        nc.scalar.activation(expw[0:rows_, off:off + diag], expw[0:rows_, off:off + diag],
                                             ACT.Exp).then_inc(S["expw_ready"], 1)
                act.wait_ge(S["acc_ready"], hd + 1)
                nc.scalar.activation(abc[:], aux[:, 496:1024], ACT.Abs).then_inc(S["absden_ready"], 1)
                for e in range(2):
                    act.wait_ge(S["hn_ready"], 2 * hd + e + 1)
                    nc.scalar.activation(expw[:, e * T:(e + 1) * T], qk[:, hd + e * A_HEADS], ACT.Square).then_inc(
                        S["hnsq_ready"], 1)
                act.wait_ge(S["hstat_ready"], hd + 1)
                nc.scalar.activation(two(rs_a[:]), aux_two(2), ACT.Ln, bias=col("eps"), scale=1.0 / A_DV).then_inc(
                    S["hms_ready"], 1)
                act.wait_ge(S["hms_ready"], hd + 1)
                nc.scalar.activation(rs_a[:], rs_a[:], ACT.Exp, scale=-0.5).then_inc(S["hrs_ready"], 1)

            for j in range(8):
                split_weights(S_O + 2 + j)
                act.wait_ge(S["psum_free"], Y_O + j + 1)
                nc.scalar.activation(tmp[:, j % 2], tmp[:, j % 2], ACT.Sigmoid).then_inc(S["osig_ready"], 1)
                act.wait_ge(S["ha_ready"], j + 1)
                nc.scalar.activation(c_hi[:, j], tmp[:, j % 2], ACT.Copy).then_inc(S["split_hi"], 1)
            for m in range(KT):
                split_weights(S_OUT0 + 2 + 2 * m)
                split_weights(S_OUT0 + 3 + 2 * m)
                next_operand(m, KT, "mlp_ln0", a_hi, 0)
            mean_square(1, -1.0)

            def mlp(s0, y0, hid, t0, q, last_quarter=None):
                for j in range(8):
                    if s0 + j + 2 < S_END:
                        split_weights(s0 + 2 + j, q * 4)
                    act.wait_ge(S["hid_ready"], hid + j + 1 + q * 8)
                    nc.scalar.activation(b_hi[:, j, t0:], tmp[:, j % 2, t0:], ACT.Copy).then_inc(S["split_hi"], 1)
                for j in range(8):
                    if not (last_quarter == 1 and s0 + 8 + j + 2 + 16 * q >= S_END):
                        split_weights(s0 + 10 + j, q * 4)
                    if last_quarter == 0:
                        next_operand(j, 2 * KT, "od_ln", a_hi, 0)

            with act.Fori(0, QUARTERS - 1) as q:
                mlp(S_MLP0, Y_MLP0, 0, 0, q)
            mlp(S_MLP0, Y_MLP0, 0, 0, QUARTERS - 1, 0)
            mean_square(2, -0.5)

            act.dma_start(g_pos[:, N_META:], positions.to_broadcast([P, SEQ])).then_inc(S["pos_loaded"], 16)
            for j in range(5):
                split_weights(S_LORA + 2 + j)
                act.wait_ge(S["psum_free"], Y_LORA + j + 1)
                nc.scalar.activation(lora_sq[:, j], lora[:, j], ACT.Square).then_inc(S["lsq_ready"], 1)
            split_weights(S_KRFF + 2)
            act.wait_ge(S["fgf_ready"], 1)
            link(nc.scalar.activation(g_l, g_f, ACT.Abs, bias=col("od_b_f", 0, HEADS)))
            link(nc.scalar.activation(g_l, g_l, ACT.Exp, scale=-1.0))
            nc.scalar.activation(g_l, g_l, ACT.Ln, bias=1.0).then_inc(S["fgl_ready"], 1)
            split_weights(S_FQK + 2)
            act.wait_ge(S["fF_ready"], 1)
            nc.scalar.activation(g_Fhi, g_F, ACT.Copy).then_inc(S["fhi_ready"], 1)
            act.wait_ge(S["flo_ready"], 1)
            for part, row in enumerate((g_Fhi.bitcast(F32), g_l)):
                act.dma_start(k_aug[HD + part:HD + part + 1].bitcast(F32), row).then_inc(
                    S["augF"], 16)
            act.wait_ge(S["augF"], 32)
            for k, width in enumerate((Q_LORA, KV_LORA)):
                act.wait_ge(S["lstat_ready"], k + 1)
                nc.scalar.activation(two(tmp[:, k]), aux_two(2 * k), ACT.Ln, bias=col("eps"),
                                     scale=1.0 / width).then_inc(S["lms_ready"], 1)
                act.wait_ge(S["lms_ready"], k + 1)
                nc.scalar.activation(tmp[:, k], tmp[:, k], ACT.Exp, scale=-0.5).then_inc(S["lrs_ready"], 1)

            def copy_pair(j, base):
                v3 = vp[:, :, j].rearrange("p b (c n) -> p b c n", c=3)
                copy_v(j, v3[0:N_META, 0, 0:3:2], v3[:, 1:NB, 0:3:2], base, True)

            def item_squares(s):
                kind, y, rows_, _, _, _ = STEPS[s]
                k = item_of(s)
                act.wait_ge(S["psum_free"], (Y_KRFF if y is None else y) + 1)
                if k == 0:
                    act.wait_ge(S["ln_ready"], 5)
                elif k >= 2:
                    act.wait_ge(S["item_done" if STEPS[s - 2][0] != "rope" else "rope_ready"],
                                k - 1 if STEPS[s - 2][0] != "rope" else rope_of(s - 2) + 1)
                nc.scalar.activation(tmp[0:rows_, k % 2], kr[:] if y is None else stg[0:rows_, s % 4],
                                     ACT.Square).then_inc(S["item_sq"], 1)

            def item_factor(s):
                _, _, rows_, _, _, inv = STEPS[s]
                k = item_of(s)
                act.wait_ge(S["item_stat"], k + 1)
                nc.scalar.activation(two(tmp[0:rows_, k % 2]), aux_two(0, rows_), ACT.Ln,
                                     bias=col("eps", {1: 0, HD: 1, C_NOPE + C_ROPE: 2}[inv], rows_),
                                     scale=float(inv)).then_inc(S["item_ms"], 1)
                act.wait_ge(S["item_ms"], k + 1)
                nc.scalar.activation(tmp[0:rows_, k % 2], tmp[0:rows_, k % 2], ACT.Exp, scale=-0.5).then_inc(
                    S["item_rs"], 1)

            for s in range(N_STEPS + 1):
                if 0 < s < D_STEPS:
                    split_weights(S_FQK + 2 + s)
                elif D_STEPS <= s < N_STEPS and s != KR_STEP:
                    sem_, tile = product_end(STEPS[s][1])
                    if sem_ == "w_used":
                        split_weights(tile + 1)
                if 1 <= s <= 5:
                    act.wait_ge(S["ln_ready"], 5)
                    nc.scalar.activation(b_hi[:, s - 1], lora[:, s - 1], ACT.Copy).then_inc(S["split_hi"], 1)
                if s < N_STEPS and STEPS[s][0] != "value":
                    item_squares(s)
                if s and STEPS[s - 1][0] != "value":
                    item_factor(s - 1)
                elif s:
                    copy_pair(s - 1 - 8, 8)
                if s == 11:
                    for k in range(2):
                        act.wait_ge(S["trig_arg"], k + 1)
                        nc.scalar.activation(sq[:, k], sq[:, k], ACT.Sin).then_inc(S["trig_ready"], 1)

            au = units(False)

            def max_row(group, row):
                act.wait_ge(S["mxrow_ready"], group + 1)
                nc.scalar.activation(neg_max[group], aux[0:HEADS, 0:SEQ], ACT.Copy, scale=-1.0).then_inc(
                    S["mxneg_ready"], 1)
                act.wait_ge(S["mxneg_ready"], group + 1)
                act.dma_start(q_of[group][row:row + 1, :, N_META:].bitcast(F32),
                              neg_max[group]).then_inc(mx_dma[group], 16)

            def attend(group):
                for hd in range(HEADS):
                    gh = group * HEADS + hd
                    if hd >= 2:
                        act.wait_ge(S["o_ready"], gh - 1)
                    for u, (j, t0, n, off, _) in enumerate(au):
                        act.wait_ge(S["l_ready"], gh * NB + u + 1)
                        bank = (gh * NB + u) % 4
                        nc.scalar.activation(pt[0:BLOCKS[j][1], hd % 2, off:off + n],
                                             aux[0:BLOCKS[j][1], bank * 512:bank * 512 + n], ACT.Exp).then_inc(
                            S["p_ready"], 1)
                    if hd % 2 == 1 and hd > 1:
                        pair_hi(group, hd // 2 - 1)
                pair_hi(group, 3)

            def pair_hi(group, pair):
                k = group * 4 + pair
                act.wait_ge(S["ot_ready"], 2 * k + 2)
                nc.scalar.activation(b_hi[:, out_tile(group, pair), N_META:], tmp[:, pair % 2, 0:SEQ],
                                     ACT.Copy).then_inc(S["split_hi"], 1)

            max_row(0, HD + 2)
            max_row(1, C_NOPE + C_ROPE)
            attend(0)
            split_weights(S_UV + 2)
            for j in range(4):
                copy_pair(j, 12)
            attend(1)

            for m in range(KT):
                split_weights(S_OUT1 + 2 + m)
                next_operand(m, 3 * KT, "mlp_ln1", a_hi, N_META)
            mean_square(3, -1.0, N_META)
            with act.Fori(0, QUARTERS - 1) as q:
                mlp(S_MLP1, Y_MLP1, 32, N_META, q)
            mlp(S_MLP1, Y_MLP1, 32, N_META, QUARTERS - 1, 1)
            out_v = out.rearrange("(m p) t -> p m t", p=P)
            for m in range(KT):
                act.wait_ge(S["h_ready"], KT + m + 1)
                act.dma_start(out_v[:, m], h[:, m, N_META:]).then_inc(S["stored"], 16)
            act.wait_ge(S["stored"], 16 * KT)

        @block.vector
        def _(dve):
            chain = [0]

            def link(ins):
                chain[0] += 1
                ins.then_inc(S["dve_chain"], 1)
                dve.wait_ge(S["dve_chain"], chain[0])

            def split_weights(nb, i4=0):
                dve.wait_ge(S["w_hi_ready"], nb + 1 + i4 * 4)
                nc.vector.tensor_tensor(w_lo[:, nb % 2], raw[:, nb % 4], w_hi[:, nb % 2].bitcast(F32),
                                        ALU.subtract).then_inc(S["w_lo_ready"], 1)

            def next_operand(m, base, gain, hi, lo, t0):
                dve.wait_ge(S["a_hi_ready"], base + m + 1)
                nc.vector.scalar_tensor_tensor(out=lo[:, m, t0:], in0=h[:, m, t0:], scalar=col(gain, m),
                                               in1=hi[:, m, t0:].bitcast(F32), op0=ALU.mult,
                                               op1=ALU.subtract).then_inc(S["operand_ready"], 1)

            def split_low(lo, hi, full, hi_count):
                dve.wait_ge(S["split_hi"], hi_count)
                nc.vector.tensor_tensor(lo, full, hi.bitcast(F32), ALU.subtract).then_inc(S["operand_ready"], 1)

            dve.wait_ge(S["lam_e_ready"], 1)
            lam = cols[:, COLS["lam"][0]:COLS["lam"][0] + KT]
            link(nc.vector.tensor_scalar(spt[:, 1], spt[:, 0], 2.0, None, ALU.add))
            link(nc.vector.reciprocal(spt[:, 1], spt[:, 1]))
            link(nc.vector.tensor_tensor(spt[:, 1], spt[:, 0], spt[:, 1], ALU.mult))
            link(nc.vector.tensor_tensor(spt[:, 2], spt[:, 1], spt[:, 1], ALU.mult))
            link(nc.vector.tensor_scalar(spt[:, 3], spt[:, 2], 1.0 / 15, None, ALU.mult))
            for k in (13, 11, 9, 7, 5, 3):
                link(nc.vector.scalar_tensor_tensor(out=spt[:, 3], in0=spt[:, 3], scalar=1.0 / k, in1=spt[:, 2],
                                                    op0=ALU.add, op1=ALU.mult))
            link(nc.vector.scalar_tensor_tensor(out=spt[:, 3], in0=spt[:, 3], scalar=1.0, in1=spt[:, 1],
                                                op0=ALU.add, op1=ALU.mult))
            link(nc.vector.tensor_scalar(spt[:, 4], lam, -1.0, 0.0, ALU.mult, ALU.max))
            link(nc.vector.scalar_tensor_tensor(out=spt[:, 3], in0=spt[:, 3], scalar=2.0, in1=spt[:, 4],
                                                op0=ALU.mult, op1=ALU.add))
            nc.vector.tensor_scalar(sp4[:], spt[:, 3], 4.0, None, ALU.mult).then_inc(S["sp4_ready"], 1)

            for m in range(KT):
                next_operand(m, 0, "ev_ln", a_hi, a_lo, 0)
                if m < 2:
                    split_weights(m)
            dve.wait_ge(S["ms_ready"], 1)

            def recurrence(g):
                dve.wait_ge(S["tanh_ready"], g + 1)
                if g:
                    dve.wait_ge(S["decay_ready"], g)
                link(nc.vector.tensor_scalar(den_t[:], gate_r[:], 1.0, None, ALU.add))
                nc.vector.reciprocal(den_t[:], den_t[:]).then_inc(S["den_ready"], 1)
                dve.wait_ge(S["sd_ready"], g + 1)
                dve.wait_ge(S["ix_ready"], g + 1)
                nc.vector.tensor_tensor(gate_i[:], gate_i[:], sqrt_t[:], ALU.mult).then_inc(S["u_ready"], 1)
                dve.wait_ge(S["decay_ready"], g + 1)
                dve.wait_ge(S["u_ready"], g + 1)
                nc.vector.tensor_tensor_scan(hs[:], decay[:], gate_i[:], 0.0, ALU.mult, ALU.add).then_inc(
                    S["hs_ready"], 1)
                dve.wait_ge(S["gelu_ready"], g + 1)
                dve.wait_ge(S["hs_ready"], g + 1)
                nc.vector.tensor_tensor(hs[:], hs[:], gel[:], ALU.mult).then_inc(S["hb_ready"], 1)

            for g in range(KT):
                dve.wait_ge(S["w_used"], 2 * g + 1)
                nc.vector.tensor_tensor(two(xb[:, 3:T + 3]), slot(2 * g), two(rstd[:]), ALU.mult).then_inc(
                    S["psum_free"], 1)
                split_weights(2 * g + 2)
                dve.wait_ge(S["conv0_ready"], g + 1)
                for j in (1, 2):
                    link(nc.vector.scalar_tensor_tensor(out=xc[:], in0=xb[:, j:j + T], scalar=col("conv_w", j * KT + g),
                                                        in1=xc[:], op0=ALU.mult, op1=ALU.add))
                nc.vector.scalar_tensor_tensor(out=xc[:], in0=xb[:, 3:3 + T], scalar=col("conv_w", 3 * KT + g),
                                               in1=xc[:], op0=ALU.mult, op1=ALU.add).then_inc(S["xc_ready"], 1)
                if g:
                    recurrence(g - 1)
                dve.wait_ge(S["w_used"], 2 * g + 2)
                nc.vector.tensor_tensor(two(gb[:]), slot(2 * g + 1), two(rstd[:]), ALU.mult).then_inc(
                    S["psum_free"], 1)
                split_weights(2 * g + 3)
                if g:
                    split_low(b_lo[:, g - 1], b_hi[:, g - 1], hs[:], g)
            recurrence(KT - 1)
            split_low(b_lo[:, KT - 1], b_hi[:, KT - 1], hs[:], KT)

            dve.wait_ge(S["w_used"], S_GATES + 1)
            link(nc.vector.tensor_tensor(two(g_i[0:A_HEADS]), slot(Y_GATES, A_HEADS), two(rstd[0:A_HEADS]), ALU.mult))
            nc.vector.tensor_tensor(two(g_f[0:A_HEADS]), slot(Y_GATES, A_HEADS, 32), two(rstd[32:32 + A_HEADS]),
                                    ALU.mult).then_inc(S["psum_free"], 1)
            dve.wait_ge(S["psum_free"], Y_GATES + 1)
            nc.vector.memset(g_m[0:A_HEADS], 0.0).then_inc(S["gf_ready"], 1)
            split_weights(S_GATES + 2)
            link(nc.vector.tensor_scalar(g_i[0:A_HEADS], g_i[0:A_HEADS], col("b_i", 0, A_HEADS), None, ALU.add))
            dve.wait_ge(S["gl_ready"], 1)
            link(nc.vector.tensor_scalar(g_f[0:A_HEADS], g_f[0:A_HEADS], col("b_f", 0, A_HEADS), 0.0, ALU.add, ALU.min))
            link(nc.vector.tensor_tensor(g_l[0:A_HEADS], g_f[0:A_HEADS], g_l[0:A_HEADS], ALU.subtract))
            link(nc.vector.tensor_tensor_scan(g_F[0:A_HEADS], g_l[0:A_HEADS], g_m[0:A_HEADS], 0.0, ALU.add, ALU.add))
            link(nc.vector.tensor_tensor_scan(g_m[0:A_HEADS], g_l[0:A_HEADS], g_i[0:A_HEADS], 0.0, ALU.add, ALU.max))
            link(nc.vector.tensor_tensor(g_i[0:A_HEADS], g_i[0:A_HEADS], g_F[0:A_HEADS], ALU.subtract))
            link(nc.vector.tensor_tensor(g_F[0:A_HEADS], g_F[0:A_HEADS], g_m[0:A_HEADS], ALU.subtract))
            nc.vector.tensor_scalar(g_m[0:A_HEADS], g_m[0:A_HEADS], -1.0, None, ALU.mult).then_inc(S["rows_ready"], 1)
            for j in range(8):
                dve.wait_ge(S["w_used"], S_QK + j + 1)
                nc.vector.tensor_tensor(two(qk[:, j]), slot(Y_QK + j), two(rstd[:]), ALU.mult).then_inc(
                    S["psum_free"], 1)
                split_weights(S_QK + 2 + j)
            for j in range(8):
                dve.wait_ge(S["w_used"], S_V + j + 1)
                if j >= 2:
                    dve.wait_ge(S["vt_ready"], j - 1)
                nc.vector.tensor_tensor(two(tmp[:, j % 2]), slot(Y_V + j), two(rstd[:]), ALU.mult).then_inc(
                    S["psum_free"], 1)
                split_weights(S_V + 2 + j)

            mu = units(True)
            for hd in range(A_HEADS):
                dve.wait_ge(S["abc_ready"], hd + 1)
                if hd == 0:
                    dve.wait_ge(S["ccol_ready"], 1)
                    dve.wait_ge(S["const_loaded"], 16)
                for j, t0, n, off, diag in mu:
                    if diag:
                        rows_ = BLOCKS[j][1]
                        nc.vector.scalar_tensor_tensor(
                            out=expw[0:rows_, off:off + diag], in0=abc[0:rows_, t0:t0 + diag],
                            scalar=ccol[0:rows_, j * A_HEADS + hd:j * A_HEADS + hd + 1],
                            in1=cm(C_MASK_ST, rows_, diag), op0=ALU.add, op1=ALU.add).then_inc(S["diag_ready"], 1)
                done = 0
                for u, (j, t0, n, off, diag) in enumerate(mu):
                    rows_ = BLOCKS[j][1]
                    done += (n > diag) + (diag > 0)
                    dve.wait_ge(S["expw_ready"], hd * N_EXP + done)
                    dve.wait_ge(S["s_ready"], hd * len(mu) + u + 1)
                    bank = 2 + u % 2
                    nc.vector.scalar_tensor_tensor(
                        out=st[0:rows_, off:off + n], in0=aux[0:rows_, bank * 512:bank * 512 + n],
                        scalar=float(A_DQK) ** -0.5, in1=expw[0:rows_, off:off + n], op0=ALU.mult,
                        op1=ALU.mult).then_inc(S["st_ready"], 1)
                dve.wait_ge(S["absden_ready"], hd + 1)
                dve.wait_ge(S["em_ready"], hd + 1)
                link(nc.vector.tensor_tensor(abc[:], abc[:], em[:], ALU.max))
                link(nc.vector.reciprocal(abc[:], abc[:]))
                for e in range(2):
                    nc.vector.tensor_tensor(qk[:, hd + e * A_HEADS], prod[:, e, 496:1024], abc[:], ALU.mult).then_inc(
                        S["hn_ready"], 1)
                dve.wait_ge(S["hrs_ready"], hd + 1)
                for e in range(2):
                    last = nc.vector.scalar_tensor_tensor(out=qk[:, hd + e * A_HEADS], in0=qk[:, hd + e * A_HEADS],
                                                          scalar=col("a_norm", e), in1=rs_a[:], op0=ALU.mult,
                                                          op1=ALU.mult)
                last.then_inc(S["head_done"], 1)

            dve.wait_ge(S["head_done"], A_HEADS)
            for j in range(8):
                dve.wait_ge(S["w_used"], S_O + j + 1)
                if j >= 2:
                    dve.wait_ge(S["split_hi"], KT + j - 1)
                nc.vector.tensor_tensor(two(tmp[:, j % 2]), slot(Y_O + j), two(rstd[:]), ALU.mult).then_inc(
                    S["psum_free"], 1)
                split_weights(S_O + 2 + j)
                dve.wait_ge(S["osig_ready"], j + 1)
                nc.vector.tensor_tensor(tmp[:, j % 2], tmp[:, j % 2], qk[:, j // 2 + (j % 2) * A_HEADS],
                                        ALU.mult).then_inc(S["ha_ready"], 1)
                split_low(c_lo[:, j], c_hi[:, j], tmp[:, j % 2], KT + j + 1)

            for m in range(KT):
                dve.wait_ge(S["w_used"], S_OUT0 + 2 * m + 1)
                split_weights(S_OUT0 + 2 + 2 * m)
                dve.wait_ge(S["w_used"], S_OUT0 + 2 * m + 2)
                nc.vector.tensor_tensor(two(h[:, m]), slot(Y_OUT0 + m), two(h[:, m]), ALU.add).then_inc(
                    S["psum_free"], 1)
                split_weights(S_OUT0 + 3 + 2 * m)
                next_operand(m, KT, "mlp_ln0", a_hi, a_lo, 0)
            dve.wait_ge(S["ms_ready"], 2)

            def mlp(s0, y0, hi0, t0, q, layer, last=False):
                real = t0 > 0
                for j in range(8):
                    y = y0 + j
                    dve.wait_ge(S["w_used"], s0 + j + 1 + q * 16)
                    if real:
                        o, i = tmp[:, j % 2, t0:], slot_real(y)
                    else:
                        o, i = two(tmp[:, j % 2]), slot(y)
                    nc.vector.tensor_scalar(o, i, 0.0, None, ALU.max).then_inc(S["psum_free"], 1)
                    split_weights(s0 + 2 + j, q * 4)
                    dve.wait_ge(S["split_hi"], hi0 + j + 1 + q * 8)
                    nc.vector.tensor_tensor(b_lo[:, j, t0:], tmp[:, j % 2, t0:], b_hi[:, j, t0:].bitcast(F32),
                                            ALU.subtract).then_inc(S["operand_ready"], 1)
                for j in range(8):
                    y = y0 + 8 + j
                    dve.wait_ge(S["w_used"], s0 + 8 + j + 1 + q * 16)
                    if real:
                        o, i, f = tmp[:, j % 2, t0:], slot_real(y), inv_ms[:, t0:]
                    else:
                        o, i, f = two(tmp[:, j % 2]), slot(y), two(inv_ms[:])
                    nc.vector.tensor_tensor(o, i, f, ALU.mult).then_inc(S["psum_free"], 1)
                    if not (last and layer == 1 and j >= 6):
                        split_weights(s0 + 10 + j, q * 4)
                    dve.wait_ge(S["psum_free"], y + 1 + q * 16)
                    add = nc.vector.tensor_tensor(h[:, j, t0:], h[:, j, t0:], tmp[:, j % 2, t0:], ALU.add)
                    if last:
                        add.then_inc(S["h_ready"], 1)
                        if layer == 0:
                            next_operand(j, 2 * KT, "od_ln", a_hi, a_lo, 0)

            with dve.Fori(0, QUARTERS - 1) as q:
                mlp(S_MLP0, Y_MLP0, 2 * KT, 0, q, 0)
            mlp(S_MLP0, Y_MLP0, 2 * KT, 0, QUARTERS - 1, 0, True)
            HI = 2 * KT + KT * QUARTERS

            dve.wait_ge(S["ms_ready"], 3)
            for j in range(5):
                dve.wait_ge(S["w_used"], S_LORA + j + 1)
                nc.vector.tensor_tensor(two(lora[:, j]), slot(Y_LORA + j), two(rstd[:]), ALU.mult).then_inc(
                    S["psum_free"], 1)
                split_weights(S_LORA + 2 + j)
            dve.wait_ge(S["w_used"], S_KRFF + 1)
            link(nc.vector.tensor_tensor(two(kr[:]), slot(Y_KRFF, C_ROPE), two(rstd[0:C_ROPE]), ALU.mult))
            nc.vector.tensor_tensor(two(g_f), slot(Y_KRFF, HEADS, 32), two(rstd[32:32 + HEADS]),
                                    ALU.mult).then_inc(S["psum_free"], 1)
            dve.wait_ge(S["psum_free"], Y_KRFF + 1)
            nc.vector.memset(g_zero, 0.0).then_inc(S["fgf_ready"], 1)
            split_weights(S_KRFF + 2)
            link(nc.vector.memset(q_aug[HD:HD + 2].bitcast(F32), 1.0))
            nc.vector.memset(k_aug[HD:HD + 3].bitcast(F32), 1.0).then_inc(S["aug_one"], 1)
            dve.wait_ge(S["aug_one"], 1)

            def evacuate(s):
                kind, y, _, _, _, _ = STEPS[s]
                sem_, count = ("w_used", S_FQK + s + 1) if s < D_STEPS else product_end(y)
                dve.wait_ge(S[sem_], count)
                if slot_moves(s, s % 4):
                    dve.wait_ge(item_dma[s % 4], slot_moves(s, s % 4))
                if s >= 4 and STEPS[s - 4][0] == "value":
                    dve.wait_ge(S["vt_ready"], 8 + s - 4 - 8 + 1)
                if s < D_STEPS:
                    ins = nc.vector.tensor_tensor(two(stg[:, s % 4]), slot(y), two(rstd[:]), ALU.mult)
                else:
                    ins = nc.vector.tensor_copy(two(stg[:, s % 4]), slot(y))
                ins.then_inc(S["psum_free"], 1)
                if s < D_STEPS:
                    split_weights(S_FQK + 2 + s)
                elif sem_ == "w_used":
                    split_weights(count + 1)

            def normalise(s):
                kind, _, rows_, _, gain, _ = STEPS[s]
                x = kr[:] if s == KR_STEP else stg[0:rows_, s % 4]
                dve.wait_ge(S["item_rs"], item_of(s) + 1)
                nc.vector.scalar_tensor_tensor(out=x, in0=x, scalar=col(gain, 0, rows_),
                                               in1=tmp[0:rows_, item_of(s) % 2], op0=ALU.mult, op1=ALU.mult).then_inc(
                    S["rope_ready" if kind == "rope" else "item_done"], 1)

            def rotate(s):
                rows_ = STEPS[s][2]
                x = kr[:] if s == KR_STEP else stg[0:rows_, s % 4]
                dve.wait_ge(S["item_rot"], rope_of(s) + 1)
                dve.wait_ge(S["trig_ready"], 2)
                link(nc.vector.tensor_tensor(two(rope_t[0:rows_]), aux_two(2, rows_), two(sq[0:rows_, 0]), ALU.mult))
                link(nc.vector.tensor_tensor(x, x, sq[0:rows_, 1], ALU.mult))
                nc.vector.tensor_tensor(x, x, rope_t[0:rows_], ALU.add).then_inc(S["item_done"], 1)

            two_pi = 2.0 * np.pi
            c1 = 6.28125
            c2 = float(np.float32(0.0019350051879882812))
            c3 = float(two_pi - c1 - c2)
            magic = 12582912.0

            def angles():
                dve.wait_ge(S["pos_loaded"], 16)
                dve.wait_ge(S["trig_pos"], 1)
                link(nc.vector.tensor_copy(angle, g_pos))
                link(nc.vector.tensor_scalar(angle[:, N_META:], angle[:, N_META:], float(N_META), None, ALU.add))
                link(nc.vector.tensor_scalar(angle, angle, col("freq"), None, ALU.mult))

            def reduced(k, shift):
                t, r = turns, sq[:, k]
                link(nc.vector.tensor_scalar(t, angle, 1.0 / two_pi, shift, ALU.mult, ALU.add))
                link(nc.vector.tensor_scalar(t, t, magic, None, ALU.add))
                link(nc.vector.tensor_scalar(t, t, magic, None, ALU.subtract))
                link(nc.vector.scalar_tensor_tensor(out=r, in0=t, scalar=-c1, in1=angle, op0=ALU.mult, op1=ALU.add))
                link(nc.vector.scalar_tensor_tensor(out=r, in0=t, scalar=-c2, in1=r, op0=ALU.mult, op1=ALU.add))
                link(nc.vector.scalar_tensor_tensor(out=r, in0=t, scalar=-c3, in1=r, op0=ALU.mult, op1=ALU.add))
                if k:
                    link(nc.vector.tensor_scalar(r, r, float(np.pi / 2), None, ALU.add))
                nc.vector.tensor_scalar(r, r, 3.1415925, -3.1415925, ALU.min, ALU.max).then_inc(S["trig_arg"], 1)

            for s in range(N_STEPS + 2):
                if s < N_STEPS and s != KR_STEP:
                    evacuate(s)
                if s == 0:
                    dve.wait_ge(S["fgl_ready"], 1)
                    link(nc.vector.tensor_scalar(g_f, g_f, col("od_b_f", 0, HEADS), 0.0, ALU.add, ALU.min))
                    link(nc.vector.tensor_tensor(g_l, g_l, g_f, ALU.subtract))
                    nc.vector.tensor_tensor_scan(g_F, g_l, g_zero, 0.0, ALU.add, ALU.add).then_inc(S["fF_ready"], 1)
                    dve.wait_ge(S["fhi_ready"], 1)
                    nc.vector.tensor_tensor(g_l, g_F, g_Fhi.bitcast(F32), ALU.subtract).then_inc(S["flo_ready"], 1)
                    for j in range(5):
                        dve.wait_ge(S["lrs_ready"], 1 if j < 3 else 2)
                        nc.vector.scalar_tensor_tensor(out=lora[:, j], in0=lora[:, j],
                                                       scalar=col("g_qa", j) if j < 3 else col("g_kva", j - 3),
                                                       in1=tmp[:, 0 if j < 3 else 1], op0=ALU.mult,
                                                       op1=ALU.mult).then_inc(S["ln_ready"], 1)
                    link(nc.vector.memset(vp[:, :, :, HD:2 * HD], 1.0))
                if 1 <= s <= 5:
                    split_low(b_lo[:, s - 1], b_hi[:, s - 1], lora[:, s - 1], HI + s)
                if s >= 2 and STEPS[s - 2][0] == "rope":
                    rotate(s - 2)
                if s and s <= N_STEPS and STEPS[s - 1][0] != "value":
                    normalise(s - 1)
                if s == 8:
                    angles()
                if s in (9, 10):
                    reduced(s - 9, 0.25 * (s - 9))
                if s == D_STEPS:
                    nc.vector.memset(a_lo[C_NOPE + C_ROPE:C_NOPE + C_ROPE + 1].bitcast(F32), 1.0).then_inc(S["aug_one"], 1)

            au = units(False)

            def maxima(group):
                for hd in range(HEADS):
                    for i in range(4):
                        k = (group * HEADS + hd) * 4 + i
                        dve.wait_ge(S["logit_ready"], k + 1)
                        n = BLOCKS[i + 1][0] + P
                        src = pair_of_banks(k)
                        if n > 512:
                            src, axes = src.rearrange("p (b n) -> p b n", b=2)[:, :, 0:n // 2], AX.XY
                        else:
                            src, axes = src[:, 0:n], AX.X
                        nc.vector.reduce_max(maxes[:, group, i, hd:hd + 1], src, axes).then_inc(S["max_ready"], 1)

            def attend(group):
                for hd in range(HEADS):
                    gh = group * HEADS + hd
                    pair = hd // 2
                    lo_, hi_ = (0, HD) if hd % 2 == 0 else (HD, 0)
                    dve.wait_ge(S["o_ready"], gh + 1)
                    if hd % 2 == 0 and pair >= 2:
                        dve.wait_ge(S["split_hi"], HI + 5 + group * 4 + pair - 1)
                    o = prod[:, gh % 2, 0:SEQ]
                    link(nc.vector.reciprocal(stg[lo_:lo_ + HD, 0, 0:SEQ], o[hi_:hi_ + HD]))
                    nc.vector.tensor_tensor(tmp[lo_:lo_ + HD, pair % 2, 0:SEQ], o[lo_:lo_ + HD],
                                            stg[lo_:lo_ + HD, 0, 0:SEQ], ALU.mult).then_inc(S["ot_ready"], 1)
                    if hd % 2 == 1:
                        tile = out_tile(group, pair)
                        split_low(b_lo[:, tile, N_META:], b_hi[:, tile, N_META:], tmp[:, pair % 2, 0:SEQ],
                                  HI + 5 + group * 4 + pair + 1)

            maxima(0)
            maxima(1)
            attend(0)
            dve.wait_ge(S["operand_ready"], R_ATT_D + 4)
            for j in range(4):
                sem_, count = product_end(Y_UV + j)
                dve.wait_ge(S[sem_], count)
                if j >= 2:
                    dve.wait_ge(S["vt_ready"], 12 + j - 1)
                nc.vector.tensor_copy(two(tmp[:, j % 2]), slot(Y_UV + j)).then_inc(S["psum_free"], 1)
            split_weights(S_UV + 2)
            attend(1)

            for m in range(KT):
                dve.wait_ge(S["w_used"], S_OUT1 + m + 1)
                nc.vector.tensor_tensor(h[:, m, N_META:], slot_real(Y_OUT1 + m), h[:, m, N_META:], ALU.add).then_inc(
                    S["psum_free"], 1)
                split_weights(S_OUT1 + 2 + m)
                next_operand(m, 3 * KT, "mlp_ln1", a_hi, a_lo, N_META)
            dve.wait_ge(S["ms_ready"], 4)
            HI1 = HI + 5 + 8
            with dve.Fori(0, QUARTERS - 1) as q:
                mlp(S_MLP1, Y_MLP1, HI1, N_META, q, 1)
            mlp(S_MLP1, Y_MLP1, HI1, N_META, QUARTERS - 1, 1, True)

        @block.tensor
        def _(pe):
            FULL = ((0, 0, HALF), (512, HALF, HALF))
            REAL = ((0, N_META, SEQ),)

            def product(nb, y, x, spans, q16=0, k0=0, nk=8, kb=0, start=True, stop=True, waits=None):
                hi, lo = x
                if start and y >= 2:
                    pe.wait_ge(S["psum_free"], y - 1 + q16)
                pe.wait_ge(S["w_lo_ready"], nb + 1 + q16)
                for k in range(nk):
                    if waits is not None:
                        pe.wait_ge(S["operand_ready"], waits + k + 1)
                    blk = slice((k0 + k) * P, (k0 + k + 1) * P)
                    for i, (w, xx) in enumerate(((w_hi, hi), (w_hi, lo), (w_lo, hi))):
                        for c, t0, n in spans:
                            last = nc.tensor.matmul(prod[:, y % 2, c:c + n], w[:, nb % 2, blk],
                                                    xx[:, kb + k, t0:t0 + n], start=start and k == 0 and i == 0,
                                                    stop=stop and k == nk - 1 and i == 2)
                return last

            A, B, C = (a_hi, a_lo), (b_hi, b_lo), (c_hi, c_lo)

            def stats(k, t0=0):
                pe.wait_ge(S["sq_summed"], (k + 1) * KT)
                if t0:
                    nc.tensor.matmul(aux[:, 0:SEQ], cm(C_ONES), sq_sum[:, t0:], start=True, stop=True).then_inc(
                        S["stat_ready"], 1)
                else:
                    for c, f, n in FULL:
                        last = nc.tensor.matmul(aux[:, c:c + n], cm(C_ONES), sq_sum[:, f:f + n], start=True, stop=True)
                    last.then_inc(S["stat_ready"], 1)

            for g in range(KT):
                product(2 * g, 2 * g, A, FULL, waits=R_X0 if g == 0 else None).then_inc(S["w_used"], 1)
                if g == 0:
                    pe.wait_ge(S["const_loaded"], 16)
                    stats(0)
                    pe.wait_ge(S["wr_loaded"], 16)
                    pe.wait_ge(S["ms_ready"], 1)
                product(2 * g + 1, 2 * g + 1, A, FULL).then_inc(S["w_used"], 1)
                pe.wait_ge(S["xc_ready"], g + 1)
                if g:
                    pe.wait_ge(S["sig_ready"], g)
                for which in range(2):
                    for c, f, n in FULL:
                        last = nc.tensor.matmul(aux[:, which * 1024 + c:which * 1024 + c + n],
                                                wr[:, (which * KT + g) * P:(which * KT + g + 1) * P], xc[:, f:f + n],
                                                start=True, stop=True)
                last.then_inc(S["gates_ready"], 1)
            product(S_GATES, Y_GATES, A, FULL).then_inc(S["w_used"], 1)
            for j in range(8):
                product(S_QK + j, Y_QK + j, A, FULL).then_inc(S["w_used"], 1)

            def transpose_v(j, y, base):
                pe.wait_ge(S["psum_free"], y + 1)
                if base + j >= 2:
                    pe.wait_ge(S["v_copied"], base + j - (base != 8))
                a = v_bank(j, base)
                for b, (t0, n) in enumerate(BLOCKS):
                    c = a if b == 0 else a + 512 + (b - 1) * P
                    src = stg[:, j] if base == 8 else tmp[:, j % 2]
                    last = nc.tensor.transpose(aux[0:n, c:c + P], src[:, t0:t0 + n], cm(C_IDENT))
                last.then_inc(S["vt_ready"], 1)

            pe.wait_ge(S["sig_ready"], KT)
            for j in range(8):
                product(S_V + j, Y_V + j, A, FULL).then_inc(S["w_used"], 1)
                if j:
                    transpose_v(j - 1, Y_V + j - 1, 0)
            transpose_v(7, Y_V + 7, 0)

            pe.wait_ge(S["rows_ready"], 1)
            pe.wait_ge(S["v_copied"], 8)
            for j, (t0, n) in enumerate(BLOCKS):
                last = nc.tensor.matmul(aux[0:n, j * A_HEADS:(j + 1) * A_HEADS], g_i[0:A_HEADS, t0:t0 + n],
                                        cm(C_IDENT, A_HEADS, A_HEADS), start=True, stop=True)
            last.then_inc(S["ccol_psum"], 1)
            pe.wait_ge(S["ccol_ready"], 1)
            pe.wait_ge(S["psum_free"], Y_V + 8)
            mu = units(True)
            for hd in range(A_HEADS):
                if hd:
                    pe.wait_ge(S["hms_ready"], hd)
                for k, row in enumerate((g_F, g_m)):
                    if k:
                        pe.wait_ge(S["abc_ready"], hd + 1)
                    for c, f, n in FULL:
                        last = nc.tensor.matmul(aux[:, 1024 + c:1024 + c + n], cm(C_SEL + hd, A_HEADS),
                                                row[0:A_HEADS, f:f + n], start=True, stop=True)
                    last.then_inc(S["bc_ready"], 1)
                pe.wait_ge(S["em_ready"], hd + 1)

                def scores(u):
                    j, t0, n, off, _ = mu[u]
                    if u >= 2:
                        pe.wait_ge(S["st_ready"], hd * len(mu) + u - 1)
                    b = (2 + u % 2) * 512
                    nc.tensor.matmul(aux[0:BLOCKS[j][1], b:b + n],
                                     qk[:, A_HEADS + hd, BLOCKS[j][0]:BLOCKS[j][0] + BLOCKS[j][1]],
                                     qk[:, hd, t0:t0 + n], start=True, stop=True).then_inc(S["s_ready"], 1)

                scores(0)
                for u, (j, t0, n, off, _) in enumerate(mu):
                    if u + 1 < len(mu):
                        scores(u + 1)
                    rows_ = BLOCKS[j][1]
                    pe.wait_ge(S["st_ready"], hd * len(mu) + u + 1)
                    for e in range(3):
                        acc = prod[:, e, 496 + t0:496 + t0 + n] if e < 2 else aux[:, 496 + t0:496 + t0 + n]
                        w = v[0:rows_, j, hd * A_DV + e * P:hd * A_DV + (e + 1) * P] if e < 2 else cm(C_ONES, rows_)
                        last = nc.tensor.matmul(acc, w, st[0:rows_, off:off + n], start=u <= 1,
                                                stop=u in (0, len(mu) - 1))
                last.then_inc(S["acc_ready"], 1)
                pe.wait_ge(S["hnsq_ready"], 2 * hd + 2)
                for e in range(2):
                    for c, f, n in FULL:
                        last = nc.tensor.matmul(aux[:, 1024 + c:1024 + c + n], cm(C_ONES),
                                                expw[:, e * T + f:e * T + f + n], start=e == 0, stop=e == 1)
                last.then_inc(S["hstat_ready"], 1)

            for j in range(8):
                product(S_O + j, Y_O + j, A, FULL).then_inc(S["w_used"], 1)
            for m in range(KT):
                first = m == 0
                product(S_OUT0 + 2 * m, Y_OUT0 + m, B, FULL, stop=False).then_inc(S["w_used"], 1)
                product(S_OUT0 + 2 * m + 1, Y_OUT0 + m, C, FULL, start=False,
                        waits=R_HA if first else None).then_inc(S["w_used"], 1)
            stats(1)

            def mlp(s0, y0, r_hid, x, hid, spans, q, first_wait, q8):
                for j in range(8):
                    product(s0 + j, y0 + j, x, spans, q * 16, waits=first_wait if j == 0 else None).then_inc(
                        S["w_used"], 1)
                for j in range(8):
                    product(s0 + 8 + j, y0 + 8 + j, hid, spans, q * 16,
                            waits=(r_hid + q * 8) if j == 0 else None).then_inc(S["w_used"], 1)

            pe.wait_ge(S["operand_ready"], R_X1 + KT)
            with pe.Fori(0, QUARTERS - 1) as q:
                mlp(S_MLP0, Y_MLP0, R_MLP0, A, B, FULL, q, None, None)
            mlp(S_MLP0, Y_MLP0, R_MLP0, A, B, FULL, QUARTERS - 1, None, None)

            product(S_LORA, Y_LORA, A, FULL, waits=R_X2).then_inc(S["w_used"], 1)
            stats(2)
            for j in range(1, 5):
                product(S_LORA + j, Y_LORA + j, A, FULL).then_inc(S["w_used"], 1)
            product(S_KRFF, Y_KRFF, A, FULL).then_inc(S["w_used"], 1)

            def lora_stats():
                pe.wait_ge(S["ms_ready"], 3)
                for k, (j0, n_) in enumerate(((0, 3), (3, 2))):
                    pe.wait_ge(S["lsq_ready"], j0 + n_)
                    for j in range(n_):
                        for c, f, n in FULL:
                            last = nc.tensor.matmul(aux[:, k * 1024 + c:k * 1024 + c + n], cm(C_ONES),
                                                    lora_sq[:, j0 + j, f:f + n], start=j == 0, stop=j == n_ - 1)
                    last.then_inc(S["lstat_ready"], 1)

            def item_stat(s):
                _, _, rows_, mat, _, _ = STEPS[s]
                k = item_of(s)
                pe.wait_ge(S["item_sq"], k + 1)
                if k:
                    pe.wait_ge(S["item_ms"], k)
                else:
                    pe.wait_ge(S["lms_ready"], 2)
                for c, f, n in FULL:
                    last = nc.tensor.matmul(aux[0:rows_, c:c + n], cm(mat, rows_, rows_), tmp[0:rows_, k % 2, f:f + n],
                                            start=True, stop=True)
                last.then_inc(S["item_stat"], 1)

            def rotate(s):
                rows_ = STEPS[s][2]
                x = kr[:] if s == KR_STEP else stg[0:rows_, s % 4]
                pe.wait_ge(S["rope_ready"], rope_of(s) + 1)
                if rope_of(s):
                    pe.wait_ge(S["item_done"], item_of(s))
                else:
                    pe.wait_ge(S["v_copied"], 12)
                for c, f, n in FULL:
                    last = nc.tensor.matmul(aux[0:rows_, 1024 + c:1024 + c + n], cm(C_ROT, rows_, rows_),
                                            x[:, f:f + n], start=True, stop=True)
                last.then_inc(S["item_rot"], 1)

            def low_rank_product(y):
                c = y - Y_UQ
                if c < 6:
                    last = product(S_UQ + c // 2, y, B, FULL, k0=3 * (c % 2), nk=3, waits=R_LORA if c == 0 else None)
                else:
                    tile, i = divmod(c - 6, 4)
                    last = product(S_UK + tile, y, B, FULL, k0=2 * i, nk=2, kb=3, waits=R_LORA + 3 if c == 6 else None)
                last.then_inc(S[product_end(y)[0]], 1)

            for s in range(N_STEPS + 2):
                if s < D_STEPS:
                    product(S_FQK + s, STEPS[s][1], A, FULL).then_inc(S["w_used"], 1)
                elif s < N_STEPS and s != KR_STEP:
                    low_rank_product(STEPS[s][1])
                if s == 0:
                    lora_stats()
                if s >= 2 and STEPS[s - 2][0] == "rope":
                    rotate(s - 2)
                if s and s <= N_STEPS:
                    if STEPS[s - 1][0] == "value":
                        transpose_v(s - 1 - 8, STEPS[s - 1][1], 8)
                    else:
                        item_stat(s - 1)

            au = units(False)

            def maxima(group, k_rows):
                if group == 0:
                    pe.wait_ge(S["augF"], 32)
                    pe.wait_ge(S["bf_ready"], 3)
                    pe.wait_ge(S["psum_free"], Y_UV)
                    pe.wait_ge(S["item_ms"], item_of(N_STEPS))
                    pe.wait_ge(S["item_done"], item_of(N_STEPS))
                pe.wait_ge(S["aug_one"], group + 1)
                last_step = (D_STEPS, N_STEPS)[group]
                for i in range(4):
                    pe.wait_ge(item_dma[i], slot_moves(last_step, i))
                q, k_ = q_of[group], k_of[group]
                for hd in range(HEADS):
                    for i in range(4):
                        k = (group * HEADS + hd) * 4 + i
                        if k >= 4:
                            pe.wait_ge(S["max_ready"], k - 3)
                        if group and hd == 0 and i == 2:
                            pe.wait_ge(S["mxneg_ready"], 1)
                        o = pair_of_banks(k)
                        qs = q[0:k_rows, hd, BLOCKS[i + 1][0]:BLOCKS[i + 1][0] + P]
                        n = BLOCKS[i + 1][0] + P
                        halves = ((0, 0, HALF), (512, HALF, HALF)) if n > 512 else ((0, 0, n),)
                        for c, f, m in halves:
                            nc.tensor.matmul(o[:, c:c + m], qs, k_[0:k_rows, hd, f:f + m], start=True,
                                             stop=c + m < halves[-1][0] + halves[-1][2])
                        nc.tensor.matmul(o[:, c + m - P:c + m], ident_bf[:], mask_ts_bf[:], start=False,
                                         stop=True).then_inc(S["logit_ready"], 1)

            def max_rows(group):
                pe.wait_ge(S["max_ready"], (group + 1) * HEADS * 4)
                for i in range(4):
                    last = nc.tensor.matmul(aux[0:HEADS, i * P:(i + 1) * P], maxes[:, group, i, :], cm(C_IDENT),
                                            start=True, stop=True)
                last.then_inc(S["mxrow_ready"], 1)

            def attend(group, row_count):
                pe.wait_ge(S["mxneg_ready"], 2)
                pe.wait_ge(mx_dma[group], 16)

                def logits(hd, u):
                    j, t0, n, off, diag = au[u]
                    k = (group * HEADS + hd) * NB + u
                    if hd > 0 or u >= 4:
                        pe.wait_ge(S["p_ready"], k - 3)
                    o = aux[0:BLOCKS[j][1], (k % 4) * 512:(k % 4) * 512 + n]
                    last = nc.tensor.matmul(
                        o, k_of[group][0:row_count, hd, BLOCKS[j][0]:BLOCKS[j][0] + BLOCKS[j][1]].bitcast(F32),
                        q_of[group][0:row_count, hd, t0:t0 + n].bitcast(F32), start=True, stop=not diag)
                    if diag:
                        last = nc.tensor.matmul(o[:, 0:P], ident_bf[:], mask_st_bf[:], start=False, stop=True)
                    last.then_inc(S["l_ready"], 1)

                def weigh(hd, u):
                    j, t0, n, off, diag = au[u]
                    gh = group * HEADS + hd
                    if u == 0 and hd >= 2:
                        pe.wait_ge(S["ot_ready"], gh - 1)
                    pe.wait_ge(S["p_ready"], gh * NB + u + 1)
                    rows_ = BLOCKS[j][1]
                    last = nc.tensor.matmul(prod[:, gh % 2, t0 - N_META:t0 - N_META + n],
                                            vp[0:rows_, j, hd // 2, (hd % 2) * HD:(hd % 2) * HD + P],
                                            pt[0:rows_, hd % 2, off:off + n], start=u == 0, stop=u == NB - 1)
                    if u == NB - 1:
                        last.then_inc(S["o_ready"], 1)

                for hd in range(HEADS):
                    for u in range(NB):
                        logits(hd, u)
                        if hd:
                            weigh(hd - 1, u)
                for u in range(NB):
                    weigh(HEADS - 1, u)
                pe.wait_ge(S["ot_ready"], (group + 1) * HEADS)

            maxima(0, HD + 2)
            max_rows(0)
            maxima(1, C_NOPE + C_ROPE)
            max_rows(1)
            attend(0, HD + 3)
            for c in range(4):
                low_rank_product(Y_UV + c)
                if c:
                    transpose_v(c - 1, Y_UV + c - 1, 12)
            transpose_v(3, Y_UV + 3, 12)
            pe.wait_ge(S["v_copied"], 16)
            attend(1, C_NOPE + C_ROPE + 1)

            pe.wait_ge(S["operand_ready"], R_ATT_C + 4)
            for m in range(KT):
                product(S_OUT1 + m, Y_OUT1 + m, B, REAL).then_inc(S["w_used"], 1)
            stats(3, N_META)
            pe.wait_ge(S["operand_ready"], R_X3 + KT)
            with pe.Fori(0, QUARTERS - 1) as q:
                mlp(S_MLP1, Y_MLP1, R_MLP1, A, B, REAL, q, None, None)
            mlp(S_MLP1, Y_MLP1, R_MLP1, A, B, REAL, QUARTERS - 1, None, None)


def _blocks(w, columns):
    return w[:, columns].reshape(-1, P, len(columns)).transpose(1, 0, 2)


def _stream(ev_w_in, ev_w_out, od_w_in, od_w_uq, od_w_ukv, od_w_out, w_ff1, w_ff2):
    s = np.zeros((S_END, P, 8, P), np.float32)
    q0, k0, v0, o0, i0, f0, x0, b0 = np.cumsum([0, 512, 512, 1024, 1024, A_HEADS, A_HEADS, D_MODEL])
    for g in range(KT):
        s[S_RG + 2 * g] = _blocks(ev_w_in, range(x0 + g * P, x0 + (g + 1) * P))
        s[S_RG + 2 * g + 1] = _blocks(ev_w_in, range(b0 + g * P, b0 + (g + 1) * P))
    s[S_GATES][:, :, 0:A_HEADS] = _blocks(ev_w_in, range(i0, i0 + A_HEADS))
    s[S_GATES][:, :, 32:32 + A_HEADS] = _blocks(ev_w_in, range(f0, f0 + A_HEADS))
    for first, at, n in ((S_QK, q0, 8), (S_V, v0, 8), (S_O, o0, 8)):
        for j in range(n):
            s[first + j] = _blocks(ev_w_in, range(at + j * P, at + (j + 1) * P))
    for m in range(KT):
        c = range(m * P, (m + 1) * P)
        s[S_OUT0 + 2 * m] = _blocks(ev_w_out[D_MODEL:], c)
        s[S_OUT0 + 2 * m + 1] = _blocks(ev_w_out[:D_MODEL], c)
        rows = _blocks(od_w_out, c)
        for group in range(2):
            for pair in range(4):
                s[S_OUT1 + m][:, out_tile(group, pair)] = rows[:, pair + (0 if group else 4)]
    for first, layer in ((S_MLP0, 0), (S_MLP1, 1)):
        for q in range(QUARTERS):
            for j in range(8):
                c = q * D_MODEL + j * P
                s[first + 16 * q + j] = _blocks(w_ff1[layer], range(c, c + P))
                s[first + 16 * q + 8 + j] = _blocks(w_ff2[layer][q * D_MODEL:(q + 1) * D_MODEL],
                                                    range(j * P, (j + 1) * P))
    kr0 = Q_LORA + KV_LORA
    fq0 = kr0 + C_ROPE
    for j in range(5):
        s[S_LORA + j] = _blocks(od_w_in, range(j * P, (j + 1) * P))
    s[S_KRFF][:, :, 0:C_ROPE] = _blocks(od_w_in, range(kr0, kr0 + C_ROPE))
    s[S_KRFF][:, :, 32:32 + HEADS] = _blocks(od_w_in, range(fq0 + 3 * 512, fq0 + 3 * 512 + HEADS))
    for j in range(12):
        s[(S_FQK if j < 8 else S_FV - 8) + j] = _blocks(od_w_in, range(fq0 + j * P, fq0 + (j + 1) * P))
    for m in range(6):
        if m < 2:
            c = [hd * 96 + C_NOPE + f for hd in range(4 * m, 4 * m + 4) for f in range(C_ROPE)]
        else:
            c = [hd * 96 + f for hd in (2 * (m - 2), 2 * (m - 2) + 1) for f in range(C_NOPE)]
        s[S_UQ + m // 2][:, 3 * (m % 2):3 * (m % 2) + 3] = _blocks(od_w_uq, c)
    for m in range(4):
        for first, off in ((S_UK, 0), (S_UV, C_NOPE)):
            c = [hd * 128 + off + f for hd in (2 * m, 2 * m + 1) for f in range(64)]
            s[first][:, 2 * m:2 * m + 2] = _blocks(od_w_ukv, c)
    return s.reshape(S_END, P, TILE)


def _columns(x):
    c = np.zeros((P, N_COLS), np.float32)

    def put(name, values):
        at = COLS[name][0]
        values = np.asarray(values, np.float32).reshape(-1, P).T
        c[:, at:at + values.shape[1]] = values

    put("ev_ln", x["ev_ln"]), put("od_ln", x["od_ln"])
    put("mlp_ln0", x["mlp_ln"][0]), put("mlp_ln1", x["mlp_ln"][1])
    for ours, theirs in (("conv_w", "ev_conv_w"), ("conv_b", "ev_conv_b"), ("b_ra", "ev_b_ra"), ("b_rx", "ev_b_rx"),
                         ("lam", "ev_lam"), ("a_norm", "ev_a_norm"), ("g_qa", "od_g_qa"), ("g_kva", "od_g_kva")):
        put(ours, x[theirs])
    for name in ("g_qn", "g_qr", "g_kn", "g_kr", "g_fq", "g_fk"):
        g = x["od_" + name].reshape(-1)
        put(name, np.tile(g, P // g.size))
    c[0:A_HEADS, COLS["b_i"][0]] = x["ev_b_if"][0, :A_HEADS]
    c[0:A_HEADS, COLS["b_f"][0]] = x["ev_b_if"][0, A_HEADS:]
    c[0:HEADS, COLS["od_b_f"][0]] = x["od_b_f"][0]
    half = C_ROPE // 2
    freqs = np.float32(10000.0) ** (-np.arange(half, dtype=np.float32) / np.float32(half))
    c[:, COLS["freq"][0]] = np.tile(freqs.astype(np.float32), P // half)
    c[:, COLS["eps"][0]:COLS["eps"][0] + 3] = [EPS, EPS * HD, EPS * (C_NOPE + C_ROPE)]
    return c


def _constants():
    c = np.zeros((N_CONST, P, P), np.float32)
    i = np.arange(P)
    c[C_IDENT] = np.eye(P)
    c[C_ONES] = 1.0
    c[C_BLK64] = (i[:, None] // 64 == i[None, :] // 64) / 64.0
    c[C_BLK32] = (i[:, None] // 32 == i[None, :] // 32) / 32.0
    for m in range(P):
        c[C_ROT, m + 16 if m % 32 < 16 else m - 16, m] = -1.0 if m % 32 < 16 else 1.0
    c[C_MASK_ST] = np.where(i[:, None] > i[None, :], MASKED, 0.0)
    c[C_MASK_TS] = c[C_MASK_ST].T
    for hd in range(A_HEADS):
        c[C_SEL + hd, hd] = 1.0
    return c.transpose(1, 0, 2).reshape(P, N_CONST * P)


def kernel(**inputs):
    import concourse.bacc as bacc
    from concourse.bass_utils import run_bass_kernel_spmd

    x = {k: np.asarray(a) for k, a in inputs.items()}
    arrays = {
        "in_h": np.ascontiguousarray(np.concatenate([x["meta"], x["x"][0]], axis=0).T),
        "in_positions": np.ascontiguousarray(x["positions"]),
        "in_stream": _stream(x["ev_w_in"][0], x["ev_w_out"][0], x["od_w_in"][0], x["od_w_uq"][0], x["od_w_ukv"][0],
                             x["od_w_out"][0], x["w_ff1"], x["w_ff2"]),
        "in_gate_w": np.ascontiguousarray(np.concatenate([x["ev_w_ra"][0], x["ev_w_rx"][0]], axis=0)),
        "in_cols": _columns(x),
        "in_const": _constants(),
    }
    nc = bacc.Bacc("TRN2", target_bir_lowering=False, num_devices=1)
    args = [nc.dram_tensor(n, a.shape, mybir.dt.from_np(a.dtype), kind="ExternalInput").ap()
            for n, a in arrays.items()]
    args.append(nc.dram_tensor("out_t", (D_MODEL, SEQ), mybir.dt.float32, kind="ExternalOutput").ap())
    trunk(nc, *args)
    r = run_bass_kernel_spmd(nc, [arrays], core_ids=[0])
    got = np.asarray(r.results[0]["out_t"])
    return np.ascontiguousarray(got.T).reshape(1, SEQ, D_MODEL)
```

```python
import numpy as np

import concourse.bass as bass
from concourse import mybir
from contextlib import ExitStack


P = 128
D_MODEL, SEQ, N_META = 1024, 512, 16
T = N_META + SEQ
HALF = T // 2
KT = D_MODEL // P
D_FF = 4 * D_MODEL
QUARTERS = D_FF // D_MODEL
A_HEADS, A_DQK, A_DV = 4, 128, 256
HEADS, C_NOPE, C_ROPE, HD = 8, 64, 32, 64
Q_LORA, KV_LORA = 384, 256
EPS = 1e-6
BLOCKS = [(i, min(P, T - i)) for i in range(0, T, P)]
NB = len(BLOCKS)
MASKED = -1e30

TILE = 8 * P
S_RG = 0
S_GATES = S_RG + 2 * KT
S_QK = S_GATES + 1
S_V = S_QK + 8
S_O = S_V + 8
S_OUT0 = S_O + 8
S_MLP0 = S_OUT0 + 16
S_LORA = S_MLP0 + 64
S_KRFF = S_LORA + 5
S_FQK = S_KRFF + 1
S_FV = S_FQK + 8
S_UQ = S_FV + 4
S_UK = S_UQ + 3
S_UV = S_UK + 1
S_OUT1 = S_UV + 1
S_MLP1 = S_OUT1 + 8
S_END = S_MLP1 + 64

Y_RG = 0
Y_GATES = Y_RG + 16
Y_QK = Y_GATES + 1
Y_V = Y_QK + 8
Y_O = Y_V + 8
Y_OUT0 = Y_O + 8
Y_MLP0 = Y_OUT0 + 8
Y_LORA = Y_MLP0 + 64
Y_KRFF = Y_LORA + 5
Y_FQK = Y_KRFF + 1
Y_FV = Y_FQK + 8
Y_UQ = Y_FV + 4
Y_UK = Y_UQ + 6
Y_UV = Y_UK + 4
Y_OUT1 = Y_UV + 4
Y_MLP1 = Y_OUT1 + 8

R_X0 = 0
R_HB = R_X0 + KT
R_HA = R_HB + KT
R_X1 = R_HA + KT
R_MLP0 = R_X1 + KT
R_X2 = R_MLP0 + KT * QUARTERS
R_LORA = R_X2 + KT
R_ATT_D = R_LORA + 5
R_ATT_C = R_ATT_D + 4
R_X3 = R_ATT_C + 4
R_MLP1 = R_X3 + KT

COLS = {}


def _col(name, n):
    COLS[name] = sum(w for _, w in COLS.values()), n


for _name, _n in (("ev_ln", 8), ("od_ln", 8), ("mlp_ln0", 8), ("mlp_ln1", 8), ("conv_w", 32), ("conv_b", 8),
                  ("b_ra", 8), ("b_rx", 8), ("lam", 8), ("a_norm", 2), ("g_qa", 3), ("g_kva", 2), ("g_qn", 1),
                  ("g_qr", 1), ("g_kn", 1), ("g_kr", 1), ("g_fq", 1), ("g_fk", 1), ("b_i", 1), ("b_f", 1),
                  ("od_b_f", 1), ("freq", 1), ("eps", 3)):
    _col(_name, _n)
N_COLS = sum(w for _, w in COLS.values())
C_IDENT, C_ONES, C_BLK64, C_BLK32, C_ROT, C_MASK_ST, C_MASK_TS, C_SEL = range(8)
STEPS = [("norm", Y_FQK + k, P, C_BLK64, "g_fq" if k < 4 else "g_fk", HD if k < 4 else 1) for k in range(8)]
STEPS += [("rope", None, C_ROPE, C_BLK32, "g_kr", 1)]
STEPS += [("value", Y_FV + j, P, None, None, None) for j in range(4)]
STEPS += [("rope", Y_UQ + c, P, C_BLK32, "g_qr", C_NOPE + C_ROPE) for c in range(2)]
STEPS += [("norm", Y_UQ + 2 + c, P, C_BLK64, "g_qn", C_NOPE + C_ROPE) for c in range(4)]
STEPS += [("norm", Y_UK + c, P, C_BLK64, "g_kn", 1) for c in range(4)]
N_STEPS = len(STEPS)
KR_STEP, V_STEP = 8, 9
D_STEPS, C_NORMS = 13, 15
MAX_UNITS = [(i, 0, P * (i + 1) + N_META) for i in range(3)] + [(3, 0, HALF), (3, HALF, HALF)]


def tile_of(s):
    return S_FQK + s - (s > KR_STEP)



def item_of(s):
    return sum(kind != "value" for kind, *_ in STEPS[:s])


def rope_of(s):
    return sum(kind == "rope" for kind, *_ in STEPS[:s])


def item_moves(s):
    kind, y, rows, _, gain, _ = STEPS[s]
    if s == KR_STEP:
        return "k", [(hd, C_NOPE, 0, C_ROPE) for hd in range(HEADS)]
    if kind == "rope":
        return "q", [(4 * (y - Y_UQ) + e, C_NOPE, e * C_ROPE, C_ROPE) for e in range(4)]
    first = s % 4 if s < D_STEPS else y - (Y_UQ + 2 if gain == "g_qn" else Y_UK)
    return ("q" if gain in ("g_fq", "g_qn") else "k"), [(2 * first + e, 0, e * HD, HD) for e in range(2)]


def slot_moves(s, slot):
    return sum(16 * len(item_moves(i)[1]) for i in range(min(s, C_NORMS)) if i % 4 == slot and STEPS[i][0] != "value")


def product_end(y):
    c = y - Y_UQ
    if c < 6:
        return ("part_ready", c // 2 + 1) if c % 2 == 0 else ("w_used", S_UQ + c // 2 + 1)
    tile, i = divmod(c - 6, 4)
    return ("part_ready", 3 + 3 * tile + i + 1) if i < 3 else ("w_used", S_UK + tile + 1)


def out0_tile(m, part):
    return S_OUT0 + (m + 2 * part if m < 2 else 2 * m + part)


def out_tile(group, pair):
    return (2, 3, 4, 7)[pair] if group else (5, 6, 0, 1)[pair]

N_CONST = C_SEL + A_HEADS


def trunk(nc, h_in, positions, stream, gate_w, cols_in, const_in, out):
    F32, F32R, BF16, I32 = mybir.dt.float32, mybir.dt.float32r, mybir.dt.bfloat16, mybir.dt.int32
    ALU, ACT, AX = mybir.AluOpType, mybir.ActivationFunctionType, mybir.AxisListType
    ctx = ExitStack()
    with ctx:
        def sb(name, shape, dt=F32, scope=ctx):
            return scope.enter_context(nc.sbuf_tensor(name, shape, dt))

        def sem(name):
            return ctx.enter_context(nc.semaphore(name))

        h = sb("h", [P, KT, T])
        a_hi, a_lo = sb("a_hi", [P, KT, T], F32R), sb("a_lo", [P, KT, T], F32R)
        b_hi, b_lo = sb("b_hi", [P, KT, T], F32R), sb("b_lo", [P, KT, T], F32R)
        raw = sb("raw", [P, 4, TILE])
        w_hi, w_lo = sb("w_hi", [P, 2, TILE], F32R), sb("w_lo", [P, 2, TILE], F32R)
        cols = sb("cols", [P, N_COLS])
        const = sb("const", [P, N_CONST * P])
        ident_bf, mask_st_bf, mask_ts_bf = (sb(n, [P, P], BF16) for n in ("ident_bf", "mask_st_bf", "mask_ts_bf"))
        inv_ms = sb("inv_ms", [P, T])
        rstd = inv_ms
        sq = sb("sq", [P, 2, T])
        sq_sum = sb("sq_sum", [P, T])
        tmp = sb("tmp", [P, 2, T])

        even = ExitStack()
        c_hi, c_lo = sb("c_hi", [P, KT, T], F32R, even), sb("c_lo", [P, KT, T], F32R, even)
        qk = sb("qk", [P, 2 * A_HEADS, T], F32, even)
        v = sb("v", [P, NB, A_HEADS * A_DV], F32, even)
        even.close()
        rg = ExitStack()
        xc, gate_i, sqrt_t, decay, gb, gel, hs = (
            sb(n, [P, 2, T], F32, rg) for n in ("xc", "gate_i", "sqrt_t", "decay", "gb", "gel", "hs"))
        gate_r = sb("gate_r", [P, T], F32, rg)
        sb("pad_rg", [P, (2 * KT - 15 + 2 * A_HEADS) * T], F32, rg)
        xb = sb("xb", [P, T + 3], F32, rg)
        wr = sb("wr", [P, 2 * KT * P], F32, rg)
        sp4, sp8 = sb("sp4", [P, KT], F32, rg), sb("sp8", [P, KT], F32, rg)
        spt = sb("spt", [P, 5, KT], F32, rg)
        rg.close()
        ml = ExitStack()
        N_PT = SEQ + sum(T - t0 for t0, _ in BLOCKS[1:])
        N_ST = N_PT + N_META
        expw = sb("expw", [P, 2, N_ST], F32, ml)
        st = sb("st", [P, N_ST], F32, ml)
        abc, em = sb("abc", [P, 2, T], F32, ml), sb("em", [P, 2, T], F32, ml)
        rs_a = sb("rs_a", [P, T], F32, ml)
        ccol = sb("ccol", [P, NB * A_HEADS], F32, ml)
        ml.close()

        odd = ExitStack()
        q_aug = sb("q_aug", [P, HEADS, T], F32R, odd)
        k_aug = sb("k_aug", [P, HEADS, T], F32R, odd)
        vp = sb("vp", [P, NB, 4, 192], F32, odd)
        pt = sb("pt", [P, 2, N_PT], F32, odd)
        kr = sb("kr", [C_ROPE, T], F32, odd)
        gate_row = sb("gate_row", [P, T], F32, odd)
        stg = sb("stg", [P, 4, T], F32, odd)
        maxes = sb("maxes", [P, 2, 5, HEADS], F32, odd)
        odd.close()
        od2 = ExitStack()
        sb("pad_aug", [P, 2 * HEADS * T], F32, od2)
        lora_sq = sb("lora_sq", [P, 5, T], F32, od2)
        sb("pad_vp", [P, NB * 4 * 192 - 5 * T], F32, od2)
        lora = sb("lora", [P, 5, T], F32, od2)
        od2.close()
        g_f, g_l, g_i, g_F, g_m = tmp[0:HEADS, 0], tmp[0:HEADS, 1], sq[0:HEADS, 0], sq[0:HEADS, 1], sq_sum[0:HEADS]
        o_f, o_l, o_zero = gate_row[0:HEADS], stg[0:HEADS, 3], stg[0:HEADS, 2]
        o_hi = gate_row[0:HEADS].bitcast(F32R)
        g_pos = sq_sum[:].bitcast(I32)
        rope_t = sq_sum
        angle, turns = lora[:, 0], lora[:, 1]
        q_of, k_of = (q_aug, a_hi), (k_aug, a_lo)
        uv = (sq[:, 0], sq[:, 1], stg[:, 2], stg[:, 3])
        lora_rs = (lora_sq[:, 0], lora_sq[:, 3])
        neg_max = (sq_sum[0:HEADS, 0:SEQ], stg[0:HEADS, 1, 0:SEQ])

        prod = ctx.enter_context(nc.psum_tensor("prod", [P, 2, 1024], F32))
        aux = ctx.enter_context(nc.psum_tensor("aux", [P, 2048], F32))

        names = ["h_loaded0", "h_loaded1", "h_loaded2", "h_loaded3", "cols_loaded", "const_loaded", "wr_loaded",
                 "raw_full0", "raw_full1", "raw_full2", "raw_full3", "w_hi_ready", "w_lo_ready", "w_used",
                 "part_ready", "psum_free", "operand_ready", "a_hi_ready", "sq_ready", "sq_summed",
                 "stat_ready", "ms_ready", "h_ready", "dve_chain", "act_chain", "pool_chain", "bf_ready",
                 "sp4_ready", "lam_e_ready", "conv0_ready", "xc_ready", "gates_ready", "sig_ready",
                 "tanh_ready", "sqrt_ready", "den_ready", "rden_ready", "ix_ready", "decay_ready", "u_ready",
                 "hs_ready", "hb_ready", "gsq_ready", "gz_ready", "gsig_ready", "gelu_ready", "split_hi",
                 "zero_ready", "gf_ready", "gl_ready", "rows_ready", "ccol_psum", "ccol_ready", "bc_ready",
                 "abc_ready", "em_ready", "diag_ready", "expw_ready", "expd_ready", "s_ready", "st_ready",
                 "acc_ready", "absden_ready", "hn_ready", "hnsq_ready", "hstat_ready", "hms_ready", "hrs_ready",
                 "head_done", "osig_ready", "ha_ready", "vt_ready", "v_copied", "hid_ready", "trig_pos",
                 "trig_ready", "trig_arg", "lsq_ready", "lstat_ready", "lms_ready", "lrs_ready", "ln_ready",
                 "fF_ready", "fgf_ready", "fgl_ready", "augF", "aug_one", "item_sq", "item_stat", "item_ms",
                 "item_rs", "item_done", "item_rot", "item_dma0", "item_dma1", "item_dma2", "item_dma3",
                 "norm_dma0", "norm_dma1", "norm_dma2", "norm_dma3", "rope_ready", "fhi_ready", "flo_ready",
                 "logit_ready", "max_ready", "maxes_ready", "mxrow_ready", "mxneg_ready", "mx_dma0", "mx_dma1",
                 "l_ready", "p_ready", "o_ready", "inv_l_ready", "ot_ready", "stored", "pos_loaded"]
        S = {n: sem(n) for n in names}
        h_loaded = [S[f"h_loaded{i}"] for i in range(4)]
        raw_full = [S[f"raw_full{i}"] for i in range(4)]
        mx_dma = [S["mx_dma0"], S["mx_dma1"]]
        item_dma = [S[f"item_dma{i}"] for i in range(4)]
        norm_dma = [S[f"norm_dma{i}"] for i in range(4)]

        def cm(i, rows_=P, width=P):
            return const[0:rows_, i * P:i * P + width]

        def col(name, j=0, rows_=P, p0=0):
            c = COLS[name][0] + j
            return cols[p0:p0 + rows_, c:c + 1]

        def two(ap):
            return ap.rearrange("p (b n) -> p b n", b=2)

        def slot_of(y):
            return 1 if Y_O <= y < Y_OUT0 else y % 2

        def slot(y, rows_=P, p0=0):
            return prod[p0:p0 + rows_, slot_of(y)].rearrange("p (b n) -> p b n", b=2)[:, :, 0:HALF]

        def slot_real(y):
            return prod[:, y % 2, 512:512 + SEQ]

        def aux_two(b, rows_=P):
            return aux[0:rows_, b * 512:(b + 2) * 512].rearrange("p (b n) -> p b n", b=2)[:, :, 0:HALF]

        def v_bank(j, base):
            return 0 if base == 8 else (j % 2) * 1024

        def max_bank(k):
            return (aux[:, 1024 + k % 2 * 512:1536 + k % 2 * 512] if k < HEADS * len(MAX_UNITS) else
                    prod[:, k % 2, 512:1024])

        def units(with_meta_queries):
            found, off = [], 0
            for j, (t0, rows_) in enumerate(BLOCKS):
                first = max(t0, N_META)
                found.append((j, first, T - first, off, t0 + rows_ - first))
                off += T - first
            if with_meta_queries:
                found.append((0, 0, N_META, off, N_META))
            return found

        def triangle(mask, j, first, n):
            at = first - BLOCKS[j][0]
            return mask[0:BLOCKS[j][1], at:at + n]

        N_OFF, N_DIAG = sum(n > diag for _, _, n, _, diag in units(True)), NB + 1

        def head_sums(e):
            real = prod[:, 0, e * 512:e * 512 + SEQ] if e < 2 else aux[:, 0:SEQ]
            return aux[:, 512 + e * N_META:512 + (e + 1) * N_META], real

        block = ctx.enter_context(nc.Block())

        @block.sync
        def _(sp):
            sp.dma_start(cols[:], cols_in).then_inc(S["cols_loaded"], 16)
            h_v = h_in.rearrange("(m p) t -> p m t", p=P)
            for m in range(0, KT, 2):
                sp.dma_start(h[:, m:m + 2], h_v[:, m:m + 2]).then_inc(h_loaded[m // 2], 16)
                if m == 0:
                    sp.dma_start(raw[:, 0], stream[0]).then_inc(raw_full[0], 16)
            sp.dma_start(raw[:, 1], stream[1]).then_inc(raw_full[1], 16)
            sp.dma_start(const[:], const_in).then_inc(S["const_loaded"], 16)
            sp.dma_start(raw[:, 2], stream[2]).then_inc(raw_full[2], 16)
            sp.dma_start(wr[:].rearrange("p (g n) -> p g n", n=P), gate_w.rearrange("g p n -> p g n")).then_inc(
                S["wr_loaded"], 16)
            sp.dma_start(raw[:, 3], stream[3]).then_inc(raw_full[3], 16)

            def load(first, iterations):
                with sp.Fori(0, iterations) as i:
                    row = sp.snap(i * 4 + first)
                    for j in range(4):
                        sp.wait_ge(S["w_lo_ready"], i * 4 + (first + j - 3))
                        sp.dma_start(raw[:, j], stream[bass.ds(row + j, 1)].rearrange("a p n -> p (a n)")).then_inc(
                            raw_full[j], 16)

            load(4, (S_END - 4) // 4)

        @block.gpsimd
        def _(pool):
            chain = [0]

            def link(ins):
                chain[0] += 1
                ins.then_inc(S["pool_chain"], 1)
                pool.wait_ge(S["pool_chain"], chain[0])

            def sum_squares(base, t0):
                for m in range(KT):
                    pool.wait_ge(S["sq_ready"], base + m + 1)
                    if m == 0:
                        nc.gpsimd.tensor_copy(sq_sum[:, t0:], sq[:, 0, t0:]).then_inc(S["sq_summed"], 1)
                    else:
                        pool.wait_ge(S["sq_summed"], base + m)
                        nc.gpsimd.tensor_tensor(sq_sum[:, t0:], sq_sum[:, t0:], sq[:, m % 2, t0:], ALU.add).then_inc(
                            S["sq_summed"], 1)

            nc.gpsimd.memset(xb[:, 0:3], 0.0).then_inc(S["zero_ready"], 1)
            sum_squares(0, 0)
            for g in range(KT + 1):
                if g:
                    j, b = g - 1, (g - 1) % 2
                    pool.wait_ge(S["sig_ready"], j + 1)
                    nc.gpsimd.tensor_tensor(gate_i[:, b], gate_i[:, b], xc[:, b], ALU.mult).then_inc(S["ix_ready"], 1)
                    pool.wait_ge(S["gsig_ready"], j + 1)
                    nc.gpsimd.tensor_tensor(gel[:, b], gel[:, b], gb[:, b], ALU.mult).then_inc(S["gelu_ready"], 1)
                if g < KT:
                    b = g % 2
                    pool.wait_ge(S["gsq_ready"], g + 1)
                    link(nc.gpsimd.tensor_scalar(gel[:, b], gel[:, b], 0.044715, 1.0, ALU.mult, ALU.add))
                    nc.gpsimd.tensor_tensor(gel[:, b], gel[:, b], gb[:, b], ALU.mult).then_inc(S["gz_ready"], 1)
            sum_squares(KT, 0)

            def mlp(y0, r0, t0, q, sq_base):
                for j in range(8):
                    pool.wait_ge(S["psum_free"], y0 + j + 1 + q * 16)
                    nc.gpsimd.tensor_tensor(tmp[:, j % 2, t0:], tmp[:, j % 2, t0:], tmp[:, j % 2, t0:],
                                            ALU.mult).then_inc(S["hid_ready"], 1)

            with pool.Fori(0, QUARTERS - 1) as q:
                mlp(Y_MLP0, 0, 0, q, None)
            mlp(Y_MLP0, 0, 0, QUARTERS - 1, None)
            sum_squares(2 * KT, 0)
            pool.wait_ge(S["stat_ready"], 3)
            nc.gpsimd.iota(g_pos[:, 0:N_META], pattern=[[1, N_META]], base=0, channel_multiplier=0).then_inc(
                S["trig_pos"], 1)
            for s in range(C_NORMS):
                if STEPS[s][0] == "value":
                    continue
                if s == KR_STEP:
                    pool.wait_ge(S["w_used"], S_FV + 4)
                group = 0 if s < KR_STEP else 1
                pool.wait_ge(S["item_done"], item_of(s) + 1)
                src = kr if s == KR_STEP else stg[:, s % 4]
                which, moves = item_moves(s)
                for hd, row, at, n in moves:
                    pool.dma_start((q_of if which == "q" else k_of)[group][row:row + n, hd].bitcast(F32), src[at:at + n]).then_inc(
                        item_dma[s % 4], 16)
            sum_squares(3 * KT, N_META)
            with pool.Fori(0, QUARTERS - 1) as q:
                mlp(Y_MLP1, 0, N_META, q, None)
            mlp(Y_MLP1, 0, N_META, QUARTERS - 1, None)

        @block.scalar
        def _(act):
            chain = [0]

            def link(ins):
                chain[0] += 1
                ins.then_inc(S["act_chain"], 1)
                act.wait_ge(S["act_chain"], chain[0])

            def split_weights(nb, i4=0):
                act.wait_ge(raw_full[nb % 4], 16 * (nb // 4 + 1) + i4 * 16)
                if nb >= 2:
                    act.wait_ge(S["w_used"], nb - 1 + i4 * 4)
                nc.scalar.activation(w_hi[:, nb % 2], raw[:, nb % 4], ACT.Copy).then_inc(S["w_hi_ready"], 1)

            def next_operand(m, base, gain, hi, t0):
                if base == 2 * KT:
                    act.wait_ge(S["h_ready"], m + 1)
                elif base:
                    act.wait_ge(S["psum_free"], {KT: Y_OUT0, 3 * KT: Y_OUT1}[base] + m + 1)
                nc.scalar.activation(hi[:, m, t0:], h[:, m, t0:], ACT.Copy, scale=col(gain, m)).then_inc(
                    S["a_hi_ready"], 1)
                if m >= 2:
                    act.wait_ge(S["sq_summed"], base + m - 1)
                nc.scalar.activation(sq[:, m % 2, t0:], h[:, m, t0:], ACT.Square).then_inc(S["sq_ready"], 1)

            def log_and_exp():
                nc.scalar.preload_act_table_set("natural_log_exp_and_others")

            def mean_square(k, power, t0=0):
                log_and_exp()
                act.wait_ge(S["stat_ready"], k + 1)
                if t0:
                    o, i = inv_ms[:, t0:], aux[:, 0:SEQ]
                else:
                    o, i = two(inv_ms[:]), aux_two(0)
                link(nc.scalar.activation(o, i, ACT.Ln, bias=col("eps"), scale=1.0 / D_MODEL))
                nc.scalar.activation(inv_ms[:, t0:], inv_ms[:, t0:], ACT.Exp, scale=power).then_inc(S["ms_ready"], 1)

            act.wait_ge(S["cols_loaded"], 16)
            lam = cols[:, COLS["lam"][0]:COLS["lam"][0] + KT]
            link(nc.scalar.activation(spt[:, 0], lam, ACT.Abs))
            nc.scalar.activation(spt[:, 0], spt[:, 0], ACT.Exp, scale=-1.0).then_inc(S["lam_e_ready"], 1)
            for m in range(KT):
                act.wait_ge(h_loaded[m // 2], 16)
                next_operand(m, 0, "ev_ln", a_hi, 0)
                if m in (0, 4):
                    split_weights(m // 4)
            mean_square(0, -0.5)

            def gates(j):
                b = j % 2
                act.wait_ge(S["gates_ready"], j + 1)
                if j == 0:
                    act.wait_ge(S["sp4_ready"], 1)
                else:
                    act.wait_ge(S["decay_ready"], j)
                if j >= 2:
                    act.wait_ge(S["hs_ready"], j - 1)
                nc.scalar.activation(two(gate_r[:]), aux_two(0), ACT.Sigmoid, bias=col("b_ra", j)).then_inc(
                    S["act_chain"], 1)
                chain[0] += 1
                nc.scalar.activation(two(gate_i[:, b]), aux_two(2), ACT.Sigmoid, bias=col("b_rx", j)).then_inc(
                    S["sig_ready"], 1)
                act.wait_ge(S["gz_ready"], j + 1)
                nc.scalar.activation(gel[:, b], gel[:, b], ACT.Sigmoid, scale=float(2.0 * np.sqrt(2.0 / np.pi))
                                     ).then_inc(S["gsig_ready"], 1)
                act.wait_ge(S["act_chain"], chain[0])
                nc.scalar.activation(sqrt_t[:, b], gate_r[:], ACT.Tanh, scale=sp4[:, j:j + 1]).then_inc(
                    S["tanh_ready"], 1)

            def decays(j):
                nc.scalar.activation(decay[:, j % 2], gate_r[:], ACT.Exp, scale=sp8[:, j:j + 1]).then_inc(
                    S["decay_ready"], 1)

            def root(j):
                act.wait_ge(S["tanh_ready"], j + 1)
                nc.scalar.activation(sqrt_t[:, j % 2], sqrt_t[:, j % 2], ACT.Sqrt).then_inc(S["sqrt_ready"], 1)

            def hb_high(j):
                act.wait_ge(S["hb_ready"], j + 1)
                nc.scalar.activation(b_hi[:, j], hs[:, j % 2], ACT.Copy).then_inc(S["split_hi"], 1)

            for g in range(KT):
                split_weights(2 * g + 2)
                act.wait_ge(S["psum_free"], 2 * g + 1)
                if g == 0:
                    act.wait_ge(S["zero_ready"], 1)
                if g >= 2:
                    act.wait_ge(S["ix_ready"], g - 1)
                nc.scalar.activation(xc[:, g % 2], xb[:, 0:T], ACT.Identity, bias=col("conv_b", g),
                                     scale=col("conv_w", g)).then_inc(S["conv0_ready"], 1)
                if g >= 2:
                    hb_high(g - 2)
                if g:
                    gates(g - 1)
                    decays(g - 1)
                split_weights(2 * g + 3)
                if g:
                    root(g - 1)
                act.wait_ge(S["psum_free"], 2 * g + 2)
                if g >= 2:
                    act.wait_ge(S["hb_ready"], g - 1)
                nc.scalar.activation(gel[:, g % 2], gb[:, g % 2], ACT.Square).then_inc(S["gsq_ready"], 1)
            split_weights(S_GATES + 2)
            hb_high(KT - 2)
            gates(KT - 1)
            split_weights(S_QK + 2)
            decays(KT - 1)
            root(KT - 1)
            act.wait_ge(S["const_loaded"], 16)
            nc.scalar.activation(ident_bf[:], cm(C_IDENT), ACT.Copy).then_inc(S["bf_ready"], 1)
            nc.scalar.activation(mask_st_bf[:], cm(C_MASK_ST), ACT.Copy).then_inc(S["bf_ready"], 1)
            nc.scalar.activation(mask_ts_bf[:], cm(C_MASK_TS), ACT.Copy).then_inc(S["bf_ready"], 1)
            log_and_exp()
            act.wait_ge(S["gf_ready"], 1)
            link(nc.scalar.activation(g_l[0:A_HEADS], g_f[0:A_HEADS], ACT.Abs, bias=col("b_f", 0, A_HEADS)))
            link(nc.scalar.activation(g_l[0:A_HEADS], g_l[0:A_HEADS], ACT.Exp, scale=-1.0))
            nc.scalar.activation(g_l[0:A_HEADS], g_l[0:A_HEADS], ACT.Ln, bias=1.0).then_inc(S["gl_ready"], 1)
            hb_high(KT - 1)
            for j in range(1, 8):
                split_weights(S_QK + 2 + j)

            def copy_v(j, dst_last, dst_full, base, pairs=False):
                act.wait_ge(S["vt_ready"], base + j + 1)
                a = v_bank(j, base)
                src = aux[0:BLOCKS[-1][1], a:a + P]
                nc.scalar.activation(dst_last, src if not pairs else src.rearrange("p (c n) -> p c n", c=2), ACT.Copy)
                src = aux[:, a + 512:a + 1024].rearrange("p (b n) -> p b n", b=4)
                if pairs:
                    for b in range(4):
                        last = nc.scalar.activation(dst_full[:, b], src[:, b].rearrange("p (c n) -> p c n", c=2),
                                                    ACT.Copy)
                else:
                    last = nc.scalar.activation(dst_full, src, ACT.Copy)
                last.then_inc(S["v_copied"], 1)

            mu = units(True)

            def offsets(hd):
                b = hd % 2
                act.wait_ge(S["bc_ready"], 2 * hd + 1)
                nc.scalar.activation(two(abc[:, b]), aux_two(2), ACT.Copy).then_inc(S["abc_ready"], 1)

            def off_diagonal(hd):
                b = hd % 2
                act.wait_ge(S["abc_ready"], hd + 1)
                if hd == 0:
                    act.wait_ge(S["ccol_ready"], 1)
                for j, t0, n, off, diag in mu:
                    rows_ = BLOCKS[j][1]
                    if n > diag:
                        nc.scalar.activation(expw[0:rows_, b, off + diag:off + n], abc[0:rows_, b, t0 + diag:t0 + n],
                                             ACT.Exp, bias=ccol[0:rows_, j * A_HEADS + hd:j * A_HEADS + hd + 1]
                                             ).then_inc(S["expw_ready"], 1)

            def diagonal(hd):
                b = hd % 2
                act.wait_ge(S["bc_ready"], 2 * hd + 2)
                nc.scalar.activation(two(em[:, b]), aux_two(2), ACT.Exp).then_inc(S["em_ready"], 1)
                act.wait_ge(S["diag_ready"], (hd + 1) * N_DIAG)
                for j, t0, n, off, diag in mu:
                    if diag:
                        x = expw[0:BLOCKS[j][1], b, off:off + diag]
                        nc.scalar.activation(x, x, ACT.Exp).then_inc(S["expd_ready"], 1)

            for j in range(8):
                split_weights(S_V + 2 + j)
                if j:
                    copy_v(j - 1, v[0:BLOCKS[-1][1], NB - 1, (j - 1) * P:j * P], v[:, 0:NB - 1, (j - 1) * P:j * P], 0)
                if j == 0:
                    act.wait_ge(S["ccol_psum"], 1)
                    nc.scalar.activation(ccol[:], aux[:, 0:NB * A_HEADS], ACT.Copy).then_inc(S["ccol_ready"], 1)
                    offsets(0)
                    off_diagonal(0)
                elif j == 1:
                    diagonal(0)
            copy_v(7, v[0:BLOCKS[-1][1], NB - 1, 7 * P:8 * P], v[:, 0:NB - 1, 7 * P:8 * P], 0)

            for hd in range(A_HEADS):
                b = hd % 2
                if hd + 1 < A_HEADS:
                    offsets(hd + 1)
                act.wait_ge(S["acc_ready"], hd + 1)
                meta, real = head_sums(2)
                nc.scalar.activation(abc[:, b, 0:N_META], meta, ACT.Abs)
                nc.scalar.activation(abc[:, b, N_META:], real, ACT.Abs).then_inc(S["absden_ready"], 1)
                act.wait_ge(S["den_ready"], hd + 1)
                link(nc.scalar.activation(abc[:, b], abc[:, b], ACT.Ln))
                nc.scalar.activation(abc[:, b], abc[:, b], ACT.Exp, scale=-1.0).then_inc(S["rden_ready"], 1)
                if hd + 1 < A_HEADS:
                    off_diagonal(hd + 1)
                for e in range(2):
                    act.wait_ge(S["hn_ready"], 2 * hd + e + 1)
                    nc.scalar.activation(st[:, e * T:(e + 1) * T], qk[:, hd + e * A_HEADS], ACT.Square).then_inc(
                        S["hnsq_ready"], 1)
                split_weights(S_O + 2 + 2 * hd)
                if hd + 1 < A_HEADS:
                    diagonal(hd + 1)
                for e in range(2):
                    act.wait_ge(S["psum_free"], Y_O + 2 * hd + e + 1)
                    nc.scalar.activation(tmp[:, e], tmp[:, e], ACT.Sigmoid).then_inc(S["osig_ready"], 1)
                log_and_exp()
                act.wait_ge(S["hstat_ready"], hd + 1)
                if hd:
                    act.wait_ge(S["head_done"], hd)
                nc.scalar.activation(two(rs_a[:]), aux_two(0), ACT.Ln, bias=col("eps"), scale=1.0 / A_DV).then_inc(
                    S["hms_ready"], 1)
                act.wait_ge(S["hms_ready"], hd + 1)
                nc.scalar.activation(rs_a[:], rs_a[:], ACT.Exp, scale=-0.5).then_inc(S["hrs_ready"], 1)
                split_weights(S_O + 3 + 2 * hd)
            split_weights(S_OUT0 + 2)
            act.wait_ge(S["head_done"], A_HEADS)
            for j in range(8):
                nc.scalar.activation(c_hi[:, j], qk[:, j // 2 + (j % 2) * A_HEADS], ACT.Copy).then_inc(
                    S["split_hi"], 1)
            for m in range(KT):
                if m:
                    split_weights(S_OUT0 + 2 + 2 * m)
                split_weights(S_OUT0 + 3 + 2 * m)
                next_operand(m, KT, "mlp_ln0", a_hi, 0)
            mean_square(1, -1.0)

            def mlp(s0, y0, hid, t0, q, last_quarter=None):
                for j in range(8):
                    if s0 + j + 2 < S_END:
                        split_weights(s0 + 2 + j, q * 4)
                    act.wait_ge(S["hid_ready"], hid + j + 1 + q * 8)
                    nc.scalar.activation(b_hi[:, j, t0:], tmp[:, j % 2, t0:], ACT.Copy).then_inc(S["split_hi"], 1)
                for j in range(8):
                    if not (last_quarter == 1 and s0 + 8 + j + 2 + 16 * q >= S_END):
                        split_weights(s0 + 10 + j, q * 4)
                    if last_quarter == 0:
                        next_operand(j, 2 * KT, "od_ln", a_hi, 0)

            with act.Fori(0, QUARTERS - 1) as q:
                mlp(S_MLP0, Y_MLP0, 0, 0, q)
            mlp(S_MLP0, Y_MLP0, 0, 0, QUARTERS - 1, 0)
            mean_square(2, -0.5)

            act.dma_start(g_pos[:, N_META:], positions.to_broadcast([P, SEQ])).then_inc(S["pos_loaded"], 16)
            for j in range(5):
                split_weights(S_LORA + 2 + j)
                act.wait_ge(S["psum_free"], Y_LORA + j + 1)
                nc.scalar.activation(lora_sq[:, j], lora[:, j], ACT.Square).then_inc(S["lsq_ready"], 1)
            split_weights(S_KRFF + 2)
            act.wait_ge(S["fgf_ready"], 1)
            link(nc.scalar.activation(o_l, o_f, ACT.Abs, bias=col("od_b_f", 0, HEADS)))
            link(nc.scalar.activation(o_l, o_l, ACT.Exp, scale=-1.0))
            nc.scalar.activation(o_l, o_l, ACT.Ln, bias=1.0).then_inc(S["fgl_ready"], 1)
            split_weights(S_FQK + 2)
            for k, width in enumerate((Q_LORA, KV_LORA)):
                act.wait_ge(S["lstat_ready"], k + 1)
                nc.scalar.activation(two(lora_rs[k]), aux_two(2 * k), ACT.Ln, bias=col("eps"),
                                     scale=1.0 / width).then_inc(S["lms_ready"], 1)
                act.wait_ge(S["lms_ready"], k + 1)
                nc.scalar.activation(lora_rs[k], lora_rs[k], ACT.Exp, scale=-0.5).then_inc(S["lrs_ready"], 1)

            def copy_pair(j, base):
                v3 = vp[:, :, j].rearrange("p b (c n) -> p b c n", c=3)
                copy_v(j, v3[0:BLOCKS[-1][1], NB - 1, 0:3:2], v3[:, 0:NB - 1, 0:3:2], base, True)

            def item_squares(s):
                kind, y, rows_, _, _, _ = STEPS[s]
                k = item_of(s)
                if s < C_NORMS:
                    act.wait_ge(S["psum_free"], (Y_KRFF if y is None else y) + 1)
                if k >= 2:
                    before = max(i for i in range(s) if item_of(i) == k - 2)
                    if STEPS[before][0] == "rope":
                        act.wait_ge(S["rope_ready"], rope_of(before) + 1)
                    else:
                        act.wait_ge(S["item_done"], k - 1)
                if s < C_NORMS:
                    nc.scalar.activation(tmp[0:rows_, k % 2], kr[:] if y is None else stg[0:rows_, s % 4],
                                         ACT.Square).then_inc(S["item_sq"], 1)
                    return
                sem_, count = product_end(y)
                act.wait_ge(S[sem_], count)
                act.wait_ge(S["psum_free"], y)
                nc.scalar.activation(two(tmp[:, k % 2]), slot(y), ACT.Square).then_inc(S["item_sq"], 1)
                if s - 4 >= C_NORMS:
                    act.wait_ge(norm_dma[s % 4], 32 * ((s - 4 - C_NORMS) // 4 + 1))
                elif STEPS[s - 4][0] == "value":
                    act.wait_ge(S["vt_ready"], 8 + s - 4 - V_STEP + 1)
                else:
                    act.wait_ge(item_dma[s % 4], slot_moves(s, s % 4))
                nc.scalar.activation(two(stg[:, s % 4]), slot(y), ACT.Copy).then_inc(S["psum_free"], 1)

            def item_factor(s):
                _, _, rows_, _, _, inv = STEPS[s]
                k = item_of(s)
                act.wait_ge(S["item_stat"], k + 1)
                nc.scalar.activation(two(tmp[0:rows_, k % 2]), aux_two(0, rows_), ACT.Ln,
                                     bias=col("eps", {1: 0, HD: 1, C_NOPE + C_ROPE: 2}[inv], rows_),
                                     scale=float(inv)).then_inc(S["item_ms"], 1)
                act.wait_ge(S["item_ms"], k + 1)
                nc.scalar.activation(tmp[0:rows_, k % 2], tmp[0:rows_, k % 2], ACT.Exp, scale=-0.5).then_inc(
                    S["item_rs"], 1)

            def move_norm(s):
                which, moves = item_moves(s)
                act.wait_ge(S["item_done"], item_of(s) + 1)
                for hd, row, at, n in moves:
                    act.dma_start((q_of if which == "q" else k_of)[1][row:row + n, hd].bitcast(F32),
                                  stg[at:at + n, s % 4]).then_inc(norm_dma[s % 4], 16)

            for s in range(N_STEPS + 2):
                if 0 < s < D_STEPS and s != KR_STEP:
                    split_weights(tile_of(s) + 2)
                elif D_STEPS <= s < N_STEPS:
                    sem_, tile = product_end(STEPS[s][1])
                    if sem_ == "w_used":
                        split_weights(tile + 1)
                if 1 <= s <= 5:
                    act.wait_ge(S["ln_ready"], s)
                    nc.scalar.activation(b_hi[:, s - 1], lora[:, s - 1], ACT.Copy).then_inc(S["split_hi"], 1)
                if s < N_STEPS and STEPS[s][0] != "value":
                    item_squares(s)
                if s and s <= N_STEPS and STEPS[s - 1][0] != "value":
                    item_factor(s - 1)
                elif s and s <= N_STEPS:
                    copy_pair(s - 1 - V_STEP, 8)
                if s - 2 >= C_NORMS:
                    move_norm(s - 2)
                if s == 1:
                    act.wait_ge(S["fF_ready"], 1)
                    nc.scalar.activation(o_hi, g_F, ACT.Copy).then_inc(S["fhi_ready"], 1)
                if s == 2:
                    act.wait_ge(S["fhi_ready"], 1)
                    act.wait_ge(S["flo_ready"], 1)
                    for part, row in enumerate((o_hi.bitcast(F32), o_l)):
                        act.dma_start(k_aug[HD + part:HD + part + 1].bitcast(F32), row).then_inc(S["augF"], 16)
                if s == KR_STEP + 1:
                    for k in range(2):
                        act.wait_ge(S["trig_arg"], k + 1)
                        nc.scalar.activation(sq[:, k], sq[:, k], ACT.Sin).then_inc(S["trig_ready"], 1)
                    log_and_exp()

            au = units(False)

            def max_row(group, row):
                act.wait_ge(S["mxrow_ready"], group + 1)
                nc.scalar.activation(neg_max[group], aux[0:HEADS, 0:SEQ], ACT.Copy, scale=-1.0).then_inc(
                    S["mxneg_ready"], 1)
                act.wait_ge(S["mxneg_ready"], group + 1)
                act.dma_start(q_of[group][row:row + 1, :, N_META:].bitcast(F32),
                              neg_max[group]).then_inc(mx_dma[group], 16)

            def inverse_sum(gh):
                lo_, hi_ = (0, HD) if gh % 2 == 0 else (HD, 0)
                x = stg[lo_:lo_ + HD, 0, 0:SEQ]
                act.wait_ge(S["o_ready"], gh + 1)
                link(nc.scalar.activation(x, prod[hi_:hi_ + HD, gh % 2, 0:SEQ], ACT.Ln))
                nc.scalar.activation(x, x, ACT.Exp, scale=-1.0).then_inc(S["inv_l_ready"], 1)

            def attend(group):
                for hd in range(HEADS):
                    gh = group * HEADS + hd
                    if hd % 2 == 1 and hd > 1:
                        pair_hi(group, hd // 2 - 1)
                    if hd >= 2:
                        act.wait_ge(S["o_ready"], gh - 1)
                    for u, (j, t0, n, off, _) in enumerate(au):
                        act.wait_ge(S["l_ready"], gh * NB + u + 1)
                        bank = (gh * NB + u) % 4
                        nc.scalar.activation(pt[0:BLOCKS[j][1], hd % 2, off:off + n],
                                             aux[0:BLOCKS[j][1], bank * 512:bank * 512 + n], ACT.Exp).then_inc(
                            S["p_ready"], 1)
                    if hd:
                        inverse_sum(gh - 1)
                inverse_sum(group * HEADS + HEADS - 1)
                if group == 0:
                    max_row(1, C_NOPE + C_ROPE)
                    for j in range(4):
                        copy_pair(j, 12)
                pair_hi(group, 3)

            def pair_hi(group, pair):
                k = group * 4 + pair
                act.wait_ge(S["ot_ready"], 2 * k + 2)
                nc.scalar.activation(b_hi[:, out_tile(group, pair), N_META:], tmp[:, pair % 2, 0:SEQ],
                                     ACT.Copy).then_inc(S["split_hi"], 1)

            max_row(0, HD + 2)
            split_weights(S_UV + 2)
            attend(0)
            attend(1)

            for m in range(KT):
                split_weights(S_OUT1 + 2 + m)
                next_operand(m, 3 * KT, "mlp_ln1", a_hi, N_META)
            mean_square(3, -1.0, N_META)
            with act.Fori(0, QUARTERS - 1) as q:
                mlp(S_MLP1, Y_MLP1, 32, N_META, q)
            mlp(S_MLP1, Y_MLP1, 32, N_META, QUARTERS - 1, 1)
            out_v = out.rearrange("(m p) t -> p m t", p=P)
            for m in range(KT):
                act.wait_ge(S["h_ready"], KT + m + 1)
                act.dma_start(out_v[:, m], h[:, m, N_META:]).then_inc(S["stored"], 16)
            act.wait_ge(S["stored"], 16 * KT)

        @block.vector
        def _(dve):
            chain = [0]

            def link(ins):
                chain[0] += 1
                ins.then_inc(S["dve_chain"], 1)
                dve.wait_ge(S["dve_chain"], chain[0])

            def split_weights(nb, i4=0):
                dve.wait_ge(S["w_hi_ready"], nb + 1 + i4 * 4)
                nc.vector.tensor_tensor(w_lo[:, nb % 2], raw[:, nb % 4], w_hi[:, nb % 2].bitcast(F32),
                                        ALU.subtract).then_inc(S["w_lo_ready"], 1)

            def next_operand(m, base, gain, hi, lo, t0):
                dve.wait_ge(S["a_hi_ready"], base + m + 1)
                nc.vector.scalar_tensor_tensor(out=lo[:, m, t0:], in0=h[:, m, t0:], scalar=col(gain, m),
                                               in1=hi[:, m, t0:].bitcast(F32), op0=ALU.mult,
                                               op1=ALU.subtract).then_inc(S["operand_ready"], 1)

            def split_low(lo, hi, full, hi_count):
                dve.wait_ge(S["split_hi"], hi_count)
                nc.vector.tensor_tensor(lo, full, hi.bitcast(F32), ALU.subtract).then_inc(S["operand_ready"], 1)

            dve.wait_ge(S["lam_e_ready"], 1)
            lam = cols[:, COLS["lam"][0]:COLS["lam"][0] + KT]
            link(nc.vector.tensor_scalar(spt[:, 1], spt[:, 0], 2.0, None, ALU.add))
            link(nc.vector.reciprocal(spt[:, 1], spt[:, 1]))
            link(nc.vector.tensor_tensor(spt[:, 1], spt[:, 0], spt[:, 1], ALU.mult))
            link(nc.vector.tensor_tensor(spt[:, 2], spt[:, 1], spt[:, 1], ALU.mult))
            link(nc.vector.tensor_scalar(spt[:, 3], spt[:, 2], 1.0 / 15, None, ALU.mult))
            for k in (13, 11, 9, 7, 5, 3):
                link(nc.vector.scalar_tensor_tensor(out=spt[:, 3], in0=spt[:, 3], scalar=1.0 / k, in1=spt[:, 2],
                                                    op0=ALU.add, op1=ALU.mult))
            link(nc.vector.scalar_tensor_tensor(out=spt[:, 3], in0=spt[:, 3], scalar=1.0, in1=spt[:, 1],
                                                op0=ALU.add, op1=ALU.mult))
            link(nc.vector.tensor_scalar(spt[:, 4], lam, -1.0, 0.0, ALU.mult, ALU.max))
            link(nc.vector.scalar_tensor_tensor(out=spt[:, 3], in0=spt[:, 3], scalar=2.0, in1=spt[:, 4],
                                                op0=ALU.mult, op1=ALU.add))
            nc.vector.tensor_scalar(sp8[:], spt[:, 3], -8.0, None, ALU.mult)
            nc.vector.tensor_scalar(sp4[:], spt[:, 3], 4.0, None, ALU.mult).then_inc(S["sp4_ready"], 1)

            for m in range(KT):
                dve.wait_ge(h_loaded[m // 2], 16)
                next_operand(m, 0, "ev_ln", a_hi, a_lo, 0)
                if m in (0, 4):
                    split_weights(m // 4)
            dve.wait_ge(S["ms_ready"], 1)

            def recurrence(j):
                b = j % 2
                dve.wait_ge(S["decay_ready"], j + 1)
                dve.wait_ge(S["sqrt_ready"], j + 1)
                link(nc.vector.scalar_tensor_tensor(out=sqrt_t[:, b], in0=decay[:, b], scalar=1.0, in1=sqrt_t[:, b],
                                                    op0=ALU.add, op1=ALU.mult))
                dve.wait_ge(S["ix_ready"], j + 1)
                nc.vector.tensor_tensor(gate_i[:, b], gate_i[:, b], sqrt_t[:, b], ALU.mult).then_inc(S["u_ready"], 1)
                if j >= 2:
                    dve.wait_ge(S["operand_ready"], R_HB + j - 1)
                dve.wait_ge(S["u_ready"], j + 1)
                nc.vector.tensor_tensor_scan(hs[:, b], decay[:, b], gate_i[:, b], 0.0, ALU.mult, ALU.add).then_inc(
                    S["hs_ready"], 1)
                dve.wait_ge(S["gelu_ready"], j + 1)
                dve.wait_ge(S["hs_ready"], j + 1)
                nc.vector.tensor_tensor(hs[:, b], hs[:, b], gel[:, b], ALU.mult).then_inc(S["hb_ready"], 1)

            def hb_low(j):
                split_low(b_lo[:, j], b_hi[:, j], hs[:, j % 2], j + 1)

            for g in range(KT):
                b = g % 2
                dve.wait_ge(S["w_used"], 2 * g + 1)
                if g:
                    dve.wait_ge(S["xc_ready"], g)
                nc.vector.tensor_tensor(two(xb[:, 3:T + 3]), slot(2 * g), two(rstd[:]), ALU.mult).then_inc(
                    S["psum_free"], 1)
                split_weights(2 * g + 2)
                dve.wait_ge(S["conv0_ready"], g + 1)
                for j in (1, 2):
                    link(nc.vector.scalar_tensor_tensor(out=xc[:, b], in0=xb[:, j:j + T],
                                                        scalar=col("conv_w", j * KT + g), in1=xc[:, b], op0=ALU.mult,
                                                        op1=ALU.add))
                nc.vector.scalar_tensor_tensor(out=xc[:, b], in0=xb[:, 3:3 + T], scalar=col("conv_w", 3 * KT + g),
                                               in1=xc[:, b], op0=ALU.mult, op1=ALU.add).then_inc(S["xc_ready"], 1)
                if g >= 2:
                    hb_low(g - 2)
                dve.wait_ge(S["w_used"], 2 * g + 2)
                if g >= 2:
                    dve.wait_ge(S["gelu_ready"], g - 1)
                nc.vector.tensor_tensor(two(gb[:, b]), slot(2 * g + 1), two(rstd[:]), ALU.mult).then_inc(
                    S["psum_free"], 1)
                split_weights(2 * g + 3)
                if g:
                    recurrence(g - 1)

            dve.wait_ge(S["w_used"], S_GATES + 1)
            link(nc.vector.tensor_tensor(two(g_i[0:A_HEADS]), slot(Y_GATES, A_HEADS), two(rstd[0:A_HEADS]), ALU.mult))
            nc.vector.tensor_tensor(two(g_f[0:A_HEADS]), slot(Y_GATES, A_HEADS, 32), two(rstd[32:32 + A_HEADS]),
                                    ALU.mult).then_inc(S["psum_free"], 1)
            split_weights(S_GATES + 2)
            dve.wait_ge(S["psum_free"], Y_GATES + 1)
            nc.vector.memset(g_m[0:A_HEADS], 0.0).then_inc(S["gf_ready"], 1)
            hb_low(KT - 2)

            def gate_rows():
                r = slice(0, A_HEADS)
                link(nc.vector.tensor_scalar(g_i[r], g_i[r], col("b_i", 0, A_HEADS), None, ALU.add))
                dve.wait_ge(S["gl_ready"], 1)
                link(nc.vector.tensor_scalar(g_f[r], g_f[r], col("b_f", 0, A_HEADS), 0.0, ALU.add, ALU.min))
                link(nc.vector.tensor_tensor(g_l[r], g_f[r], g_l[r], ALU.subtract))
                link(nc.vector.tensor_tensor_scan(g_F[r], g_l[r], g_m[r], 0.0, ALU.add, ALU.add))
                link(nc.vector.tensor_tensor_scan(g_m[r], g_l[r], g_i[r], 0.0, ALU.add, ALU.max))
                link(nc.vector.tensor_tensor(g_i[r], g_i[r], g_F[r], ALU.subtract))
                link(nc.vector.tensor_tensor(g_F[r], g_F[r], g_m[r], ALU.subtract))
                nc.vector.tensor_scalar(g_m[r], g_m[r], -1.0, None, ALU.mult).then_inc(S["rows_ready"], 1)

            for j in range(8):
                dve.wait_ge(S["w_used"], S_QK + j + 1)
                nc.vector.tensor_tensor(two(qk[:, j]), slot(Y_QK + j), two(rstd[:]), ALU.mult).then_inc(
                    S["psum_free"], 1)
                split_weights(S_QK + 2 + j)
                if j == 0:
                    recurrence(KT - 1)
                elif j == 1:
                    hb_low(KT - 1)
                elif j == 2:
                    gate_rows()
            mu = units(True)

            def diagonal(hd):
                b = hd % 2
                dve.wait_ge(S["abc_ready"], hd + 1)
                if hd == 0:
                    dve.wait_ge(S["ccol_ready"], 1)
                    dve.wait_ge(S["const_loaded"], 16)
                for j, t0, n, off, diag in mu:
                    if diag:
                        rows_ = BLOCKS[j][1]
                        nc.vector.scalar_tensor_tensor(
                            out=expw[0:rows_, b, off:off + diag], in0=abc[0:rows_, b, t0:t0 + diag],
                            scalar=ccol[0:rows_, j * A_HEADS + hd:j * A_HEADS + hd + 1],
                            in1=triangle(cm(C_MASK_ST), j, t0, diag), op0=ALU.add, op1=ALU.add).then_inc(S["diag_ready"], 1)

            for j in range(8):
                dve.wait_ge(S["w_used"], S_V + j + 1)
                if j >= 2:
                    dve.wait_ge(S["vt_ready"], j - 1)
                nc.vector.tensor_tensor(two(tmp[:, j % 2]), slot(Y_V + j), two(rstd[:]), ALU.mult).then_inc(
                    S["psum_free"], 1)
                split_weights(S_V + 2 + j)
                if j == 0:
                    diagonal(0)

            def norm_head(hd):
                dve.wait_ge(S["hrs_ready"], hd + 1)
                for e in range(2):
                    x = qk[:, hd + e * A_HEADS]
                    nc.vector.scalar_tensor_tensor(out=x, in0=x, scalar=col("a_norm", e), in1=rs_a[:], op0=ALU.mult,
                                                   op1=ALU.mult).then_inc(S["ha_ready"], 1)

            def gate_head(hd):
                dve.wait_ge(S["osig_ready"], 2 * hd + 2)
                dve.wait_ge(S["ha_ready"], 2 * hd + 2)
                for e in range(2):
                    x = qk[:, hd + e * A_HEADS]
                    last = nc.vector.tensor_tensor(x, x, tmp[:, e], ALU.mult)
                last.then_inc(S["head_done"], 1)

            for hd in range(A_HEADS):
                b = hd % 2
                for u, (j, t0, n, off, diag) in enumerate(mu):
                    rows_ = BLOCKS[j][1]
                    if u == 0:
                        dve.wait_ge(S["expw_ready"], (hd + 1) * N_OFF)
                        dve.wait_ge(S["expd_ready"], (hd + 1) * N_DIAG)
                    dve.wait_ge(S["s_ready"], hd * len(mu) + u + 1)
                    bank = 2 + u % 2
                    nc.vector.scalar_tensor_tensor(
                        out=st[0:rows_, off:off + n], in0=aux[0:rows_, bank * 512:bank * 512 + n],
                        scalar=float(A_DQK) ** -0.5, in1=expw[0:rows_, b, off:off + n], op0=ALU.mult,
                        op1=ALU.mult).then_inc(S["st_ready"], 1)
                    if hd and u == 1:
                        norm_head(hd - 1)
                    if hd and u == 2:
                        gate_head(hd - 1)
                if hd:
                    split_weights(S_O + 1 + 2 * hd)
                dve.wait_ge(S["absden_ready"], hd + 1)
                nc.vector.tensor_tensor(abc[:, b], abc[:, b], em[:, b], ALU.max).then_inc(S["den_ready"], 1)
                dve.wait_ge(S["rden_ready"], hd + 1)
                for e in range(2):
                    meta, real = head_sums(e)
                    x = qk[:, hd + e * A_HEADS]
                    nc.vector.tensor_tensor(x[:, 0:N_META], meta, abc[:, b, 0:N_META], ALU.mult)
                    nc.vector.tensor_tensor(x[:, N_META:], real, abc[:, b, N_META:], ALU.mult).then_inc(
                        S["hn_ready"], 1)
                for e in range(2):
                    j = 2 * hd + e
                    dve.wait_ge(S["w_used"], S_O + j + 1)
                    if hd:
                        dve.wait_ge(S["head_done"], hd)
                    nc.vector.tensor_tensor(two(tmp[:, e]), slot(Y_O + j), two(rstd[:]), ALU.mult).then_inc(
                        S["psum_free"], 1)
                    if e == 0:
                        split_weights(S_O + 2 + j)
                        if hd + 1 < A_HEADS:
                            diagonal(hd + 1)
            split_weights(S_O + 9)
            norm_head(A_HEADS - 1)
            gate_head(A_HEADS - 1)
            split_weights(S_OUT0 + 2)
            for j in range(8):
                split_low(c_lo[:, j], c_hi[:, j], qk[:, j // 2 + (j % 2) * A_HEADS], KT + j + 1)

            for m in range(KT):
                if m:
                    split_weights(S_OUT0 + 2 + 2 * m)
                if m == 0:
                    split_weights(S_OUT0 + 3)
                dve.wait_ge(S["w_used"], out0_tile(m, 1) + 1)
                nc.vector.tensor_tensor(two(h[:, m]), slot(Y_OUT0 + m), two(h[:, m]), ALU.add).then_inc(
                    S["psum_free"], 1)
                if m:
                    split_weights(S_OUT0 + 3 + 2 * m)
                next_operand(m, KT, "mlp_ln0", a_hi, a_lo, 0)
            dve.wait_ge(S["ms_ready"], 2)

            def mlp(s0, y0, hi0, t0, q, layer, last=False):
                real = t0 > 0
                for j in range(8):
                    y = y0 + j
                    dve.wait_ge(S["w_used"], s0 + j + 1 + q * 16)
                    if real:
                        o, i = tmp[:, j % 2, t0:], slot_real(y)
                    else:
                        o, i = two(tmp[:, j % 2]), slot(y)
                    nc.vector.tensor_scalar(o, i, 0.0, None, ALU.max).then_inc(S["psum_free"], 1)
                    split_weights(s0 + 2 + j, q * 4)
                    dve.wait_ge(S["split_hi"], hi0 + j + 1 + q * 8)
                    nc.vector.tensor_tensor(b_lo[:, j, t0:], tmp[:, j % 2, t0:], b_hi[:, j, t0:].bitcast(F32),
                                            ALU.subtract).then_inc(S["operand_ready"], 1)
                for j in range(8):
                    y = y0 + 8 + j
                    dve.wait_ge(S["w_used"], s0 + 8 + j + 1 + q * 16)
                    if real:
                        o, i, f = tmp[:, j % 2, t0:], slot_real(y), inv_ms[:, t0:]
                    else:
                        o, i, f = two(tmp[:, j % 2]), slot(y), two(inv_ms[:])
                    nc.vector.tensor_tensor(o, i, f, ALU.mult).then_inc(S["psum_free"], 1)
                    if not (last and layer == 1 and j >= 6):
                        split_weights(s0 + 10 + j, q * 4)
                    dve.wait_ge(S["psum_free"], y + 1 + q * 16)
                    add = nc.vector.tensor_tensor(h[:, j, t0:], h[:, j, t0:], tmp[:, j % 2, t0:], ALU.add)
                    if last:
                        add.then_inc(S["h_ready"], 1)
                        if layer == 0:
                            next_operand(j, 2 * KT, "od_ln", a_hi, a_lo, 0)

            with dve.Fori(0, QUARTERS - 1) as q:
                mlp(S_MLP0, Y_MLP0, 2 * KT, 0, q, 0)
            mlp(S_MLP0, Y_MLP0, 2 * KT, 0, QUARTERS - 1, 0, True)
            HI = 2 * KT + KT * QUARTERS

            dve.wait_ge(S["ms_ready"], 3)
            for j in range(5):
                dve.wait_ge(S["w_used"], S_LORA + j + 1)
                nc.vector.tensor_tensor(two(lora[:, j]), slot(Y_LORA + j), two(rstd[:]), ALU.mult).then_inc(
                    S["psum_free"], 1)
                split_weights(S_LORA + 2 + j)
            dve.wait_ge(S["w_used"], S_KRFF + 1)
            link(nc.vector.tensor_tensor(two(kr[:]), slot(Y_KRFF, C_ROPE), two(rstd[0:C_ROPE]), ALU.mult))
            nc.vector.tensor_tensor(two(o_f), slot(Y_KRFF, HEADS, 32), two(rstd[32:32 + HEADS]),
                                    ALU.mult).then_inc(S["psum_free"], 1)
            dve.wait_ge(S["psum_free"], Y_KRFF + 1)
            nc.vector.memset(o_zero, 0.0).then_inc(S["fgf_ready"], 1)
            split_weights(S_KRFF + 2)
            link(nc.vector.memset(q_aug[HD:HD + 2].bitcast(F32), 1.0))
            nc.vector.memset(k_aug[HD:HD + 3].bitcast(F32), 1.0).then_inc(S["aug_one"], 1)
            dve.wait_ge(S["aug_one"], 1)

            def evacuate(s):
                kind, y, _, _, _, _ = STEPS[s]
                sem_, count = ("w_used", tile_of(s) + 1) if s < D_STEPS else product_end(y)
                if s >= C_NORMS:
                    if sem_ == "w_used":
                        split_weights(count + 1)
                    return
                dve.wait_ge(S[sem_], count)
                if s == 3:
                    dve.wait_ge(S["augF"], 32)
                if s >= 4 and STEPS[s - 4][0] == "value":
                    dve.wait_ge(S["vt_ready"], 8 + s - 4 - V_STEP + 1)
                elif s >= 4 and s - 4 != KR_STEP:
                    dve.wait_ge(item_dma[s % 4], slot_moves(s, s % 4))
                if s < D_STEPS:
                    ins = nc.vector.tensor_tensor(two(stg[:, s % 4]), slot(y), two(rstd[:]), ALU.mult)
                else:
                    ins = nc.vector.tensor_copy(two(stg[:, s % 4]), slot(y))
                ins.then_inc(S["psum_free"], 1)
                if s < D_STEPS:
                    split_weights(tile_of(s) + 2)
                elif sem_ == "w_used":
                    split_weights(count + 1)

            def normalise(s):
                kind, _, rows_, _, gain, _ = STEPS[s]
                x = kr[:] if s == KR_STEP else stg[0:rows_, s % 4]
                dve.wait_ge(S["item_rs"], item_of(s) + 1)
                nc.vector.scalar_tensor_tensor(out=x, in0=x, scalar=col(gain, 0, rows_),
                                               in1=tmp[0:rows_, item_of(s) % 2], op0=ALU.mult, op1=ALU.mult).then_inc(
                    S["rope_ready" if kind == "rope" else "item_done"], 1)

            def rotate(s):
                rows_ = STEPS[s][2]
                x = kr[:] if s == KR_STEP else stg[0:rows_, s % 4]
                dve.wait_ge(S["item_rot"], rope_of(s) + 1)
                dve.wait_ge(S["trig_ready"], 2)
                link(nc.vector.tensor_tensor(two(rope_t[0:rows_]), aux_two(2, rows_), two(sq[0:rows_, 0]), ALU.mult))
                link(nc.vector.tensor_tensor(x, x, sq[0:rows_, 1], ALU.mult))
                nc.vector.tensor_tensor(x, x, rope_t[0:rows_], ALU.add).then_inc(S["item_done"], 1)

            two_pi = 2.0 * np.pi
            c1 = 6.28125
            c2 = float(np.float32(0.0019350051879882812))
            c3 = float(two_pi - c1 - c2)
            magic = 12582912.0

            def angles():
                dve.wait_ge(S["pos_loaded"], 16)
                dve.wait_ge(S["trig_pos"], 1)
                link(nc.vector.tensor_copy(angle, g_pos))
                link(nc.vector.tensor_scalar(angle[:, N_META:], angle[:, N_META:], float(N_META), None, ALU.add))
                link(nc.vector.tensor_scalar(angle, angle, col("freq"), None, ALU.mult))

            def whole_turns(shift):
                t = turns
                link(nc.vector.tensor_scalar(t, angle, 1.0 / two_pi, shift, ALU.mult, ALU.add))
                link(nc.vector.tensor_scalar(t, t, magic, None, ALU.add))
                link(nc.vector.tensor_scalar(t, t, magic, None, ALU.subtract))

            def less_turns(r):
                t = turns
                link(nc.vector.scalar_tensor_tensor(out=r, in0=t, scalar=-c1, in1=angle, op0=ALU.mult, op1=ALU.add))
                link(nc.vector.scalar_tensor_tensor(out=r, in0=t, scalar=-c2, in1=r, op0=ALU.mult, op1=ALU.add))
                link(nc.vector.scalar_tensor_tensor(out=r, in0=t, scalar=-c3, in1=r, op0=ALU.mult, op1=ALU.add))

            def trig_argument(k):
                r = sq[:, k]
                if k:
                    link(nc.vector.tensor_scalar(r, r, float(np.pi / 2), None, ALU.add))
                nc.vector.tensor_scalar(r, r, 3.1415925, -3.1415925, ALU.min, ALU.max).then_inc(S["trig_arg"], 1)

            def maxima(group, hd):
                for i, _ in enumerate(MAX_UNITS):
                    k = (group * HEADS + hd) * len(MAX_UNITS) + i
                    dve.wait_ge(S["logit_ready"], k + 1)
                    nc.vector.reduce_max(maxes[:, group, i, hd:hd + 1], max_bank(k)[:, 0:MAX_UNITS[i][2]],
                                         AX.X).then_inc(S["max_ready"], 1)

            def last_maxima(group):
                dve.wait_ge(S["max_ready"], (group + 1) * HEADS * len(MAX_UNITS))
                nc.vector.tensor_tensor(maxes[:, group, 3], maxes[:, group, 3], maxes[:, group, 4],
                                        ALU.max).then_inc(S["maxes_ready"], 1)

            for s in range(N_STEPS + 2):
                if s < N_STEPS and s != KR_STEP:
                    evacuate(s)
                if s == 0:
                    for j in range(5):
                        dve.wait_ge(S["lrs_ready"], 1 if j < 3 else 2)
                        nc.vector.scalar_tensor_tensor(out=lora[:, j], in0=lora[:, j],
                                                       scalar=col("g_qa", j) if j < 3 else col("g_kva", j - 3),
                                                       in1=lora_rs[0 if j < 3 else 1], op0=ALU.mult,
                                                       op1=ALU.mult).then_inc(S["ln_ready"], 1)
                    dve.wait_ge(S["fgl_ready"], 1)
                    link(nc.vector.tensor_scalar(o_f, o_f, col("od_b_f", 0, HEADS), 0.0, ALU.add, ALU.min))
                    link(nc.vector.tensor_tensor(o_l, o_l, o_f, ALU.subtract))
                    nc.vector.tensor_tensor_scan(g_F, o_l, o_zero, 0.0, ALU.add, ALU.add).then_inc(S["fF_ready"], 1)
                if 1 <= s <= 5:
                    split_low(b_lo[:, s - 1], b_hi[:, s - 1], lora[:, s - 1], HI + s)
                if s == 2:
                    dve.wait_ge(S["ln_ready"], 5)
                    link(nc.vector.memset(vp[:, :, :, HD:2 * HD], 1.0))
                rope_next = s and s <= N_STEPS and STEPS[s - 1][0] == "rope"
                if rope_next:
                    normalise(s - 1)
                if s >= 2 and STEPS[s - 2][0] == "rope":
                    rotate(s - 2)
                if C_NORMS + 2 <= s:
                    maxima(0, s - C_NORMS - 2)
                if s and s <= N_STEPS and STEPS[s - 1][0] == "norm":
                    normalise(s - 1)
                if s == 1:
                    dve.wait_ge(S["fhi_ready"], 1)
                    nc.vector.tensor_tensor(o_l, g_F, o_hi.bitcast(F32), ALU.subtract).then_inc(S["flo_ready"], 1)
                if s == 3:
                    angles()
                elif s == 4:
                    whole_turns(0.0)
                    less_turns(sq[:, 0])
                elif s == 5:
                    trig_argument(0)
                    whole_turns(0.25)
                elif s == 6:
                    less_turns(sq[:, 1])
                elif s == 7:
                    trig_argument(1)
                if s == D_STEPS:
                    nc.vector.memset(a_lo[C_NOPE + C_ROPE:C_NOPE + C_ROPE + 1].bitcast(F32), 1.0).then_inc(
                        S["aug_one"], 1)
            last_maxima(0)

            au = units(False)

            def pair_low(group, pair):
                tile = out_tile(group, pair)
                split_low(b_lo[:, tile, N_META:], b_hi[:, tile, N_META:], tmp[:, pair % 2, 0:SEQ],
                          HI + 5 + group * 4 + pair + 1)

            def attend(group):
                for step in range(HEADS + 1):
                    if group == 0 and step < HEADS:
                        maxima(1, step)
                    if group == 0 and step == HEADS - 1:
                        last_maxima(1)
                    if step == 0:
                        continue
                    hd = step - 1
                    gh = group * HEADS + hd
                    pair = hd // 2
                    lo_ = HD * (hd % 2)
                    dve.wait_ge(S["inv_l_ready"], gh + 1)
                    if hd % 2 == 0 and pair >= 2:
                        dve.wait_ge(S["split_hi"], HI + 5 + group * 4 + pair - 1)
                    o = prod[:, gh % 2, 0:SEQ]
                    nc.vector.tensor_tensor(tmp[lo_:lo_ + HD, pair % 2, 0:SEQ], o[lo_:lo_ + HD],
                                            stg[lo_:lo_ + HD, 0, 0:SEQ], ALU.mult).then_inc(S["ot_ready"], 1)
                    if hd and hd % 2 == 0:
                        pair_low(group, pair - 1)
                pair_low(group, 3)

            dve.wait_ge(S["psum_free"], Y_UV)
            for j in range(4):
                sem_, count = product_end(Y_UV + j)
                dve.wait_ge(S[sem_], count)
                if j == 2:
                    for slot_ in (2, 3):
                        dve.wait_ge(norm_dma[slot_], 64)
                nc.vector.tensor_copy(two(uv[j]), slot(Y_UV + j)).then_inc(S["psum_free"], 1)
            split_weights(S_UV + 2)
            attend(0)
            attend(1)

            for m in range(KT):
                dve.wait_ge(S["w_used"], S_OUT1 + m + 1)
                nc.vector.tensor_tensor(h[:, m, N_META:], slot_real(Y_OUT1 + m), h[:, m, N_META:], ALU.add).then_inc(
                    S["psum_free"], 1)
                split_weights(S_OUT1 + 2 + m)
                next_operand(m, 3 * KT, "mlp_ln1", a_hi, a_lo, N_META)
            dve.wait_ge(S["ms_ready"], 4)
            HI1 = HI + 5 + 8
            with dve.Fori(0, QUARTERS - 1) as q:
                mlp(S_MLP1, Y_MLP1, HI1, N_META, q, 1)
            mlp(S_MLP1, Y_MLP1, HI1, N_META, QUARTERS - 1, 1, True)

        @block.tensor
        def _(pe):
            FULL = ((0, 0, HALF), (512, HALF, HALF))
            REAL = ((512, N_META, SEQ),)

            def product(nb, y, x, spans, q16=0, k0=0, nk=8, kb=0, start=True, stop=True, waits=None,
                        ks=None):
                hi, lo = x
                if start and y >= 2:
                    pe.wait_ge(S["psum_free"], y - (not Y_O <= y <= Y_OUT0) + q16)
                pe.wait_ge(S["w_lo_ready"], nb + 1 + q16)
                for i_k, k in enumerate(range(nk) if ks is None else ks):
                    if waits is not None:
                        pe.wait_ge(S["operand_ready"], waits + k + 1)
                    blk = slice((k0 + k) * P, (k0 + k + 1) * P)
                    for i, (w, xx) in enumerate(((w_hi, hi), (w_hi, lo), (w_lo, hi))):
                        for c, t0, n in spans:
                            last = nc.tensor.matmul(prod[:, slot_of(y), c:c + n], w[:, nb % 2, blk],
                                                    xx[:, kb + k, t0:t0 + n], start=start and i_k == 0 and i == 0,
                                                    stop=stop and i_k == (nk if ks is None else len(ks)) - 1 and i == 2)
                return last

            A, B, C = (a_hi, a_lo), (b_hi, b_lo), (c_hi, c_lo)

            def stats(k, t0=0):
                pe.wait_ge(S["sq_summed"], (k + 1) * KT)
                if t0:
                    nc.tensor.matmul(aux[:, 0:SEQ], cm(C_ONES), sq_sum[:, t0:], start=True, stop=True).then_inc(
                        S["stat_ready"], 1)
                else:
                    for c, f, n in FULL:
                        last = nc.tensor.matmul(aux[:, c:c + n], cm(C_ONES), sq_sum[:, f:f + n], start=True, stop=True)
                    last.then_inc(S["stat_ready"], 1)

            def gate_products(j):
                pe.wait_ge(S["xc_ready"], j + 1)
                if j:
                    pe.wait_ge(S["sig_ready"], j)
                else:
                    pe.wait_ge(S["wr_loaded"], 16)
                    pe.wait_ge(S["ms_ready"], 1)
                for which in range(2):
                    for c, f, n in FULL:
                        last = nc.tensor.matmul(aux[:, which * 1024 + c:which * 1024 + c + n],
                                                wr[:, (which * KT + j) * P:(which * KT + j + 1) * P],
                                                xc[:, j % 2, f:f + n], start=True, stop=True)
                last.then_inc(S["gates_ready"], 1)

            for g in range(KT):
                product(2 * g, 2 * g, A, FULL, waits=R_X0 if g == 0 else None).then_inc(S["w_used"], 1)
                if g == 0:
                    pe.wait_ge(S["const_loaded"], 16)
                    stats(0)
                else:
                    gate_products(g - 1)
                product(2 * g + 1, 2 * g + 1, A, FULL).then_inc(S["w_used"], 1)
            product(S_GATES, Y_GATES, A, FULL).then_inc(S["w_used"], 1)
            gate_products(KT - 1)
            for j in range(8):
                product(S_QK + j, Y_QK + j, A, FULL).then_inc(S["w_used"], 1)

            def transpose_v(j, y, base):
                pe.wait_ge(S["psum_free"], y + 1)
                if base == 8:
                    pe.wait_ge(S["item_ms"], 9)
                if base + j >= 2:
                    pe.wait_ge(S["v_copied"], base + j - (base != 8))
                a = v_bank(j, base)
                for b, (t0, n) in enumerate(BLOCKS):
                    c = a if b == NB - 1 else a + 512 + b * P
                    src = tmp[:, j % 2] if base == 0 else stg[:, (V_STEP + j) % 4] if base == 8 else uv[j]
                    last = nc.tensor.transpose(aux[0:n, c:c + P], src[:, t0:t0 + n], cm(C_IDENT))
                last.then_inc(S["vt_ready"], 1)

            def broadcast(hd, k):
                if k:
                    pe.wait_ge(S["abc_ready"], hd + 1)
                for c, f, n in FULL:
                    last = nc.tensor.matmul(aux[:, 1024 + c:1024 + c + n], cm(C_SEL + hd, A_HEADS),
                                            (g_F, g_m)[k][0:A_HEADS, f:f + n], start=True, stop=True)
                last.then_inc(S["bc_ready"], 1)

            pe.wait_ge(S["sig_ready"], KT)
            for j in range(8):
                product(S_V + j, Y_V + j, A, FULL).then_inc(S["w_used"], 1)
                if j == 0:
                    pe.wait_ge(S["rows_ready"], 1)
                    for i, (t0, n) in enumerate(BLOCKS):
                        last = nc.tensor.matmul(aux[0:n, i * A_HEADS:(i + 1) * A_HEADS], g_i[0:A_HEADS, t0:t0 + n],
                                                cm(C_IDENT, A_HEADS, A_HEADS), start=True, stop=True)
                    last.then_inc(S["ccol_psum"], 1)
                    broadcast(0, 0)
                elif j == 1:
                    pe.wait_ge(S["ccol_ready"], 1)
                elif j == 2:
                    pe.wait_ge(S["em_ready"], 1)
                if j:
                    transpose_v(j - 1, Y_V + j - 1, 0)
                if j == 1:
                    broadcast(0, 1)
            transpose_v(7, Y_V + 7, 0)

            pe.wait_ge(S["v_copied"], 8)
            pe.wait_ge(S["psum_free"], Y_V + 8)
            mu = units(True)

            def scores(hd, u):
                j, t0, n, off, _ = mu[u]
                if u >= 2:
                    pe.wait_ge(S["st_ready"], hd * len(mu) + u - 1)
                b = (2 + u % 2) * 512
                nc.tensor.matmul(aux[0:BLOCKS[j][1], b:b + n],
                                 qk[:, A_HEADS + hd, BLOCKS[j][0]:BLOCKS[j][0] + BLOCKS[j][1]],
                                 qk[:, hd, t0:t0 + n], start=True, stop=True).then_inc(S["s_ready"], 1)

            for hd in range(A_HEADS):
                pe.wait_ge(S["em_ready"], hd + 1)
                if hd:
                    pe.wait_ge(S["hn_ready"], 2 * hd)
                scores(hd, 0)
                for u, (j, t0, n, off, _) in enumerate(mu):
                    if u + 1 < len(mu):
                        scores(hd, u + 1)
                    rows_ = BLOCKS[j][1]
                    pe.wait_ge(S["st_ready"], hd * len(mu) + u + 1)
                    for e in range(3):
                        meta, real = head_sums(e)
                        if hd and u == 0 and e == 2:
                            pe.wait_ge(S["hms_ready"], hd)
                        acc = meta if t0 == 0 else real[:, t0 - N_META:t0 - N_META + n]
                        w = v[0:rows_, j, hd * A_DV + e * P:hd * A_DV + (e + 1) * P] if e < 2 else cm(C_ONES, rows_)
                        last = nc.tensor.matmul(acc, w, st[0:rows_, off:off + n], start=u in (0, len(mu) - 1),
                                                stop=u >= len(mu) - 2)
                last.then_inc(S["acc_ready"], 1)
                for e in range(2):
                    if hd + 1 < A_HEADS:
                        broadcast(hd + 1, e)
                    product(S_O + 2 * hd + e, Y_O + 2 * hd + e, A, FULL).then_inc(S["w_used"], 1)
                pe.wait_ge(S["hnsq_ready"], 2 * hd + 2)
                for e in range(2):
                    for c, f, n in FULL:
                        last = nc.tensor.matmul(aux[:, c:c + n], cm(C_ONES),
                                                st[:, e * T + f:e * T + f + n], start=e == 0, stop=e == 1)
                last.then_inc(S["hstat_ready"], 1)

            def out0(m, part):
                t = out0_tile(m, part)
                product(t, Y_OUT0 + m, (B, C)[part], FULL, start=part == 0, stop=part == 1,
                        waits=R_HA if (m, part) == (0, 1) else None).then_inc(S["w_used"], 1)

            for m, part in [(0, 0), (1, 0), (0, 1), (1, 1)] + [(m, part) for m in range(2, KT) for part in range(2)]:
                out0(m, part)

            def mlp(s0, y0, r_hid, x, hid, spans, q, first_wait=None, stats_k=None):
                for j in range(8):
                    product(s0 + j, y0 + j, x, spans, q * 16, waits=first_wait if j == 0 else None).then_inc(
                        S["w_used"], 1)
                    if j == 0 and stats_k is not None:
                        stats(stats_k, spans[0][1])
                for j in range(8):
                    product(s0 + 8 + j, y0 + 8 + j, hid, spans, q * 16,
                            waits=(r_hid + q * 8) if j == 0 else None).then_inc(S["w_used"], 1)

            mlp(S_MLP0, Y_MLP0, R_MLP0, A, B, FULL, 0, R_X1, 1)
            with pe.Fori(0, QUARTERS - 2) as q:
                mlp(S_MLP0 + 16, Y_MLP0 + 16, R_MLP0 + KT, A, B, FULL, q)
            mlp(S_MLP0, Y_MLP0, R_MLP0, A, B, FULL, QUARTERS - 1)

            product(S_LORA, Y_LORA, A, FULL, waits=R_X2).then_inc(S["w_used"], 1)
            stats(2)
            for j in range(1, 5):
                product(S_LORA + j, Y_LORA + j, A, FULL).then_inc(S["w_used"], 1)
            product(S_KRFF, Y_KRFF, A, FULL).then_inc(S["w_used"], 1)

            def lora_stats():
                pe.wait_ge(S["ms_ready"], 3)
                for k, (j0, n_) in enumerate(((0, 3), (3, 2))):
                    pe.wait_ge(S["lsq_ready"], j0 + n_)
                    for j in range(n_):
                        for c, f, n in FULL:
                            last = nc.tensor.matmul(aux[:, k * 1024 + c:k * 1024 + c + n], cm(C_ONES),
                                                    lora_sq[:, j0 + j, f:f + n], start=j == 0, stop=j == n_ - 1)
                    last.then_inc(S["lstat_ready"], 1)

            def item_stat(s):
                _, _, rows_, mat, _, _ = STEPS[s]
                k = item_of(s)
                pe.wait_ge(S["item_sq"], k + 1)
                if k:
                    pe.wait_ge(S["item_ms"], k)
                    if s >= D_STEPS:
                        pe.wait_ge(S["v_copied"], 12)
                else:
                    pe.wait_ge(S["lms_ready"], 2)
                for c, f, n in FULL:
                    last = nc.tensor.matmul(aux[0:rows_, c:c + n], cm(mat, rows_, rows_), tmp[0:rows_, k % 2, f:f + n],
                                            start=True, stop=True)
                last.then_inc(S["item_stat"], 1)

            def rotate(s):
                rows_ = STEPS[s][2]
                x = kr[:] if s == KR_STEP else stg[0:rows_, s % 4]
                pe.wait_ge(S["rope_ready"], rope_of(s) + 1)
                if rope_of(s):
                    pe.wait_ge(S["item_done"], item_of(s))
                for c, f, n in FULL:
                    last = nc.tensor.matmul(aux[0:rows_, 1024 + c:1024 + c + n], cm(C_ROT, rows_, rows_),
                                            x[:, f:f + n], start=True, stop=True)
                last.then_inc(S["item_rot"], 1)

            def low_rank_product(y):
                c = y - Y_UQ
                if c < 6:
                    last = product(S_UQ + c // 2, y, B, FULL, k0=3 * (c % 2), nk=3, waits=R_LORA if c == 0 else None)
                else:
                    tile, i = divmod(c - 6, 4)
                    last = product(S_UK + tile, y, B, FULL, k0=2 * i, nk=2, kb=3, waits=R_LORA + 3 if c == 6 else None)
                last.then_inc(S[product_end(y)[0]], 1)

            def maxima(group, hd, first, last):
                for u in range(first, last):
                    k = (group * HEADS + hd) * len(MAX_UNITS) + u
                    if k == HEADS * len(MAX_UNITS):
                        pe.wait_ge(S["aug_one"], 2)
                        for i in range(4):
                            pe.wait_ge(item_dma[i], slot_moves(N_STEPS, i))
                            pe.wait_ge(norm_dma[i], 64)
                        pe.wait_ge(S["psum_free"], Y_UV + 4)
                    elif k == 0:
                        pe.wait_ge(S["augF"], 32)
                        pe.wait_ge(S["aug_one"], 1)
                        pe.wait_ge(S["bf_ready"], 3)
                        pe.wait_ge(S["item_done"], item_of(C_NORMS))
                        for i in range(4):
                            pe.wait_ge(item_dma[i], slot_moves(KR_STEP, i))
                    if k >= 2:
                        pe.wait_ge(S["max_ready"], k - 1)
                    i, f, n = MAX_UNITS[u]
                    o, rows_ = max_bank(k), (HD + 2, C_NOPE + C_ROPE)[group]
                    diag = u < 3 or u == 4
                    ins = nc.tensor.matmul(o[:, 0:n],
                                           q_of[group][0:rows_, hd, N_META + P * i:N_META + P * (i + 1)],
                                           k_of[group][0:rows_, hd, f:f + n], start=True, stop=not diag)
                    if diag:
                        ins = nc.tensor.matmul(o[:, n - P:n], ident_bf[:], mask_ts_bf[:], start=False, stop=True)
                    ins.then_inc(S["logit_ready"], 1)

            for s in range(N_STEPS + 2):
                if s < D_STEPS and s != KR_STEP:
                    product(tile_of(s), STEPS[s][1], A, FULL).then_inc(S["w_used"], 1)
                elif D_STEPS <= s < N_STEPS:
                    low_rank_product(STEPS[s][1])
                if s == 0:
                    lora_stats()
                if C_NORMS + 2 <= s:
                    maxima(0, s - C_NORMS - 2, 0, 2)
                if s and s <= N_STEPS:
                    if STEPS[s - 1][0] == "value":
                        transpose_v(s - 1 - V_STEP, STEPS[s - 1][1], 8)
                    else:
                        item_stat(s - 1)
                if s >= 2 and STEPS[s - 2][0] == "rope":
                    rotate(s - 2)
                if C_NORMS + 2 <= s:
                    maxima(0, s - C_NORMS - 2, 2, 5)

            au = units(False)

            def max_rows(group):
                pe.wait_ge(S["maxes_ready"], group + 1)
                if group == 0:
                    pe.wait_ge(S["item_ms"], item_of(N_STEPS))
                else:
                    pe.wait_ge(S["p_ready"], HEADS * NB)
                for i in range(4):
                    last = nc.tensor.matmul(aux[0:HEADS, i * P:(i + 1) * P], maxes[:, group, i, :], cm(C_IDENT),
                                            start=True, stop=True)
                last.then_inc(S["mxrow_ready"], 1)

            def attend(group, row_count):
                pe.wait_ge(S["mxneg_ready"], group + 1)
                if group == 0:
                    pe.wait_ge(S["psum_free"], Y_UV + 4)
                pe.wait_ge(mx_dma[group], 16)

                def logits(hd, u):
                    j, t0, n, off, diag = au[u]
                    k = (group * HEADS + hd) * NB + u
                    if hd > 0 or u >= 4:
                        pe.wait_ge(S["p_ready"], k - 3)
                    o = aux[0:BLOCKS[j][1], (k % 4) * 512:(k % 4) * 512 + n]
                    last = nc.tensor.matmul(
                        o, k_of[group][0:row_count, hd, BLOCKS[j][0]:BLOCKS[j][0] + BLOCKS[j][1]].bitcast(F32),
                        q_of[group][0:row_count, hd, t0:t0 + n].bitcast(F32), start=True, stop=False)
                    rows_ = BLOCKS[j][1]
                    last = nc.tensor.matmul(o[:, 0:diag], ident_bf[0:rows_, 0:rows_],
                                            triangle(mask_st_bf, j, t0, diag), start=False, stop=True)
                    last.then_inc(S["l_ready"], 1)

                def weigh(hd, u):
                    j, t0, n, off, diag = au[u]
                    gh = group * HEADS + hd
                    if u == 0 and gh >= 2:
                        pe.wait_ge(S["ot_ready"], gh - 1)
                    pe.wait_ge(S["p_ready"], gh * NB + u + 1)
                    rows_ = BLOCKS[j][1]
                    last = nc.tensor.matmul(prod[:, gh % 2, t0 - N_META:t0 - N_META + n],
                                            vp[0:rows_, j, hd // 2, (hd % 2) * HD:(hd % 2) * HD + P],
                                            pt[0:rows_, hd % 2, off:off + n], start=u == 0, stop=u == NB - 1)
                    if u == NB - 1:
                        last.then_inc(S["o_ready"], 1)

                for hd in range(HEADS):
                    for u in range(NB):
                        logits(hd, u)
                        if hd:
                            weigh(hd - 1, u)
                        if group == 0:
                            maxima(1, hd, u, u + 1)
                for u in range(NB):
                    if group == 0 and u == NB - 1:
                        max_rows(1)
                    weigh(HEADS - 1, u)

            max_rows(0)
            for c in range(4):
                low_rank_product(Y_UV + c)
            attend(0, HD + 3)
            pe.wait_ge(S["mxneg_ready"], 2)
            for j in range(4):
                transpose_v(j, Y_UV + j, 12)
            pe.wait_ge(S["v_copied"], 16)
            attend(1, C_NOPE + C_ROPE + 1)

            last_tiles = [out_tile(1, 2), out_tile(1, 3)]
            for n, tiles in enumerate(([k for k in range(8) if k not in last_tiles], last_tiles[:1], last_tiles[1:])):
                pe.wait_ge(S["operand_ready"], R_ATT_C + 2 + n)
                for m in range(2):
                    last = product(S_OUT1 + m, Y_OUT1 + m, B, REAL, ks=tiles, start=n == 0, stop=n == 2)
                    if n == 2:
                        last.then_inc(S["w_used"], 1)
            for m in range(2, KT):
                product(S_OUT1 + m, Y_OUT1 + m, B, REAL).then_inc(S["w_used"], 1)
            mlp(S_MLP1, Y_MLP1, R_MLP1, A, B, REAL, 0, R_X3, 3)
            with pe.Fori(0, QUARTERS - 2) as q:
                mlp(S_MLP1 + 16, Y_MLP1 + 16, R_MLP1 + KT, A, B, REAL, q)
            mlp(S_MLP1, Y_MLP1, R_MLP1, A, B, REAL, QUARTERS - 1)


def _blocks(w, columns):
    return w[:, columns].reshape(-1, P, len(columns)).transpose(1, 0, 2)


def _stream(ev_w_in, ev_w_out, od_w_in, od_w_uq, od_w_ukv, od_w_out, w_ff1, w_ff2):
    s = np.zeros((S_END, P, 8, P), np.float32)
    q0, k0, v0, o0, i0, f0, x0, b0 = np.cumsum([0, 512, 512, 1024, 1024, A_HEADS, A_HEADS, D_MODEL])
    for g in range(KT):
        s[S_RG + 2 * g] = _blocks(ev_w_in, range(x0 + g * P, x0 + (g + 1) * P))
        s[S_RG + 2 * g + 1] = _blocks(ev_w_in, range(b0 + g * P, b0 + (g + 1) * P))
    s[S_GATES][:, :, 0:A_HEADS] = _blocks(ev_w_in, range(i0, i0 + A_HEADS))
    s[S_GATES][:, :, 32:32 + A_HEADS] = _blocks(ev_w_in, range(f0, f0 + A_HEADS))
    for first, at, n in ((S_QK, q0, 8), (S_V, v0, 8), (S_O, o0, 8)):
        for j in range(n):
            s[first + j] = _blocks(ev_w_in, range(at + j * P, at + (j + 1) * P))
    for m in range(KT):
        c = range(m * P, (m + 1) * P)
        s[out0_tile(m, 0)] = _blocks(ev_w_out[D_MODEL:], c)
        s[out0_tile(m, 1)] = _blocks(ev_w_out[:D_MODEL], c)
        rows = _blocks(od_w_out, c)
        for group in range(2):
            for pair in range(4):
                s[S_OUT1 + m][:, out_tile(group, pair)] = rows[:, pair + (0 if group else 4)]
    for first, layer in ((S_MLP0, 0), (S_MLP1, 1)):
        for q in range(QUARTERS):
            for j in range(8):
                c = q * D_MODEL + j * P
                s[first + 16 * q + j] = _blocks(w_ff1[layer], range(c, c + P))
                s[first + 16 * q + 8 + j] = _blocks(w_ff2[layer][q * D_MODEL:(q + 1) * D_MODEL],
                                                    range(j * P, (j + 1) * P))
    kr0 = Q_LORA + KV_LORA
    fq0 = kr0 + C_ROPE
    for j in range(5):
        s[S_LORA + j] = _blocks(od_w_in, range(j * P, (j + 1) * P))
    s[S_KRFF][:, :, 0:C_ROPE] = _blocks(od_w_in, range(kr0, kr0 + C_ROPE))
    s[S_KRFF][:, :, 32:32 + HEADS] = _blocks(od_w_in, range(fq0 + 3 * 512, fq0 + 3 * 512 + HEADS))
    for j in range(12):
        s[(S_FQK if j < 8 else S_FV - 8) + j] = _blocks(od_w_in, range(fq0 + j * P, fq0 + (j + 1) * P))
    for m in range(6):
        if m < 2:
            c = [hd * 96 + C_NOPE + f for hd in range(4 * m, 4 * m + 4) for f in range(C_ROPE)]
        else:
            c = [hd * 96 + f for hd in (2 * (m - 2), 2 * (m - 2) + 1) for f in range(C_NOPE)]
        s[S_UQ + m // 2][:, 3 * (m % 2):3 * (m % 2) + 3] = _blocks(od_w_uq, c)
    for m in range(4):
        for first, off in ((S_UK, 0), (S_UV, C_NOPE)):
            c = [hd * 128 + off + f for hd in (2 * m, 2 * m + 1) for f in range(64)]
            s[first][:, 2 * m:2 * m + 2] = _blocks(od_w_ukv, c)
    return s.reshape(S_END, P, TILE)


def _columns(x):
    c = np.zeros((P, N_COLS), np.float32)

    def put(name, values):
        at = COLS[name][0]
        values = np.asarray(values, np.float32).reshape(-1, P).T
        c[:, at:at + values.shape[1]] = values

    put("ev_ln", x["ev_ln"]), put("od_ln", x["od_ln"])
    put("mlp_ln0", x["mlp_ln"][0]), put("mlp_ln1", x["mlp_ln"][1])
    for ours, theirs in (("conv_w", "ev_conv_w"), ("conv_b", "ev_conv_b"), ("b_ra", "ev_b_ra"), ("b_rx", "ev_b_rx"),
                         ("lam", "ev_lam"), ("a_norm", "ev_a_norm"), ("g_qa", "od_g_qa"), ("g_kva", "od_g_kva")):
        put(ours, x[theirs])
    for name in ("g_qn", "g_qr", "g_kn", "g_kr", "g_fq", "g_fk"):
        g = x["od_" + name].reshape(-1)
        put(name, np.tile(g, P // g.size))
    c[0:A_HEADS, COLS["b_i"][0]] = x["ev_b_if"][0, :A_HEADS]
    c[0:A_HEADS, COLS["b_f"][0]] = x["ev_b_if"][0, A_HEADS:]
    c[0:HEADS, COLS["od_b_f"][0]] = x["od_b_f"][0]
    half = C_ROPE // 2
    freqs = np.float32(10000.0) ** (-np.arange(half, dtype=np.float32) / np.float32(half))
    c[:, COLS["freq"][0]] = np.tile(freqs.astype(np.float32), P // half)
    c[:, COLS["eps"][0]:COLS["eps"][0] + 3] = [EPS, EPS * HD, EPS * (C_NOPE + C_ROPE)]
    return c


def _constants():
    c = np.zeros((N_CONST, P, P), np.float32)
    i = np.arange(P)
    c[C_IDENT] = np.eye(P)
    c[C_ONES] = 1.0
    c[C_BLK64] = (i[:, None] // 64 == i[None, :] // 64) / 64.0
    c[C_BLK32] = (i[:, None] // 32 == i[None, :] // 32) / 32.0
    for m in range(P):
        c[C_ROT, m + 16 if m % 32 < 16 else m - 16, m] = -1.0 if m % 32 < 16 else 1.0
    c[C_MASK_ST] = np.where(i[:, None] > i[None, :], MASKED, 0.0)
    c[C_MASK_TS] = c[C_MASK_ST].T
    for hd in range(A_HEADS):
        c[C_SEL + hd, hd] = 1.0
    return c.transpose(1, 0, 2).reshape(P, N_CONST * P)


def kernel(**inputs):
    import concourse.bacc as bacc
    from concourse.bass_utils import run_bass_kernel_spmd

    x = {k: np.asarray(a) for k, a in inputs.items()}
    arrays = {
        "in_h": np.ascontiguousarray(np.concatenate([x["meta"], x["x"][0]], axis=0).T),
        "in_positions": np.ascontiguousarray(x["positions"]),
        "in_stream": _stream(x["ev_w_in"][0], x["ev_w_out"][0], x["od_w_in"][0], x["od_w_uq"][0], x["od_w_ukv"][0],
                             x["od_w_out"][0], x["w_ff1"], x["w_ff2"]),
        "in_gate_w": np.ascontiguousarray(np.concatenate([x["ev_w_ra"][0], x["ev_w_rx"][0]], axis=0)),
        "in_cols": _columns(x),
        "in_const": _constants(),
    }
    nc = bacc.Bacc("TRN2", target_bir_lowering=False, num_devices=1)
    args = [nc.dram_tensor(n, a.shape, mybir.dt.from_np(a.dtype), kind="ExternalInput").ap()
            for n, a in arrays.items()]
    args.append(nc.dram_tensor("out_t", (D_MODEL, SEQ), mybir.dt.float32, kind="ExternalOutput").ap())
    trunk(nc, *args)
    r = run_bass_kernel_spmd(nc, [arrays], core_ids=[0])
    got = np.asarray(r.results[0]["out_t"])
    return np.ascontiguousarray(got.T).reshape(1, SEQ, D_MODEL)
```
